# Optimizing a Trainium2 kernel written in Bass

```python
import math
import jax
import jax.numpy as jnp
from jax import lax
import numpy as np

D_MODEL = 1024
BATCH = 1
SEQ = 512
DEPTH = 2
DEC_BATCH = 8
DEC_SEQ = 4
PAST_LEN = 256
PAGE_SIZE = 128

HEAD_DIM = 64
MIX_WIDTH = D_MODEL
N_GDN_HEADS = (MIX_WIDTH // 2) // HEAD_DIM
GDN_W = N_GDN_HEADS * HEAD_DIM
N_NSA_HEADS = (MIX_WIDTH - GDN_W) // HEAD_DIM
NSA_W = N_NSA_HEADS * HEAD_DIM
N_KV_HEADS = max(1, N_NSA_HEADS // 4)
GQA_GROUP = N_NSA_HEADS // N_KV_HEADS
KV_W = N_KV_HEADS * HEAD_DIM
CONV_W = 4
GDN_CHUNK = 64
CMP_BLOCK = 32
SEL_BLOCK = 64
TOP_K = 16
WINDOW = 512
NSA_QBLOCK = 64
WIN_QBLOCK = 128
D_FF = 4 * D_MODEL
ROPE_THETA = 10000.0
NORM_EPS = 1e-6
PROJ_WIDTHS = (3 * GDN_W, GDN_W, N_GDN_HEADS, N_GDN_HEADS, NSA_W, 6 * KV_W, 3 * N_NSA_HEADS)
D_PROJ = sum(PROJ_WIDTHS)

kernel_name = 'hymba_gdn_nsa_step'

def rmsnorm(x, g):
    xf = x.astype(jnp.float32)
    y = xf * lax.rsqrt(jnp.mean(xf * xf, axis=-1, keepdims=True) + NORM_EPS)
    return (y * g.astype(jnp.float32)).astype(x.dtype)

def l2norm(x):
    return x * lax.rsqrt(jnp.sum(x * x, axis=-1, keepdims=True) + NORM_EPS)

def rope(x, pos):
    half = HEAD_DIM // 2
    inv_freq = ROPE_THETA ** (-jnp.arange(half, dtype=jnp.float32) / half)
    ang = pos.astype(jnp.float32)[:, None] * inv_freq[None, :]
    cos = jnp.cos(ang)[None, :, None, :]
    sin = jnp.sin(ang)[None, :, None, :]
    xf = x.astype(jnp.float32)
    x1, x2 = xf[..., :half], xf[..., half:]
    return jnp.concatenate([x1 * cos - x2 * sin, x2 * cos + x1 * sin], axis=-1).astype(x.dtype)

def masked_softmax(s, mask):
    s = jnp.where(mask, s, -jnp.inf)
    m = jnp.max(s, axis=-1, keepdims=True)
    m = jnp.where(jnp.isfinite(m), m, 0.0)
    e = jnp.exp(s - m)
    return e / jnp.maximum(jnp.sum(e, axis=-1, keepdims=True), 1e-30)

def project(x, norm_g, w_in):
    b, t, _ = x.shape
    h = rmsnorm(x, norm_g)
    cuts = np.cumsum(PROJ_WIDTHS)[:-1].tolist()
    qkv_pre, z, a, beta_logit, q, kv6, gate_logit = jnp.split(h @ w_in, cuts, axis=-1)
    return (qkv_pre, z, a, beta_logit,
            q.reshape(b, t, N_NSA_HEADS, HEAD_DIM),
            kv6.reshape(b, t, 6, N_KV_HEADS, HEAD_DIM),
            gate_logit.reshape(b, t, N_NSA_HEADS, 3))

def gated_delta(q, k, v, g, beta, s0):
    b, t, h, dk = q.shape
    dv = v.shape[-1]
    c = GDN_CHUNK
    n = -(-t // c)
    pad = n * c - t

    def chunks(a):
        a = jnp.pad(a.astype(jnp.float32), [(0, 0), (0, pad)] + [(0, 0)] * (a.ndim - 2))
        a = a.reshape((b, n, c) + a.shape[2:])
        return jnp.moveaxis(a, 3, 2).swapaxes(0, 1)

    qc, kc, vc, gc, bc = chunks(q), chunks(k), chunks(v), chunks(g), chunks(beta)
    gcum = jnp.cumsum(gc, axis=-1)
    incl = jnp.tril(jnp.ones((c, c), dtype=bool))
    strict = jnp.tril(jnp.ones((c, c), dtype=bool), -1)
    decay = jnp.exp(jnp.where(incl, gcum[..., :, None] - gcum[..., None, :], -jnp.inf))
    a_mat = jnp.where(strict, bc[..., :, None] * jnp.einsum('nbhid,nbhjd->nbhij', kc, kc) * decay, 0.0)
    eye = jnp.broadcast_to(jnp.eye(c, dtype=jnp.float32), a_mat.shape)
    t_inv = lax.linalg.triangular_solve(a_mat + eye, eye, left_side=True, lower=True)
    w = jnp.einsum('nbhij,nbhjd->nbhid', t_inv, kc * (bc * jnp.exp(gcum))[..., None])
    u0 = jnp.einsum('nbhij,nbhjd->nbhid', t_inv, vc * bc[..., None])
    qk = jnp.einsum('nbhid,nbhjd->nbhij', qc, kc) * decay

    def step(s, inp):
        q_n, k_n, g_n, w_n, u0_n, qk_n = inp
        u = u0_n - jnp.einsum('bhcd,bhde->bhce', w_n, s)
        o = (jnp.einsum('bhcd,bhde->bhce', q_n * jnp.exp(g_n)[..., None], s)
             + jnp.einsum('bhij,bhje->bhie', qk_n, u))
        g_last = g_n[..., -1:]
        s = s * jnp.exp(g_last)[..., None] + jnp.einsum(
            'bhcd,bhce->bhde', k_n * jnp.exp(g_last - g_n)[..., None], u)
        return s, o

    s_fin, o = lax.scan(step, s0.astype(jnp.float32), (qc, kc, gcum, w, u0, qk))
    o = jnp.moveaxis(o.swapaxes(0, 1), 2, 3).reshape(b, n * c, h, dv)[:, :t]
    return o, s_fin

def gdn_mixer(qkv_pre, z, a, beta_logit, conv_buf, s0, conv_w, a_log, dt_bias, norm_g):
    b, t, _ = qkv_pre.shape
    xp = jnp.concatenate([conv_buf.astype(qkv_pre.dtype), qkv_pre], axis=1)
    conv = sum(xp[:, i:i + t] * conv_w[i] for i in range(CONV_W))
    new_buf = xp[:, t:]
    qkv = jax.nn.silu(conv.astype(jnp.float32)).reshape(b, t, 3, N_GDN_HEADS, HEAD_DIM)
    q = l2norm(qkv[:, :, 0]) * HEAD_DIM ** -0.5
    k = l2norm(qkv[:, :, 1])
    v = qkv[:, :, 2]
    g = -jnp.exp(a_log.astype(jnp.float32)) * jax.nn.softplus(a.astype(jnp.float32) + dt_bias.astype(jnp.float32))
    beta = jax.nn.sigmoid(beta_logit.astype(jnp.float32))
    o, s_new = gated_delta(q, k, v, g, beta, s0)
    o = rmsnorm(o, norm_g) * jax.nn.silu(z.astype(jnp.float32).reshape(b, t, N_GDN_HEADS, HEAD_DIM))
    return o.reshape(b, t, GDN_W), new_buf, s_new

def compress_kv(k, v, lp):
    b, l = k.shape[:2]
    nc = l // CMP_BLOCK

    def phi(r, pe, w):
        blocks = r[:, :nc * CMP_BLOCK].reshape(b, nc, CMP_BLOCK, N_KV_HEADS, HEAD_DIM)
        return jnp.einsum('bnckd,cde->bnke', blocks + pe[:, None, :], w)

    end_pos = (jnp.arange(nc) + 1) * CMP_BLOCK - 1
    return rope(phi(k, lp['cmp_pe_k'], lp['cmp_w_k']), end_pos), phi(v, lp['cmp_pe_v'], lp['cmp_w_v'])

def to_blocks(k, v):
    b, l = k.shape[:2]
    n = -(-l // SEL_BLOCK)
    rows = jnp.stack([k, v], axis=2)
    rows = jnp.pad(rows, [(0, 0), (0, n * SEL_BLOCK - l), (0, 0), (0, 0), (0, 0)])
    return rows.reshape(b, n, SEL_BLOCK, 2, N_KV_HEADS, HEAD_DIM).transpose(0, 4, 1, 2, 3, 5)

def kv_rows(k_cmp, v_cmp, k_sel, v_sel):
    return jnp.stack([k_cmp, v_cmp, k_sel, v_sel], axis=3).transpose(0, 2, 1, 3, 4)

def nsa_cmp_sel(q, pos0, ck, cv, fetch_sel, n_sel):
    b, t = q.shape[:2]
    nc = ck.shape[1]
    qb = math.gcd(t, NSA_QBLOCK)
    ratio = SEL_BLOCK // CMP_BLOCK
    k_top = min(TOP_K, n_sel)
    scale = HEAD_DIM ** -0.5
    f32 = jnp.float32
    cmp_end = (jnp.arange(nc) + 1) * CMP_BLOCK - 1
    blk = jnp.arange(n_sel)

    def one_block(i):
        qi = lax.dynamic_slice_in_dim(q, i * qb, qb, axis=1).reshape(b, qb, N_KV_HEADS, GQA_GROUP, HEAD_DIM)
        qpos = pos0 + i * qb + jnp.arange(qb)
        s_c = jnp.einsum('btkgd,bnkd->btkgn', qi, ck, preferred_element_type=f32) * scale
        p_c = masked_softmax(s_c, (cmp_end[None, :] <= qpos[:, None])[None, :, None, None, :])
        o_c = jnp.einsum('btkgn,bnkd->btkgd', p_c, cv.astype(f32))
        imp = jnp.pad(p_c.sum(axis=3), [(0, 0), (0, 0), (0, 0), (0, n_sel * ratio - nc)])
        imp = imp.reshape(b, qb, N_KV_HEADS, n_sel, ratio).sum(-1)
        cur = qpos // SEL_BLOCK
        valid = blk[None, :] * SEL_BLOCK <= qpos[:, None]
        forced = (blk[None, :] == 0) | (blk[None, :] == cur[:, None]) | (blk[None, :] == cur[:, None] - 1)
        score = jnp.where(forced[None, :, None, :], jnp.inf,
                          jnp.where(valid[None, :, None, :], imp, -jnp.inf))
        _, idx = lax.top_k(score, k_top)
        kv = fetch_sel(idx)
        tok = idx[..., None] * SEL_BLOCK + jnp.arange(SEL_BLOCK)
        mask_s = (tok <= qpos[None, :, None, None, None]).reshape(b, qb, N_KV_HEADS, 1, k_top * SEL_BLOCK)
        s_s = jnp.einsum('btkgd,btknsd->btkgns', qi, kv[..., 0, :], preferred_element_type=f32) * scale
        p_s = masked_softmax(s_s.reshape(b, qb, N_KV_HEADS, GQA_GROUP, k_top * SEL_BLOCK), mask_s)
        p_s = p_s.reshape(b, qb, N_KV_HEADS, GQA_GROUP, k_top, SEL_BLOCK)
        o_s = jnp.einsum('btkgns,btknsd->btkgd', p_s, kv[..., 1, :].astype(f32))
        return o_c, o_s

    o_c, o_s = lax.map(one_block, jnp.arange(t // qb))
    merge = lambda o: jnp.moveaxis(o, 0, 1).reshape(b, t, N_NSA_HEADS, HEAD_DIM)
    return merge(o_c), merge(o_s)

def window_attn(q, pos0, kw, vw):
    b, t = q.shape[:2]
    qb = math.gcd(t, WIN_QBLOCK)
    span = WINDOW + qb
    scale = HEAD_DIM ** -0.5

    def one_block(i):
        qi = lax.dynamic_slice_in_dim(q, i * qb, qb, axis=1).reshape(b, qb, N_KV_HEADS, GQA_GROUP, HEAD_DIM)
        ki = lax.dynamic_slice_in_dim(kw, i * qb, span, axis=1)
        vi = lax.dynamic_slice_in_dim(vw, i * qb, span, axis=1)
        qpos = pos0 + i * qb + jnp.arange(qb)
        kpos = pos0 - WINDOW + i * qb + jnp.arange(span)
        mask = ((kpos[None, :] >= 0) & (kpos[None, :] <= qpos[:, None])
                & (kpos[None, :] >= qpos[:, None] - WINDOW))
        s = jnp.einsum('btkgd,bskd->btkgs', qi, ki, preferred_element_type=jnp.float32) * scale
        p = masked_softmax(s, mask[None, :, None, None, :])
        return jnp.einsum('btkgs,bskd->btkgd', p, vi.astype(jnp.float32))

    o = lax.map(one_block, jnp.arange(t // qb))
    return jnp.moveaxis(o, 0, 1).reshape(b, t, N_NSA_HEADS, HEAD_DIM)

def layer_front(x, pos, lp, conv_buf, s0):
    qkv_pre, z, a, beta_logit, q, kv6, gate_logit = project(x, lp['norm_mix'], lp['w_in'])
    o_gdn, conv_new, s_new = gdn_mixer(qkv_pre, z, a, beta_logit, conv_buf, s0, lp['conv_w'],
                                       lp['a_log'], lp['dt_bias'], lp['gdn_norm'])
    q = rope(q, pos)
    k_cmp, v_cmp = kv6[:, :, 0], kv6[:, :, 1]
    k_sel, v_sel = rope(kv6[:, :, 2], pos), kv6[:, :, 3]
    k_win, v_win = rope(kv6[:, :, 4], pos), kv6[:, :, 5]
    return o_gdn, conv_new, s_new, q, k_cmp, v_cmp, k_sel, v_sel, k_win, v_win, gate_logit

def layer_back(x, o_gdn, gate_logit, o_c, o_s, o_w, lp):
    b, t, _ = x.shape
    gates = jax.nn.sigmoid(gate_logit.astype(jnp.float32))
    o_nsa = (gates[..., 0:1] * o_c + gates[..., 1:2] * o_s + gates[..., 2:3] * o_w).reshape(b, t, NSA_W)
    mixed = jnp.concatenate([o_gdn, o_nsa], axis=-1).astype(x.dtype)
    x = x + mixed @ lp['w_out']
    h = rmsnorm(x, lp['norm_mlp'])
    return x + jnp.square(jax.nn.relu(h @ lp['w_up'])) @ lp['w_down']

def prompt_layer(x, lp):
    b, t, _ = x.shape
    pos = jnp.arange(t)
    conv0 = jnp.zeros((b, CONV_W - 1, 3 * GDN_W), x.dtype)
    s0 = jnp.zeros((b, N_GDN_HEADS, HEAD_DIM, HEAD_DIM), jnp.float32)
    (o_gdn, conv_new, s_new, q, k_cmp, v_cmp, k_sel, v_sel, k_win, v_win,
     gate_logit) = layer_front(x, pos, lp, conv0, s0)
    ck, cv = compress_kv(k_cmp, v_cmp, lp)
    blocks = to_blocks(k_sel, v_sel)
    bi = jnp.arange(b)[:, None, None, None]
    hi = jnp.arange(N_KV_HEADS)[None, None, :, None]
    o_c, o_s = nsa_cmp_sel(q, 0, ck, cv, lambda idx: blocks[bi, hi, idx], blocks.shape[2])
    pad = [(0, 0), (WINDOW, 0), (0, 0), (0, 0)]
    o_w = window_attn(q, 0, jnp.pad(k_win, pad), jnp.pad(v_win, pad))
    y = layer_back(x, o_gdn, gate_logit, o_c, o_s, o_w, lp)
    win_new = jnp.stack([k_win, v_win], axis=2)[:, t - min(WINDOW, t):]
    return y, kv_rows(k_cmp, v_cmp, k_sel, v_sel), win_new, s_new, conv_new

def sample_layer(x, lp, pool, page_table, win_buf, s0, conv_buf):
    b, t, _ = x.shape
    past = page_table.shape[1] * PAGE_SIZE
    pos = past + jnp.arange(t)
    (o_gdn, conv_new, s_new, q, k_cmp, v_cmp, k_sel, v_sel, k_win, v_win,
     gate_logit) = layer_front(x, pos, lp, conv_buf, s0)
    past_cmp = pool[page_table, :, :, :2].transpose(0, 1, 3, 4, 2, 5).reshape(b, past, 2, N_KV_HEADS, HEAD_DIM)
    ck, cv = compress_kv(jnp.concatenate([past_cmp[:, :, 0], k_cmp], axis=1),
                         jnp.concatenate([past_cmp[:, :, 1], v_cmp], axis=1), lp)
    new_blocks = to_blocks(k_sel, v_sel)
    n_new = new_blocks.shape[2]
    n_past = past // SEL_BLOCK
    per_page = PAGE_SIZE // SEL_BLOCK
    pool_blocks = pool.reshape(pool.shape[0], N_KV_HEADS, per_page, SEL_BLOCK, 4, HEAD_DIM)
    bi = jnp.arange(b)[:, None, None, None]
    hi = jnp.arange(N_KV_HEADS)[None, None, :, None]

    def fetch(idx):
        pidx = jnp.minimum(idx, n_past - 1)
        phys = page_table[bi, pidx // per_page]
        old = pool_blocks[phys, hi, pidx % per_page, :, 2:]
        new = new_blocks[bi, hi, jnp.clip(idx - n_past, 0, n_new - 1)]
        return jnp.where((idx < n_past)[..., None, None, None], old, new)

    o_c, o_s = nsa_cmp_sel(q, past, ck, cv, fetch, n_past + n_new)
    wb = win_buf.shape[1]
    win_rows = jnp.concatenate([win_buf.astype(x.dtype), jnp.stack([k_win, v_win], axis=2)], axis=1)
    win_pad = jnp.pad(win_rows, [(0, 0), (WINDOW - wb, 0), (0, 0), (0, 0), (0, 0)])
    o_w = window_attn(q, past, win_pad[:, :, 0], win_pad[:, :, 1])
    y = layer_back(x, o_gdn, gate_logit, o_c, o_s, o_w, lp)
    return y, kv_rows(k_cmp, v_cmp, k_sel, v_sel), win_rows[:, t:], s_new, conv_new

def setup_inputs(seed: int = 0) -> dict:
    key = jax.random.key(seed)
    ks = jax.random.split(key, 24)
    f32 = jnp.float32
    n_pages = PAST_LEN // PAGE_SIZE
    n_pool = (DEC_BATCH * n_pages * 5) // 4
    win_buf = min(WINDOW, PAST_LEN)

    def nrm(k, shape, scale):
        return jax.random.normal(k, shape, f32) * scale

    page_table = jax.random.permutation(ks[3], n_pool)[:DEC_BATCH * n_pages].reshape(DEC_BATCH, n_pages).astype(jnp.int32)
    dt = jnp.exp(jax.random.uniform(ks[11], (DEPTH, N_GDN_HEADS), f32, math.log(1e-3), math.log(1e-1)))
    return {
        'x_prompt': nrm(ks[0], (BATCH, SEQ, D_MODEL), 1.0),
        'x_sample': nrm(ks[1], (DEC_BATCH, DEC_SEQ, D_MODEL), 1.0),
        'cache_kv': nrm(ks[2], (DEPTH, n_pool, N_KV_HEADS, PAGE_SIZE, 4, HEAD_DIM), 1.0),
        'page_table': page_table,
        'state_win': nrm(ks[4], (DEPTH, DEC_BATCH, win_buf, 2, N_KV_HEADS, HEAD_DIM), 1.0),
        'state_gdn': nrm(ks[5], (DEPTH, DEC_BATCH, N_GDN_HEADS, HEAD_DIM, HEAD_DIM), 0.1),
        'state_conv': nrm(ks[6], (DEPTH, DEC_BATCH, CONV_W - 1, 3 * GDN_W), 1.0),
        'norm_mix': 1.0 + nrm(ks[7], (DEPTH, D_MODEL), 0.02),
        'w_in': nrm(ks[8], (DEPTH, D_MODEL, D_PROJ), D_MODEL ** -0.5),
        'conv_w': nrm(ks[9], (DEPTH, CONV_W, 3 * GDN_W), CONV_W ** -0.5),
        'a_log': jnp.log(jax.random.uniform(ks[10], (DEPTH, N_GDN_HEADS), f32, 1.0, 16.0)),
        'dt_bias': dt + jnp.log(-jnp.expm1(-dt)),
        'gdn_norm': 1.0 + nrm(ks[12], (DEPTH, HEAD_DIM), 0.02),
        'cmp_pe_k': nrm(ks[13], (DEPTH, CMP_BLOCK, HEAD_DIM), 0.2),
        'cmp_w_k': nrm(ks[14], (DEPTH, CMP_BLOCK, HEAD_DIM, HEAD_DIM), (CMP_BLOCK * HEAD_DIM) ** -0.5),
        'cmp_pe_v': nrm(ks[15], (DEPTH, CMP_BLOCK, HEAD_DIM), 0.2),
        'cmp_w_v': nrm(ks[16], (DEPTH, CMP_BLOCK, HEAD_DIM, HEAD_DIM), (CMP_BLOCK * HEAD_DIM) ** -0.5),
        'w_out': nrm(ks[17], (DEPTH, MIX_WIDTH, D_MODEL), MIX_WIDTH ** -0.5),
        'norm_mlp': 1.0 + nrm(ks[18], (DEPTH, D_MODEL), 0.02),
        'w_up': nrm(ks[19], (DEPTH, D_MODEL, D_FF), D_MODEL ** -0.5),
        'w_down': nrm(ks[20], (DEPTH, D_FF, D_MODEL), D_FF ** -0.5),
        'norm_final': 1.0 + nrm(ks[21], (D_MODEL,), 0.02),
    }

def reference(x_prompt, x_sample, cache_kv, page_table, state_win, state_gdn, state_conv,
              norm_mix, w_in, conv_w, a_log, dt_bias, gdn_norm, cmp_pe_k, cmp_w_k, cmp_pe_v, cmp_w_v,
              w_out, norm_mlp, w_up, w_down, norm_final):
    xp, xs = x_prompt, x_sample
    rows_p, rows_s, win_p, win_s, gdn_p, gdn_s, conv_p, conv_s = [], [], [], [], [], [], [], []
    for l in range(DEPTH):
        lp = {'norm_mix': norm_mix[l], 'w_in': w_in[l], 'conv_w': conv_w[l], 'a_log': a_log[l],
              'dt_bias': dt_bias[l], 'gdn_norm': gdn_norm[l], 'cmp_pe_k': cmp_pe_k[l], 'cmp_w_k': cmp_w_k[l],
              'cmp_pe_v': cmp_pe_v[l], 'cmp_w_v': cmp_w_v[l], 'w_out': w_out[l], 'norm_mlp': norm_mlp[l],
              'w_up': w_up[l], 'w_down': w_down[l]}
        xp, r, w, s, c = prompt_layer(xp, lp)
        rows_p.append(r)
        win_p.append(w)
        gdn_p.append(s)
        conv_p.append(c)
        xs, r, w, s, c = sample_layer(xs, lp, cache_kv[l], page_table, state_win[l], state_gdn[l], state_conv[l])
        rows_s.append(r)
        win_s.append(w)
        gdn_s.append(s)
        conv_s.append(c)
    y_prompt = rmsnorm(xp, norm_final)
    y_sample = rmsnorm(xs, norm_final)
    return (y_prompt, y_sample, jnp.stack(rows_p), jnp.stack(rows_s), jnp.stack(win_p), jnp.stack(win_s),
            jnp.stack(gdn_p), jnp.stack(gdn_s), jnp.stack(conv_p), jnp.stack(conv_s))


_drawn_inputs = setup_inputs


def setup_inputs(seed=0):
    import zlib

    import numpy as np

    out = dict(_drawn_inputs(seed))
    spreads = {}
    factors = {}
    for name, (base, spread) in spreads.items():
        noise = np.random.default_rng([zlib.crc32(name.encode()), seed]).standard_normal(out[name].shape)
        drawn = base * np.exp(spread * noise) if base else spread * noise
        out[name] = jnp.asarray(drawn.astype(out[name].dtype))
    for name, factor in factors.items():
        out[name] = (out[name] * factor).astype(out[name].dtype)
    return out
```

```python
from contextlib import ExitStack

import numpy as np

import concourse.bass as bass
from concourse import mybir

F32 = mybir.dt.float32
I32 = mybir.dt.int32
ALU = mybir.AluOpType
ACT = mybir.ActivationFunctionType
AX = mybir.AxisListType

P = 128
D = 1024
SEQ = 512
DEPTH = 2
NB = 8
NT = 4
NS = NB * NT
TOK = SEQ + NS
HALF = TOK // 2
PAST = 256
PAGE = 128
HD = 64
NH = 8
KVH = 2
GQA = NH // KVH
KT = D // P
CONV = 4
CHUNK = 64
CMP = 32
SEL = 64
TOP_K = 16
WINDOW = 512
DFF = 4 * D
EPS = 1e-6
THETA = 10000.0
NEG = -1e30
FLOOR = -1e25
N_POOL = NB * (PAST // PAGE) * 5 // 4
C_QKV = 3 * NH * HD
O_Z = C_QKV
O_AB = O_Z + NH * HD
O_Q = O_AB + 2 * NH
O_KV = O_Q + NH * HD
O_GATE = O_KV + 6 * KVH * HD
D_PROJ = O_GATE + 3 * NH
assert SEQ // SEL <= TOP_K and PAST // SEL + 1 <= TOP_K
assert SEQ <= WINDOW and PAST + NT <= WINDOW
TT = SEQ // P
NCP = SEQ // CMP
NCS = PAST // CMP
assert (PAST + NT) // CMP == NCS
NCA = NCP + NB * NCS
SLOT = 256
NSLOT = 4
GROUP = 1024
NGROUP = DFF // GROUP
BASE = 8
NPG = NB * (PAST // PAGE)
LEVELS = [16, 32, 64]
SCALE = HD ** -0.5
FRONT = 20
SMALLW = 2 * NH + 3 * NH

CONSTS = {}


def _consts():
    k = np.arange(P)[:, None]
    i = np.arange(P)[None, :]
    t = {}
    t["ident"] = (k == i)
    t["ones"] = np.ones((P, P))
    t["headones"] = (k // HD == i // HD)
    for name, c in (("p", CHUNK), ("s", NT)):
        same = k // c == i // c
        t["cum" + name] = same & (k <= i)
        t["seg" + name] = same
        t["neg" + name] = np.where(same & (k <= i), 0.0, NEG)
    t["upper"] = (k // BASE == i // BASE) & (k < i)
    t["lower"] = (k // BASE == i // BASE) & (k > i)
    b = BASE
    while b < CHUNK:
        t["low" + str(2 * b)] = (k // (2 * b) == i // (2 * b)) & (k // b != i // b) & (k > i)
        b *= 2
    t["causal"] = np.where(i <= k, 0.0, NEG)
    end = (np.arange(NCP) + 1) * CMP - 1
    t["cmpneg"] = np.concatenate([np.where(end[None, :] <= k + P * q, 0.0, NEG) for q in range(TT)], 1)
    new = np.arange(NT)[None, :]
    t["newneg"] = np.where(new <= k % NT, 0.0, NEG)
    d, e = k % HD, i % HD
    t["rot"] = (k // HD == i // HD) * ((d == e + HD // 2) * -1.0 + (d == e - HD // 2) * 1.0)
    inv = np.float32(THETA) ** (-np.arange(HD // 2, dtype=np.float32) / np.float32(HD // 2))
    pos = np.concatenate([np.arange(SEQ), np.tile(PAST + np.arange(NT), NB)]).astype(np.float32)
    cpos = np.concatenate([end, np.tile(end[:NCS], NB)]).astype(np.float32)
    freq = inv[np.arange(P) % (HD // 2)].astype(np.float32)
    for name, x in (("", pos), ("c", cpos)):
        ang = (x[None, :] * freq[:, None]).astype(np.float32)
        t["cos" + name] = np.cos(ang)
        t["sin" + name] = np.sin(ang)
    row_b, row_h, row_t = np.arange(P) // 32, np.arange(P) % 32 // NT, np.arange(P) % NT
    for g in range(2):
        t["pick" + str(g)] = (k == ((4 * g + row_b) * NT + row_t)[None, :])
    t["rowhead"] = (row_h[:, None] == np.arange(NH)[None, :])
    t["seqof"] = (k // NT == np.arange(NB)[None, :])
    at, cols = 0, []
    for name, v in t.items():
        v = np.asarray(v, dtype=np.float32)
        CONSTS[name] = (at, v.shape[1])
        at += v.shape[1]
        cols.append(v)
    return np.ascontiguousarray(np.concatenate(cols, 1))


CONST_TABLE = _consts()
NCONST = CONST_TABLE.shape[1]


class Signal:

    def __init__(self, sem):
        self.sem, self.n = sem, 0

    def on(self, instruction):
        instruction.then_inc(self.sem, 1)
        self.n += 1
        return self.n


def build(nc, A, O):
    ctx = ExitStack()
    with ctx:
        def sb(name, shape, dt=F32, into=ctx):
            return into.enter_context(nc.sbuf_tensor(name, shape, dt))

        signals = {}

        def S(name):
            if name not in signals:
                signals[name] = Signal(ctx.enter_context(nc.semaphore(name)))
            return signals[name]

        setup = ctx.enter_context(nc.semaphore("setup_loaded"))
        ps = ctx.enter_context(nc.psum_tensor("ps", [P, 8, 512], F32))

        xT = sb("xT_sb", [P, KT, TOK])
        hT = sb("hT", [P, KT, TOK])
        mixT = sb("mixT", [P, KT, TOK])
        wring = sb("wring", [P, NSLOT, KT * SLOT])
        cst = sb("cst", [P, NCONST])
        pages = sb("pages", [1, NPG], I32)
        gmix = sb("gmix", [P, KT])
        gmlp = sb("gmlp", [P, KT])
        gfin = sb("gfin", [P, KT])
        ggdn = sb("ggdn", [P, 1])
        convw = sb("convw", [P, 12, CONV])
        dtb = sb("dtb", [P, NH])
        alog = sb("alog", [P, NH])
        tok_small = sb("tok_small", [P, TT + 1, SMALLW])
        sig = sb("sig", [P, TT + 1, 4 * NH])
        rs = sb("rs", [P, TOK])
        Eg = mixT[:, 4:8, :]
        osq = mixT[:, 4:8, :]

        def C(name, rows=P, cols=None):
            at, n = CONSTS[name]
            return cst[0:rows, at:at + (cols or n)]

        def bc(ap, n):
            return ap.unsqueeze(2).to_broadcast([ap.shape[0], ap.shape[1], n])

        def mid(ap, n):
            return ap.unsqueeze(1).to_broadcast([ap.shape[0], n, ap.shape[1]])

        with ExitStack() as gdn_ctx:
            qkv = sb("qkv", [P, 12, TOK], into=gdn_ctx)
            zT = sb("zT", [P, 4, TOK], into=gdn_ctx)
            xs = sb("xs", [P, 12, NB, CONV - 1 + NT], into=gdn_ctx)
            ctail = sb("ctail", [P, 12, 3 + NB * 3], into=gdn_ctx)
            St = sb("St", [P, 4, HD], into=gdn_ctx)
            Stmp = sb("Stmp", [P, 4, HD], into=gdn_ctx)
            gtok = sb("gtok", [P, TT + 1, NH], into=gdn_ctx)
            gt2 = sb("gt2", [P, TT + 1, NH], into=gdn_ctx)
            gt3 = sb("gt3", [P, TT + 1, NH], into=gdn_ctx)
            gcum = sb("gcum", [P, TT + 1, NH], into=gdn_ctx)
            egc = sb("egc", [P, TT + 1, NH], into=gdn_ctx)
            edec = sb("edec", [P, TT + 1, NH], into=gdn_ctx)
            qkm = sb("qkm", [P, NH, P], into=gdn_ctx)
            kdec = sb("kdec", [P, NH, HD], into=gdn_ctx)
            kb = sb("kb", [P, NH, HD], into=gdn_ctx)
            vtok = sb("vtok", [P, NH, HD], into=gdn_ctx)
            u0 = sb("u0", [P, NH, HD], into=gdn_ctx)
            wqT = sb("wqT", [P, 2, 4, P], into=gdn_ctx)
            u = sb("u", [P, NH, HD], into=gdn_ctx)
            with ExitStack() as prep_ctx:
                names = ["a", "b", "c", "d", "e", "f", "m16", "m32", "m64"]
                prep = {n: sb("prep_" + n, [P, 2, 4, P], into=prep_ctx) for n in names}
            with ExitStack() as conv_ctx:
                pre = sb("pre", [P, 3, TOK], into=conv_ctx)
                sq = sb("sq", [P, 4, TOK], into=conv_ctx)
                cmul = sb("cmul", [P, 12, NS], into=conv_ctx)
                r_a = sb("r_a", [P, 4, TOK], into=conv_ctx)
            with ExitStack() as sample_ctx:
                Ss = sb("Ss", [P, NB, 4, HD], into=sample_ctx)
                um = sb("um", [NS, NH, NB, HD], into=sample_ctx)
                xuT = sb("xuT", [P, 4, 2, NS], into=sample_ctx)
                sadd = sb("sadd", [P, 2, NB, HD], into=sample_ctx)
        with ExitStack() as nsa_ctx:
            nsaT = sb("nsaT", [P, 10, TOK], into=nsa_ctx)
            selp = sb("selp", [P, NB, 2, 2, P], into=nsa_ctx)
            winp = sb("winp", [P, NB, 2, 2 * P], into=nsa_ctx)
            kselT = sb("kselT", [P, NB, PAST + NT], into=nsa_ctx)
            kwinT = sb("kwinT", [P, NB, PAST + NT], into=nsa_ctx)
            vtp = sb("vtp", [P, 2, TT, P], into=nsa_ctx)
            vnew = sb("vnew", [NT, 2, NB, P], into=nsa_ctx)
            ckT = sb("ckT", [P, 2, NCA + 1], into=nsa_ctx)
            ckr = sb("ckr", [P, NCA], into=nsa_ctx)
            cvp = sb("cvp", [NCP, P], into=nsa_ctx)
            cvs = sb("cvs", [NCS, NB, P], into=nsa_ctx)
            pe = sb("pe", [P, 2, CMP], into=nsa_ctx)
            qs = sb("qs", [P, NB, KVH, GQA, NT], into=nsa_ctx)
            pc = sb("pc", [P, NH, NCP], into=nsa_ctx)
            pcT = sb("pcT", [NCP, NH, P], into=nsa_ctx)
            stat = sb("stat", [P, 96], into=nsa_ctx)
            att = sb("att", [P, 2, 2, 512], into=nsa_ctx)
            attT = sb("attT", [P, 2, 512], into=nsa_ctx)
        with ExitStack() as mlp_ctx:
            uT = sb("uT", [P, 8, TOK], into=mlp_ctx)
            rl = sb("rl", [P, 2, TOK], into=mlp_ctx)
        cmp_rows = att[:, :, :, :].rearrange("p a b c -> p (a b c)").rearrange(
            "p (b g s e) -> p b g s e", b=4, g=2, s=2)
        cmpT = hT[:, :, :].rearrange("p a b -> p (a b)")[:, 0:2 * NB * PAST].rearrange(
            "p (s b t) -> p s b t", s=2, b=NB)

        def whole(pair, rows=P):
            return ps[0:rows, 2 * pair:2 * pair + 2, 0:HALF]

        def halves(ap):
            return ap.rearrange("p (a b) -> p a b", a=2)

        def heads4(ap, n):
            return ap.rearrange("p (h i) -> p h i", h=4)[:, :, 0:n]

        def tile_len(q):
            return P if q < TT else NS

        def cols(q):
            return slice(P * q, P * q + tile_len(q))

        def par(h):
            return slice(HD * (h % 2), HD * (h % 2) + HD)

        def wslot(c):
            return wring[:, c % NSLOT, :].rearrange("p (k n) -> p k n", k=KT)

        def front_chunks(l):
            w_in = A["w_in"][l].rearrange("(k p) n -> p k n", p=P)
            w_out = A["w_out"][l]
            out = {}
            for c in range(6):
                out[c] = [(wslot(c), w_in[:, :, SLOT * c:SLOT * (c + 1)])]
            for c in range(2):
                out[6 + c] = [(wslot(6 + c), w_in[:, :, O_Z + SLOT * c:O_Z + SLOT * (c + 1)])]
            out[8] = [(wslot(8)[:, :, 0:2 * NH], w_in[:, :, O_AB:O_AB + 2 * NH]),
                      (wslot(8)[:, :, 2 * NH:SMALLW], w_in[:, :, O_GATE:O_GATE + 3 * NH])]
            for c in range(2):
                out[9 + c] = [(wslot(9 + c)[:, :, P * j + HD * g:P * j + HD * (g + 1)],
                               w_in[:, :, O_Q + HD * (GQA * g + 2 * c + j):O_Q + HD * (GQA * g + 2 * c + j + 1)])
                              for j in range(2) for g in range(KVH)]
            for c in range(3):
                out[11 + c] = [(wslot(11 + c), w_in[:, :, O_KV + SLOT * c:O_KV + SLOT * (c + 1)])]
            for c, name in enumerate(("cmp_w_k", "cmp_w_v")):
                dst = wring[:, (14 + c) % NSLOT, :].rearrange("p (c e) -> p c e", c=CMP)
                src = A[name][l].rearrange("c d e -> d c e")
                out[14 + c] = [(dst[HD * g:HD * (g + 1)], src) for g in range(KVH)]
            for c in range(4):
                n0, n1 = SLOT * c, SLOT * (c + 1)
                gdn = w_out[0:NH * HD, n0:n1].rearrange("(k p) n -> p k n", p=P)
                out[16 + c] = [(wslot(16 + c)[:, 0:4, :], gdn)]
                for g in range(KVH):
                    rows = w_out[(NH + GQA * g) * HD:(NH + GQA * (g + 1)) * HD, n0:n1]
                    out[16 + c].append((wslot(16 + c)[HD * g:HD * (g + 1), 4:8, :],
                                        rows.rearrange("(j d) n -> d j n", d=HD)))
            return out

        parts = {c: len(v) for c, v in front_chunks(0).items()}
        ld = [S(f"weights_in_slot{s}") for s in range(NSLOT)]

        def landed(c):
            return 16 * sum(parts[x] for x in range(c % NSLOT, c + 1, NSLOT))

        front_total = [landed(FRONT - NSLOT + s) for s in range(NSLOT)]

        def used(c):
            if c <= 8:
                return S("proj").sem, min(2 * (c + 1), 17)
            if c <= 13:
                return S("proj").sem, 17 + 2 * (c - 8)
            if c <= 15:
                return S("cmp").sem, c - 13
            return S("res").sem, 2 * (c - 15)

        tiles = [(c, P * j, P) for c in range(8) for j in range(2)] + [(8, 0, SMALLW)]
        tiles += [(c, P * j, P) for c in range(9, 14) for j in range(2)]
        N_GDN = 17
        N_TILES = len(tiles)
        ROPED = (0, 1, 2, 3, 6, 8)
        UNITS = TT * NH
        SCHEDULE = []
        for q in range(TT):
            if q:
                SCHEDULE.append(("w", NH * q - 1))
            SCHEDULE += [("c", q), ("s", NH * q)]
            for h in range(1, NH):
                SCHEDULE += [("s", NH * q + h), ("w", NH * q + h - 1)]
        SCHEDULE.append(("w", UNITS - 1))

        with nc.Block() as block:
            @block.sync
            def _(sp):
                sp.dma_start(cst[:], A["consts"]).then_inc(setup, 16)
                sp.dma_start(xT[:], A["xT"]).then_inc(setup, 16)
                sp.dma_start(pages[:], A["page_table"]).then_inc(setup, 16)
                sp.dma_start(gfin[:], A["norm_final"]).then_inc(setup, 16)
                sp.wait_ge(setup, 64)

        def norm_tensor(t, name, sq_of):
            for k in range(KT):
                t.wait_ge(S(name + "_square").sem, k + 1)
                for h in range(2):
                    x = t.matmul(ps[:, h, 0:HALF], C("ones"), sq_of(k)[:, HALF * h:HALF * (h + 1)],
                                 start=(k == 0), stop=(k == KT - 1), skip_group_check=True)
                S(name + "_sum").on(x)

        def norm_scalar(act, name, sq_of, ring):
            for k in range(KT):
                if k >= ring:
                    act.wait_ge(S(name + "_sum").sem, k - ring + 1)
                S(name + "_square").on(nc.scalar.activation(sq_of(k), xT[:, k, :], ACT.Square))
            act.wait_ge(S(name + "_mean").sem, 1)
            S(name + "_root").on(nc.scalar.activation(rs[:], rs[:], ACT.Sqrt))

        def norm_vector(v, name, g, out, ready):
            v.wait_ge(S(name + "_sum").sem, KT)
            S(name + "_mean").on(v.tensor_scalar(halves(rs[:]), whole(0), 1.0 / D, EPS, ALU.mult, ALU.add))
            v.wait_ge(S(name + "_root").sem, 1)
            S("v_step").on(v.reciprocal(rs[:], rs[:]))
            v.wait_ge(S("v_step").sem, S("v_step").n)
            for k in range(KT):
                S(ready).on(v.scalar_tensor_tensor(out[:, k, :], xT[:, k, :], g[:, k:k + 1], rs[:],
                                                   ALU.mult, ALU.mult))

        with nc.Fori(0, DEPTH) as l:
            with nc.Block() as block:

                @block.sync
                def _(sp):
                    for dst, name in ((gmix, "norm_mix"), (gmlp, "norm_mlp"), (ggdn, "gdn_norm"), (convw, "conv_w")):
                        sp.dma_start(dst[:], A[name][l]).then_inc(S("params").sem, 16)
                    for dst, name in ((dtb, "dt_bias"), (alog, "a_log")):
                        sp.dma_start(dst[:], A[name][l].partition_broadcast(P)).then_inc(S("params").sem, 16)
                    chunks = front_chunks(l)

                    def load(c):
                        if c >= NSLOT:
                            sp.wait_ge(*used(c - NSLOT))
                        for dst, src in chunks[c]:
                            sp.dma_start(dst, src).then_inc(ld[c % NSLOT].sem, 16)

                    load(0)
                    sp.dma_start(xs[:, :, :, 0:3], A["state_conv"][l]).then_inc(S("conv_state_in").sem, 16)
                    for c in range(1, NSLOT):
                        load(c)
                    sp.dma_start(O["win_past"][l], A["state_win"][l][:, NT:PAST]).then_inc(S("window_kept").sem, 16)
                    for c in range(NSLOT, 13):
                        load(c)
                    sp.wait_ge(S("u0_out").sem, 2 * (TT + 1))
                    sp.wait_ge(S("wT_out").sem, 2 * (TT + 1))
                    sp.dma_start(Ss[:], A["state_gdn"][l]).then_inc(S("states_in").sem, 16)
                    sp.wait_ge(S("tail_out").sem, 13)
                    sp.dma_start(O["conv_T"][l], ctail[:]).then_inc(S("gdn_stored").sem, 16)
                    sp.wait_ge(S("state").sem, 2 * TT + 1)
                    sp.dma_start(O["gdn_p"][l], St[:]).then_inc(S("gdn_stored").sem, 16)
                    sp.wait_ge(S("sdS_out").sem, 4)
                    sp.dma_start(O["gdn_s"][l], Ss[:]).then_inc(S("gdn_stored").sem, 16)
                    sp.wait_ge(S("gdn_stored").sem, 48)
                    sp.wait_ge(S("gdn_mixed").sem, 4)
                    load(13)
                    for s, name in enumerate(("cmp_pe_k", "cmp_pe_v")):
                        for g in range(KVH):
                            sp.dma_start(pe[HD * g:HD * (g + 1), s, :], A[name][l]).then_inc(S("pe_in").sem, 16)
                    win = A["state_win"][l].rearrange("b (g p) s h d -> p b g (s h d)", p=P)
                    for b in range(NB):
                        sp.dma_start(winp[:, b], win[:, b]).then_inc(S("window_in").sem, 16)
                    for b in range(NB):
                        if b == 4:
                            sp.wait_ge(S("kpast_turned").sem, 2 * 4)
                        for pg in range(2):
                            i = 2 * b + pg
                            phys = sp.value_load(pages[0:1, i:i + 1], min_val=0, max_val=N_POOL - 1)
                            page = A["cache_kv"][l, bass.ds(phys, 1)]
                            for g in range(KVH):
                                src = page[0, g]
                                cc = slice(HD * g, HD * (g + 1))
                                sp.dma_start(selp[:, b, pg, :, cc], src[:, 2:4, :]).then_inc(S("pages_in").sem, 16)
                                sp.dma_start(cmp_rows[:, b % 4, pg, :, cc], src[:, 0:2, :]).then_inc(S("pages_in").sem, 16)
                    for c in range(14, FRONT):
                        load(c)
                    sp.wait_ge(S("rope_done").sem, len(ROPED))
                    sp.dma_start(O["rows_T"][l], nsaT[:, 4:10, :]).then_inc(S("rows_stored").sem, 16)
                    with sp.Fori(0, NGROUP) as m:
                        up = A["w_up"][l].rearrange("(k p) n -> p k n", p=P)
                        down = A["w_down"][l].rearrange("(m k p) n -> m p k n", p=P, k=8)[m]
                        for c in range(8):
                            if c < 4:
                                sp.wait_ge(S("res").sem, m * 8 + 2 * (c + 1))
                                src = up[:, :, bass.ds(m * GROUP + c * SLOT, SLOT)]
                            else:
                                sp.wait_ge(S("up").sem, m * 8 + 2 * (c - 3))
                                src = down[:, :, (c - 4) * SLOT:(c - 3) * SLOT]
                            sp.dma_start(wslot(c), src).then_inc(ld[c % NSLOT].sem, 16)
                    sp.wait_ge(S("window_kept").sem, 16)
                    sp.wait_ge(S("rows_stored").sem, 16)

                @block.tensor
                def _(t):
                    def mm(out, lhsT, rhs, start=True, stop=True):
                        return t.matmul(out, lhsT, rhs, start=start, stop=stop, skip_group_check=True)

                    def dense(pair, w, src, M=P):
                        for k in range(KT):
                            for h in range(2):
                                x = mm(ps[0:M, 2 * pair + h, 0:HALF], w(k), src[:, k, HALF * h:HALF * (h + 1)],
                                       start=(k == 0), stop=(k == KT - 1))
                        return x

                    norm_tensor(t, "norm1", lambda k: sq[:, k % 4, :])

                    def project(n):
                        c, col, M = tiles[n]
                        t.wait_ge(ld[c % NSLOT].sem, landed(c))
                        if n == 0:
                            t.wait_ge(S("h_ready").sem, KT)
                        if n >= 4:
                            t.wait_ge(S("proj_out").sem, n - 3)
                        S("proj").on(dense(n % 4, lambda k: wslot(c)[:, k, col:col + M], hT, M))

                    for n in range(N_GDN):
                        project(n)

                    for n in range(8):
                        t.wait_ge(S("l2_square").sem, n + 1)
                        t.wait_ge(S("proj_out").sem, N_GDN)
                        if n >= 4:
                            t.wait_ge(S("l2_out").sem, n - 3)
                        for h in range(2):
                            x = mm(ps[:, 2 * (n % 4) + h, 0:HALF], C("headones"),
                                   sq[:, n % 4, HALF * h:HALF * (h + 1)])
                        S("l2_sum").on(x)

                    t.wait_ge(S("l2_out").sem, 8)
                    for q in range(TT + 1):
                        n = tile_len(q)
                        x = t.transpose(ps[0:n, 0, SMALLW * q:SMALLW * (q + 1)],
                                        rs[0:SMALLW, P * q:P * q + n], C("ident", SMALLW, SMALLW))
                    S("small_turned").on(x)

                    t.wait_ge(S("g_ready").sem, 1)
                    for j, m in enumerate(("cum", "seg")):
                        mm(ps[:, 1, 64 * j:64 * j + TT * NH], C(m + "p"),
                           gtok[:, 0:TT, :].rearrange("p a b -> p (a b)"))
                        x = mm(ps[0:NS, 1, 64 * j + TT * NH:64 * j + (TT + 1) * NH], C(m + "s", NS, NS),
                               gtok[0:NS, TT, :])
                    S("gcum_sum").on(x)
                    for q in range(TT + 1):
                        n = tile_len(q)
                        for h in range(NH):
                            x = mm(ps[par(h), 2 + q, P * (h // 2):P * (h // 2) + n],
                                   gtok[0:n, q, h:h + 1].to_broadcast([n, HD]),
                                   C("cump" if q < TT else "cums", n, n))
                        S("gchan_sum").on(x)

                    def prepare(q):
                        n = tile_len(q)
                        if q == 0:
                            t.wait_ge(S("Eg_out").sem, TT + 1)
                            t.wait_ge(S("gates_act").sem, 7)
                            t.wait_ge(S("l2_done").sem, 8)
                        else:
                            t.wait_ge(S("state").sem, 2 * q + 1)
                            t.wait_ge(S("oT_out").sem, 2 * q)
                        for s in range(2):
                            for hp in range(4):
                                x = t.transpose(ps[0:n, s, P * hp:P * (hp + 1)], qkv[:, 4 + 4 * s + hp, cols(q)],
                                                C("ident"))
                        S("kv_turned").on(x)
                        for hf in range(2):
                            b0 = 2 + 3 * hf
                            for h in range(4):
                                hh = 4 * hf + h
                                for s in range(2):
                                    at = 2 * P * s + P * (h // 2)
                                    x = mm(ps[0:n, b0 + h % 2, at:at + n], qkv[par(hh), 4 + hh // 2, cols(q)],
                                           qkv[par(hh), 4 - 4 * s + hh // 2, cols(q)])
                            S("gram").on(x)
                            t.wait_ge(S("gU_ready").sem, 2 * q + hf + 1)
                            S("grow").on(mm(heads4(ps[0:n, b0 + 2, :], n), C("ones", n, n),
                                            prep["d"][0:n, hf, :, 0:n]))

                        def each(bank, lhsT, rhs, hf):
                            for h in range(4):
                                x = mm(ps[0:n, bank, P * h:P * h + n], prep[lhsT][0:n, hf, h, 0:n],
                                       prep[rhs][0:n, hf, h, 0:n])
                            return x

                        def turn(bank, name, hf):
                            for h in range(4):
                                x = t.transpose(ps[0:n, bank, P * h:P * h + n], prep[name][0:n, hf, h, 0:n],
                                                C("ident", n, n))
                            return x

                        for hf in range(2):
                            t.wait_ge(S("B_ready").sem, 2 * q + hf + 1)
                            S("A_turned").on(turn(2 + 3 * hf, "b", hf))
                        for hf in range(2):
                            t.wait_ge(S("D_ready").sem, 2 * q + hf + 1)
                            t.wait_ge(S("AD_ready").sem, 2 * q + hf + 1)
                            S("D2").on(each(3 + 3 * hf, "c", "d", hf))
                        for hf in range(2):
                            t.wait_ge(S("D2_out").sem, 2 * q + hf + 1)
                            S("D2T").on(turn(2 + 3 * hf, "f", hf))
                        for hf in range(2):
                            t.wait_ge(S("ID2T_out").sem, 2 * q + hf + 1)
                            S("P1").on(each(3 + 3 * hf, "c", "e", hf))
                            if q < TT:
                                S("D4").on(each(4 + 3 * hf, "b", "f", hf))
                        if q < TT:
                            for hf in range(2):
                                t.wait_ge(S("ID4_out").sem, 2 * q + hf + 1)
                                S("ID4T").on(turn(2 + 3 * hf, "f", hf))
                            for hf in range(2):
                                t.wait_ge(S("ID4T_out").sem, 2 * q + hf + 1)
                                t.wait_ge(S("P1_out").sem, 2 * q + hf + 1)
                                S("Pn").on(each(3 + 3 * hf, "b", "d", hf))
                            for i, lev in enumerate(LEVELS):
                                cur = "ed"[i % 2]
                                for hf in range(2):
                                    t.wait_ge(S("Pn_out").sem, 2 * (4 * q + i) + hf + 1)
                                    if i == 0:
                                        t.wait_ge(S("M_ready").sem, 2 * q + hf + 1)
                                    S("X").on(each(2 + 3 * hf, "m" + str(lev), cur, hf))
                                    S("PT").on(turn(4 + 3 * hf, cur, hf))
                                for hf in range(2):
                                    t.wait_ge(S("IX_out").sem, 2 * (3 * q + i) + hf + 1)
                                    t.wait_ge(S("PT_out").sem, 2 * (3 * q + i) + hf + 1)
                                    S("Pn").on(each(3 + 3 * hf, "b", "f", hf))
                        t.wait_ge(S("kb_out").sem, 2 * q + 2)
                        t.wait_ge(S("v_out").sem, q + 1)
                        for hf in range(2):
                            if q < TT:
                                t.wait_ge(S("Pn_out").sem, 2 * (4 * q + 3) + hf + 1)
                            else:
                                t.wait_ge(S("P1_out").sem, 2 * q + hf + 1)
                            for h in range(4):
                                hh = 4 * hf + h
                                mm(ps[0:n, 2 + 3 * hf, HD * h:HD * (h + 1)], prep["d"][0:n, hf, h, 0:n],
                                   vtok[0:n, hh, :])
                                x = mm(ps[par(hh), 4 + 3 * hf, P * (h // 2):P * (h // 2) + n],
                                       kb[0:n, hh, :], prep["d"][0:n, hf, h, 0:n])
                            S("wu").on(x)

                    def scan(q):
                        for half in range(2):
                            n = 2 * q + half
                            rows = slice(HD * half, HD * half + HD)
                            t.wait_ge(S("u0_out").sem, 2 * (q + 1))
                            t.wait_ge(S("wT_out").sem, 2 * (q + 1))
                            t.wait_ge(S("state").sem, n + 1)
                            t.wait_ge(S("qe_out").sem, q + 1)
                            for h in range(NH):
                                x = mm(ps[rows, h % 2, HD * (h // 2):HD * (h // 2 + 1)], wqT[par(h), 0, h // 2, rows],
                                       St[par(h), h // 2, :])
                            S("wS").on(x)
                            if n:
                                t.wait_ge(S("oT_out").sem, n)
                            for h in range(NH):
                                x = mm(ps[par(h), 2, HD * (h // 2):HD * (h // 2 + 1)], St[par(h), h // 2, :],
                                       qkv[par(h), h // 2, P * q + HD * half:P * q + HD * (half + 1)])
                            S("oS").on(x)
                            t.wait_ge(S("u_out").sem, n + 1)
                            for h in range(NH):
                                x = mm(ps[par(h), 4, HD * (h // 2):HD * (h // 2 + 1)], kdec[rows, h, :], u[rows, h, :])
                            S("dS").on(x)
                            for h in range(NH):
                                x = mm(ps[par(h), 3, HD * (h // 2):HD * (h // 2 + 1)], u[rows, h, :], qkm[rows, h, rows])
                            S("oU").on(x)

                    for q in range(TT):
                        prepare(q)
                        scan(q)
                    prepare(TT)

                    t.wait_ge(S("u0_out").sem, 2 * (TT + 1))
                    t.wait_ge(S("wT_out").sem, 2 * (TT + 1))
                    t.wait_ge(S("qe_out").sem, TT + 1)
                    t.wait_ge(S("states_in").sem, 16)
                    for b in range(NB):
                        for h in range(NH):
                            out = ps[par(h), 0, 64 * (h // 2):64 * (h // 2 + 1)].rearrange("p (s i) -> p s i", s=2)
                            x = mm(out[:, :, NT * b:NT * (b + 1)], Ss[par(h), b, h // 2, :],
                                   wqT[par(h), :, h // 2, NT * b:NT * (b + 1)])
                    S("sample_mm").on(x)
                    t.wait_ge(S("sample_dve").sem, 1)
                    for hp in range(4):
                        x = t.transpose(ps[0:NS, 1, P * hp:P * (hp + 1)], xuT[:, hp, 0, :], C("ident"))
                    S("sample_mm").on(x)
                    t.wait_ge(S("sample_dve").sem, 2)
                    for h in range(NH):
                        x = mm(ps[par(h), 2, NS * (h // 2):NS * (h // 2 + 1)], u[0:NS, h, :], qkm[0:NS, h, 0:NS])
                    S("sample_mm").on(x)
                    for hp in range(4):
                        for h in (2 * hp, 2 * hp + 1):
                            t.wait_ge(S("um_out").sem, h + 1)
                            x = mm(ps[par(h), 3 + hp, :], kdec[0:NS, h, :], um[:, h, :, :].rearrange("p b e -> p (b e)"))
                        S("sdS").on(x)

                    t.wait_ge(S("sdS_out").sem, 4)
                    for hp in range(4):
                        t.wait_ge(S("o_square").sem, hp + 1)
                        for h in range(2):
                            x = mm(ps[:, 2 * hp + h, 0:HALF], C("headones"), osq[:, hp, HALF * h:HALF * (h + 1)])
                        S("o_sum").on(x)

                    t.wait_ge(S("gdn_mixed").sem, 4)
                    for n in range(N_GDN, N_TILES):
                        project(n)
                    t.wait_ge(S("proj_out").sem, N_TILES)
                    for i, n in enumerate(ROPED):
                        if i >= 4:
                            t.wait_ge(S("rope_sin").sem, i - 3)
                        for h in range(2):
                            x = mm(ps[:, 2 * (i % 4) + h, 0:HALF], C("rot"), nsaT[:, n, HALF * h:HALF * (h + 1)])
                        S("rot").on(x)
                    t.wait_ge(S("rope_sin").sem, len(ROPED))
                    for s in range(2):
                        for q in range(TT):
                            x = t.transpose(ps[:, s, P * q:P * (q + 1)], nsaT[:, 7 + 2 * s, P * q:P * (q + 1)],
                                            C("ident"))
                        S("v_turned").on(x)
                    for s in range(2):
                        for b in range(NB):
                            x = t.transpose(ps[0:NT, 2 + 2 * s + b // 4, P * (b % 4):P * (b % 4 + 1)],
                                            nsaT[:, 7 + 2 * s, SEQ + NT * b:SEQ + NT * (b + 1)], C("ident"))
                        S("v_turned").on(x)
                    t.wait_ge(S("window_in").sem, 16 * NB)
                    for i in range(2 * NB):
                        b = i // 2
                        if i % 2 == 0:
                            t.wait_ge(S("pages_in").sem, 16 * 32 if b < 4 else 16 * 64)
                        if i >= 2:
                            t.wait_ge(S("kpast_out").sem, i - 1)
                        bank = 6 + i % 2
                        if i % 2 == 0:
                            for pg in range(2):
                                t.transpose(ps[:, bank, P * pg:P * (pg + 1)], selp[:, b, pg, 0, :], C("ident"))
                                x = t.transpose(ps[:, bank, P * (2 + pg):P * (3 + pg)], winp[:, b, pg, 0:P], C("ident"))
                            S("kpast_turned").on(x)
                        else:
                            for s in range(2):
                                for pg in range(2):
                                    x = t.transpose(ps[:, bank, P * (2 * s + pg):P * (2 * s + pg + 1)],
                                                    cmp_rows[:, b % 4, pg, s, :], C("ident"))
                            S("kpast_turned").on(x)
                    t.wait_ge(S("kpast_out").sem, 2 * NB)
                    t.wait_ge(S("pe_in").sem, 64)
                    t.wait_ge(S("v_copied").sem, 2)
                    for s in range(2):
                        t.wait_ge(ld[(14 + s) % NSLOT].sem, landed(14 + s))
                        w = wring[:, (14 + s) % NSLOT, :].rearrange("p (c e) -> p c e", c=CMP)
                        for g in range(KVH):
                            r = slice(HD * g, HD * (g + 1))
                            for c in range(CMP):
                                mm(ps[r, s, 0:NCP], w[r, c, :],
                                   nsaT[r, 4 + s, 0:SEQ].rearrange("p (n c) -> p n c", c=CMP)[:, :, c],
                                   start=(c == 0), stop=(c == CMP - 1))
                                mm(ps[r, s, NCP:NCA], w[r, c, :],
                                   cmpT[r, s, :, :].rearrange("p b (n c) -> p (b n) c", c=CMP)[:, :, c],
                                   start=False, stop=(c == CMP - 1))
                                x = mm(ps[r, s, NCA:NCA + 1], w[r, c, :], pe[r, s, c:c + 1],
                                       start=False, stop=(c == CMP - 1))
                        S("cmp").on(x)
                    t.wait_ge(S("ck_out").sem, 2)
                    t.wait_ge(S("v_copied").sem, 4)
                    S("ck_rot").on(mm(ps[:, 2, 0:NCA], C("rot"), ckT[:, 0, 0:NCA]))
                    t.transpose(ps[0:NCP, 3, 0:P], ckT[:, 1, 0:NCP], C("ident"))
                    for b in range(NB):
                        x = t.transpose(ps[0:NCS, 4 + b // 4, P * (b % 4):P * (b % 4 + 1)],
                                        ckT[:, 1, NCP + NCS * b:NCP + NCS * (b + 1)], C("ident"))
                    S("cv_turned").on(x)

                    t.wait_ge(S("ck_done").sem, 1)
                    t.wait_ge(S("rope_done").sem, len(ROPED))
                    t.wait_ge(S("cv_out").sem, 2)

                    def compressed(q):
                        if q:
                            t.wait_ge(S("p_exp").sem, 2 * NH * q)
                        for h in range(NH):
                            r = slice(HD * (h // GQA), HD * (h // GQA) + HD)
                            x = mm(ps[:, h // GQA, NCP * (h % GQA):NCP * (h % GQA + 1)],
                                   nsaT[r, h % GQA, P * q:P * (q + 1)], ckr[r, 0:NCP])
                        S("cs").on(x)
                        t.wait_ge(S("pc_ready").sem, q + 1)
                        for h in range(NH):
                            x = t.transpose(ps[0:NCP, 2 + h // 4, P * (h % 4):P * (h % 4 + 1)], pc[:, h, :], C("ident"))
                        S("pc_turned").on(x)

                    def scores(uu):
                        q, h = divmod(uu, NH)
                        r = slice(HD * (h // GQA), HD * (h // GQA) + HD)
                        if h == 0:
                            t.wait_ge(S("pcT_out").sem, q + 1)
                        if uu >= 2:
                            t.wait_ge(S("p_exp").sem, 2 * (uu - 1))
                        for s in range(2):
                            x = mm(ps[:, 2 * (uu % 2) + s, 0:P * (q + 1)], nsaT[r, h % GQA, P * q:P * (q + 1)],
                                   nsaT[r, 6 + 2 * s, 0:P * (q + 1)])
                        S("score").on(x)

                    def weigh(uu):
                        q, h = divmod(uu, NH)
                        g = h // GQA
                        for s in range(2):
                            t.wait_ge(S("p_scaled").sem, 2 * uu + s + 1)
                            if uu:
                                t.wait_ge(S(f"pT_out{s}").sem, uu)
                            for kt in range(q + 1):
                                x = t.transpose(ps[:, 4 + s, P * kt:P * (kt + 1)],
                                                att[:, uu % 2, s, P * kt:P * (kt + 1)], C("ident"))
                            S("pT").on(x)
                        if uu >= 2:
                            t.wait_ge(S("nsa_out").sem, uu - 1)
                        out = ps[HD * g:HD * (g + 1), 6 + uu % 2, 0:P]
                        mm(out, cvp[:, HD * g:HD * (g + 1)], pcT[:, h, :], stop=False)
                        for s in range(2):
                            t.wait_ge(S(f"pT_out{s}").sem, uu + 1)
                            for kt in range(q + 1):
                                x = mm(out, vtp[:, s, kt, HD * g:HD * (g + 1)], attT[:, s, P * kt:P * (kt + 1)],
                                       start=False, stop=(s == 1 and kt == q))
                        S("nsa").on(x)

                    for what, i in SCHEDULE:
                        {"c": compressed, "s": scores, "w": weigh}[what](i)
                    t.wait_ge(S("nsa_out").sem, UNITS)

                    t.wait_ge(S("qs_ready").sem, 3)
                    t.wait_ge(S("knew_out").sem, 2)
                    for g in range(2):
                        for b4 in range(4):
                            b = 4 * g + b4
                            q32 = qs[:, b, :, :, :].rearrange("p a b c -> p (a b c)")
                            r = slice(32 * b4, 32 * b4 + 32)
                            mm(ps[r, 0, 0:PAST + NT], q32, kselT[:, b, :])
                            mm(ps[r, 1, 0:PAST + NT], q32, kwinT[:, b, :])
                            mm(ps[r, 2, 0:NCS], q32, ckr[:, NCP + NCS * b:NCP + NCS * (b + 1)])
                        S("ss").on(mm(ps[:, 3, 0:3 * NH], C("pick" + str(g), NS), sig[0:NS, TT, NH:4 * NH]))
                        t.wait_ge(S("sp_ready").sem, 3 * (g + 1))
                        for s in range(2):
                            for i, (a, n) in enumerate(((0, P), (P, P), (PAST, NT))):
                                t.transpose(ps[0:n, 4 + s, P * i:P * (i + 1)], att[:, 0, s, a:a + n], C("ident"))
                        x = t.transpose(ps[0:NCS, 6, 0:P], att[:, 1, 0, 0:NCS], C("ident"))
                        S("spT").on(x)
                        t.wait_ge(S("spT_out").sem, 5 * (g + 1))
                        for b4 in range(4):
                            b = 4 * g + b4
                            c = slice(32 * b4, 32 * b4 + 32)
                            out = ps[:, 7, 32 * b:32 * b + 32]
                            mm(out, cvs[:, b, :], att[0:NCS, 1, 1, c], stop=False)
                            for s in range(2):
                                for pg in range(2):
                                    v = selp[:, b, pg, 1, :] if s == 0 else winp[:, b, pg, P:2 * P]
                                    mm(out, v, attT[:, s, P * pg + 32 * b4:P * pg + 32 * b4 + 32], start=False, stop=False)
                                x = mm(out, vnew[:, s, b, :], attT[0:NT, s, 2 * P + 32 * b4:2 * P + 32 * b4 + 32],
                                       start=False, stop=(s == 1))
                        S("so_att").on(x)

                    t.wait_ge(S("nsa_mixed").sem, 2)
                    for d in range(KT):
                        c = 16 + d // 2
                        t.wait_ge(ld[c % NSLOT].sem, landed(c))
                        if d >= 4:
                            t.wait_ge(S("res_added").sem, d - 3)
                        col = P * (d % 2)
                        S("res").on(dense(d % 4, lambda k: wslot(c)[:, k, col:col + P], mixT))
                    t.wait_ge(S("res_added").sem, KT)

                    norm_tensor(t, "norm2", lambda k: mixT[:, k, :])
                    t.wait_ge(S("h2_ready").sem, KT)
                    with t.Fori(0, NGROUP) as m:
                        for i in range(16):
                            c = i // 2
                            t.wait_ge(ld[c % NSLOT].sem, m * 32 + (front_total[c % NSLOT] + 16 * (c // 4 + 1)))
                            if i < 4:
                                t.wait_ge(S("res_added").sem, m * 8 + (5 + i))
                            elif i < 12:
                                t.wait_ge(S("relu_done").sem, m * 8 + (i - 3))
                            else:
                                t.wait_ge(S("res_added").sem, m * 8 + (8 + i - 11))
                            if i == 8:
                                t.wait_ge(S("u_ready").sem, m * 8 + 8)
                            col = P * (i % 2)
                            dense(i % 4, lambda k: wslot(c)[:, k, col:col + P], hT if i < 8 else uT
                                  ).then_inc(S("up" if i < 8 else "res").sem, 1)

                @block.scalar
                def _(act):
                    A1 = nc.scalar.activation
                    norm_scalar(act, "norm1", lambda k: sq[:, k % 4, :], 4)
                    act.wait_ge(S("params").sem, 16 * 6)

                    def out_of(n, rows=P):
                        act.wait_ge(S("proj").sem, n + 1)
                        return whole(n % 4, rows)

                    for n in range(12):
                        src = out_of(n)
                        if n >= 3:
                            act.wait_ge(S("conv_done").sem, n - 2)
                            act.wait_ge(S("tail_out").sem, n - 2)
                        S("pre_out").on(A1(halves(pre[:, n % 3, :]), src, ACT.Copy))
                        S("proj_out").on(A1(halves(qkv[:, n, :]), src, ACT.Copy, scale=convw[:, n, CONV - 1:CONV]))
                    for n in range(12, 16):
                        S("proj_out").on(A1(halves(zT[:, n - 12, :]), out_of(n), ACT.Silu))
                    act.wait_ge(S("h_ready").sem, KT)
                    S("proj_out").on(A1(halves(rs[0:SMALLW, :]), out_of(16, SMALLW), ACT.Copy))
                    act.wait_ge(S("conv_done").sem, 12)
                    act.wait_ge(S("sconv_done").sem, 1)
                    for n in range(12):
                        S("silu").on(A1(qkv[:, n, :], qkv[:, n, :], ACT.Silu))

                    def l2_square(n):
                        if n >= 4:
                            act.wait_ge(S("l2_sum").sem, n - 3)
                        act.wait_ge(S("silu").sem, n + 1)
                        S("l2_square").on(A1(sq[:, n % 4, :], qkv[:, n, :], ACT.Square))

                    for n in range(4):
                        l2_square(n)
                    for n in range(8):
                        if n + 4 < 8:
                            l2_square(n + 4)
                        act.wait_ge(S("l2_out").sem, n + 1)
                        S("l2_root").on(A1(r_a[:, n % 4, :], r_a[:, n % 4, :], ACT.Sqrt))

                    act.wait_ge(S("small_turned").sem, 1)
                    act.wait_ge(S("zeroed").sem, 4)
                    W4 = TT * SMALLW
                    A1(tok_small[:, 0:TT, :].rearrange("p a b -> p (a b)"), ps[:, 0, 0:W4], ACT.Copy)
                    S("gates_act").on(A1(tok_small[0:NS, TT, :], ps[0:NS, 0, W4:W4 + SMALLW], ACT.Copy))
                    S("gates_act").on(A1(alog[:], alog[:], ACT.Exp))
                    act.wait_ge(S("gates_act").sem, 1)
                    S("gates_act").on(A1(sig[:], tok_small[:, :, NH:SMALLW], ACT.Exp, scale=-1.0))
                    act.wait_ge(S("absx").sem, 1)
                    S("gates_act").on(A1(gt3[:], gt3[:], ACT.Exp, scale=-1.0))
                    act.wait_ge(S("gates_act").sem, 4)
                    S("gates_act").on(A1(gt3[:], gt3[:], ACT.Ln, bias=1.0))
                    act.wait_ge(S("gcum_out").sem, 1)
                    S("gates_act").on(A1(egc[:], gcum[:], ACT.Exp))
                    act.wait_ge(S("gdiff").sem, 1)
                    S("gates_act").on(A1(edec[:], edec[:], ACT.Exp))
                    for q in range(TT + 1):
                        n = tile_len(q)
                        act.wait_ge(S("gchan_sum").sem, q + 1)
                        S("Eg_out").on(A1(Eg[:, :, cols(q)], heads4(ps[:, 2 + q, :], n), ACT.Exp))

                    def prepare(q):
                        n = tile_len(q)

                        def out(sem, name, hf, bank, wait):
                            act.wait_ge(S(wait).sem, S(sem).n + 1)
                            S(sem).on(A1(prep[name][0:n, hf, :, 0:n], heads4(ps[0:n, bank, :], n), ACT.Copy))

                        act.wait_ge(S("kv_turned").sem, q + 1)
                        S("v_out").on(A1(vtok[0:n].rearrange("p h d -> p (h d)"), ps[0:n, 1, :], ACT.Copy))
                        for hf in range(2):
                            act.wait_ge(S("G_masked").sem, 2 * q + hf + 1)
                            S("E_ready").on(A1(prep["a"][0:n, hf, :, 0:n], prep["a"][0:n, hf, :, 0:n], ACT.Exp))
                        for hf in range(2):
                            out("A_out", "a", hf, 2 + 3 * hf, "A_turned")
                        for hf in range(2):
                            out("D2_out", "f", hf, 3 + 3 * hf, "D2")
                        for hf in range(2):
                            out("D2T_out", "b", hf, 2 + 3 * hf, "D2T")
                        if q < TT:
                            for hf in range(2):
                                out("ID4T_out", "b", hf, 2 + 3 * hf, "ID4T")
                            for i in range(3):
                                for hf in range(2):
                                    out("PT_out", "b", hf, 4 + 3 * hf, "PT")
                        for hf in range(2):
                            act.wait_ge(S("wu").sem, 2 * q + hf + 1)
                            S("wT_out").on(A1(wqT[:, 0, 2 * hf:2 * hf + 2, 0:n],
                                              ps[:, 4 + 3 * hf, 0:2 * P].rearrange("p (a i) -> p a i", a=2)[:, :, 0:n],
                                              ACT.Copy))

                    for q in range(TT):
                        prepare(q)
                        for half in range(2):
                            n = 2 * q + half
                            act.wait_ge(S("oS").sem, n + 1)
                            S("oS_out").on(A1(mixT[:, 0:4, HD * n:HD * (n + 1)],
                                              ps[:, 2, 0:4 * HD].rearrange("p (a i) -> p a i", a=4), ACT.Copy))
                    prepare(TT)

                    act.wait_ge(S("sample_dve").sem, 3)
                    act.wait_ge(S("sadd_out").sem, 4)
                    act.wait_ge(S("oT_out").sem, 2 * TT)
                    for hp in range(4):
                        S("o_square").on(A1(osq[:, hp, :], mixT[:, hp, :], ACT.Square))
                    for hp in range(4):
                        act.wait_ge(S("o_mean").sem, hp + 1)
                        S("o_root").on(A1(qkv[:, 8 + hp, :], qkv[:, 8 + hp, :], ACT.Sqrt))

                    act.wait_ge(S("gdn_stored").sem, 48)
                    for n in range(N_GDN, N_TILES):
                        S("proj_out").on(A1(halves(nsaT[:, n - N_GDN, :]), out_of(n), ACT.Copy))
                    for s in range(2):
                        act.wait_ge(S("v_turned").sem, s + 1)
                        S("v_copied").on(A1(vtp[:, s].rearrange("p a b -> p (a b)"), ps[:, s, :], ACT.Copy))
                    for s in range(2):
                        act.wait_ge(S("v_turned").sem, s + 3)
                        S("v_copied").on(A1(vnew[:, s].rearrange("p (a b) e -> p a (b e)", a=2),
                                          ps[0:NT, 2 + 2 * s:4 + 2 * s, :], ACT.Copy))
                    act.wait_ge(S("cv_turned").sem, 1)
                    S("cv_out").on(A1(cvp[:], ps[0:NCP, 3, 0:P], ACT.Copy))
                    S("cv_out").on(A1(cvs[:].rearrange("p (a b) e -> p a (b e)", a=2), ps[0:NCS, 4:6, :], ACT.Copy))

                    def compressed(q):
                        act.wait_ge(S("c_max").sem, q + 1)
                        S("c_exp").on(A1(pc[:], pc[:], ACT.Exp, scale=SCALE))
                        act.wait_ge(S("pc_turned").sem, q + 1)
                        S("pcT_out").on(A1(pcT[:].rearrange("p (a b) e -> p a (b e)", a=2), ps[0:NCP, 2:4, :], ACT.Copy))

                    def scores(uu):
                        q, n, z = uu // NH, P * (uu // NH + 1), uu % 2
                        act.wait_ge(S("p_max").sem, uu + 1)
                        if uu >= 2:
                            act.wait_ge(S("pT").sem, 2 * (uu - 1))
                        for s in range(2):
                            S("p_exp").on(A1(att[:, z, s, 0:n], ps[:, 2 * z + s, 0:n], ACT.Exp,
                                             bias=stat[:, 8 * z + 2 + s:8 * z + 3 + s], scale=SCALE,
                                             accum_out=stat[:, 8 * z + 4 + s:8 * z + 5 + s]))

                    def weigh(uu):
                        q, h = divmod(uu, NH)
                        n, g = P * (q + 1), h // GQA
                        act.wait_ge(S("pT").sem, 2 * uu + 1)
                        if uu:
                            act.wait_ge(S("nsa").sem, uu)
                        S("pT_out0").on(A1(attT[:, 0, 0:n], ps[:, 4, 0:n], ACT.Copy))
                        act.wait_ge(S("nsa").sem, uu + 1)
                        r = slice(HD * g, HD * (g + 1))
                        S("nsa_out").on(A1(mixT[r, 4 + h % GQA, P * q:P * (q + 1)], ps[r, 6 + uu % 2, 0:P], ACT.Copy))

                    for what, i in SCHEDULE:
                        {"c": compressed, "s": scores, "w": weigh}[what](i)

                    for g in range(2):
                        act.wait_ge(S("s_max").sem, g + 1)
                        A1(att[:, 1, 0, 0:NCS], ps[:, 2, 0:NCS], ACT.Exp, bias=stat[:, 27:28], scale=SCALE,
                           accum_out=stat[:, 30:31])
                        for s in range(2):
                            x = A1(att[:, 0, s, 0:PAST + NT], ps[:, s, 0:PAST + NT], ACT.Exp,
                                   bias=stat[:, 28 + s:29 + s], scale=SCALE, accum_out=stat[:, 31 + s:32 + s])
                        S("s_exp").on(x)
                        act.wait_ge(S("spT").sem, g + 1)
                        S("spT_out").on(A1(att[0:NCS, 1, 1, 0:P], ps[0:NCS, 6, 0:P], ACT.Copy))
                        for s in range(2):
                            S("spT_out").on(A1(attT[:, s, 0:2 * P], ps[:, 4 + s, 0:2 * P], ACT.Copy))
                            S("spT_out").on(A1(attT[0:NT, s, 2 * P:3 * P], ps[0:NT, 4 + s, 2 * P:3 * P], ACT.Copy))

                    act.wait_ge(S("res_added").sem, KT)
                    norm_scalar(act, "norm2", lambda k: mixT[:, k, :], KT)
                    act.wait_ge(S("rows_stored").sem, 16)
                    with act.Fori(0, NGROUP) as m:
                        for i in range(8):
                            act.wait_ge(S("up").sem, m * 8 + (i + 1))
                            A1(halves(rl[:, i % 2, :]), whole(i % 4), ACT.Relu).then_inc(S("relu_done").sem, 1)
                            act.wait_ge(S("relu_done").sem, m * 8 + (i + 1))
                            A1(uT[:, i, :], rl[:, i % 2, :], ACT.Square).then_inc(S("u_ready").sem, 1)

                @block.vector
                def _(v):
                    def done(sem, instruction):
                        S(sem).on(instruction)
                        v.wait_ge(S(sem).sem, S(sem).n)

                    S("zeroed").on(v.memset(tok_small[:], 0.0))
                    S("zeroed").on(v.memset(gcum[:], 0.0))
                    S("zeroed").on(v.memset(edec[:], 0.0))
                    S("zeroed").on(v.memset(gt2[:], 0.0))
                    S("state").on(v.memset(St[:], 0.0))
                    v.wait_ge(S("params").sem, 16 * 6)
                    norm_vector(v, "norm1", gmix, hT, "h_ready")

                    for n in range(12):
                        v.wait_ge(S("pre_out").sem, n + 1)
                        v.wait_ge(S("proj_out").sem, n + 1)
                        for s in range(1, CONV):
                            x = v.scalar_tensor_tensor(qkv[:, n, s:SEQ], pre[:, n % 3, 0:SEQ - s],
                                                       convw[:, n, CONV - 1 - s:CONV - s], qkv[:, n, s:SEQ],
                                                       ALU.mult, ALU.add)
                            done("v_step" if s < CONV - 1 else "conv_done", x)

                    def l2_sum(n):
                        v.wait_ge(S("l2_sum").sem, n + 1)
                        if n >= 4:
                            v.wait_ge(S("l2_done").sem, n - 3)
                        S("l2_out").on(v.tensor_scalar(halves(r_a[:, n % 4, :]), whole(n % 4), EPS, None, ALU.add))

                    def l2_scale(n):
                        v.wait_ge(S("l2_root").sem, n + 1)
                        done("v_step", v.reciprocal(r_a[:, n % 4, :], r_a[:, n % 4, :]))
                        S("l2_done").on(v.scalar_tensor_tensor(qkv[:, n, :], qkv[:, n, :], SCALE if n < 4 else 1.0,
                                                               r_a[:, n % 4, :], ALU.mult, ALU.mult))

                    for n in range(9):
                        if n < 8:
                            l2_sum(n)
                        if n:
                            l2_scale(n - 1)

                    v.wait_ge(S("gates_act").sem, 1)
                    done("v_step", v.tensor_tensor(gt2[:], tok_small[:, :, 0:NH], mid(dtb[:], TT + 1), ALU.add))
                    done("v_step", v.tensor_scalar(gt3[:], gt2[:], -1.0, None, ALU.mult))
                    done("absx", v.tensor_tensor(gt3[:], gt3[:], gt2[:], ALU.max))
                    v.wait_ge(S("gates_act").sem, 3)
                    done("v_step", v.tensor_scalar(sig[:], sig[:], 1.0, None, ALU.add))
                    done("v_step", v.reciprocal(sig[:], sig[:]))
                    v.wait_ge(S("gates_act").sem, 5)
                    done("v_step", v.scalar_tensor_tensor(gt2[:], gt2[:], 0.0, gt3[:], ALU.max, ALU.add))
                    v.wait_ge(S("gates_act").sem, 2)
                    done("v_step", v.tensor_tensor(gtok[:], gt2[:], mid(alog[:], TT + 1), ALU.mult))
                    done("g_ready", v.tensor_scalar(gtok[:], gtok[:], -1.0, None, ALU.mult))
                    v.wait_ge(S("gcum_sum").sem, 1)
                    NG = TT * NH

                    def flat(ap):
                        return ap.rearrange("p a b -> p (a b)")

                    v.tensor_copy(flat(gcum[:, 0:TT, :]), ps[:, 1, 0:NG])
                    done("gcum_out", v.tensor_copy(gcum[0:NS, TT, :], ps[0:NS, 1, NG:NG + NH]))
                    v.tensor_tensor(flat(edec[:, 0:TT, :]), ps[:, 1, 64:64 + NG], flat(gcum[:, 0:TT, :]), ALU.subtract)
                    done("gdiff", v.tensor_tensor(edec[0:NS, TT, :], ps[0:NS, 1, 64 + NG:64 + NG + NH],
                                                  gcum[0:NS, TT, :], ALU.subtract))

                    def prepare(q):
                        n = tile_len(q)

                        def pr(name, hf):
                            return prep[name][0:n, hf, :, 0:n]

                        def bank(b):
                            return heads4(ps[0:n, b, :], n)

                        v.wait_ge(S("kv_turned").sem, q + 1)
                        v.wait_ge(S("gates_act").sem, 7)
                        k_ps = ps[0:n, 0, :].rearrange("p (h d) -> p h d", h=NH)
                        S("kb_out").on(v.tensor_tensor(kb[0:n], k_ps, bc(egc[0:n, q, :], HD), ALU.mult))
                        S("kb_out").on(v.tensor_tensor(kdec[0:n], k_ps, bc(edec[0:n, q, :], HD), ALU.mult))
                        for hf in range(2):
                            v.wait_ge(S("grow").sem, 2 * q + hf + 1)
                            S("G_diff").on(v.tensor_tensor(pr("a", hf), bank(4 + 3 * hf),
                                                           bc(gcum[0:n, q, 4 * hf:4 * hf + 4], n), ALU.subtract))
                        for hf in range(2):
                            v.wait_ge(S("E_ready").sem, 2 * q + hf + 1)
                            b0 = 2 + 3 * hf

                            def gram(s):
                                return ps[0:n, b0:b0 + 2, 2 * P * s:2 * P * (s + 1)].rearrange(
                                    "p b (a i) -> p a b i", a=2)[:, :, :, 0:n]

                            def pairs(ap):
                                return ap.rearrange("p (a b) i -> p a b i", b=2)

                            v.tensor_tensor(pairs(qkm[0:n, 4 * hf:4 * hf + 4, 0:n]), gram(1), pairs(pr("a", hf)), ALU.mult)
                            S("GE_out").on(v.tensor_tensor(pairs(pr("b", hf)), gram(0), pairs(pr("a", hf)), ALU.mult))
                        for hf in range(2):
                            v.wait_ge(S("B_ready").sem, 2 * q + hf + 1)
                            done("v_step", v.tensor_tensor(pr("d", hf), pr("b", hf), mid(C("upper", n, n), 4), ALU.mult))
                            S("D_ready").on(v.tensor_tensor(pr("e", hf), mid(C("ident", n, n), 4), pr("d", hf),
                                                            ALU.subtract))
                        for hf in range(2):
                            v.wait_ge(S("P1").sem, 2 * q + hf + 1)
                            v.wait_ge(S("D_ready").sem, 2 * q + 2)
                            S("P1_out").on(v.tensor_copy(pr("d", hf), bank(3 + 3 * hf)))
                            if q < TT:
                                v.wait_ge(S("D4").sem, 2 * q + hf + 1)
                                S("ID4_out").on(v.tensor_tensor(pr("f", hf), bank(4 + 3 * hf),
                                                                mid(C("ident", n, n), 4), ALU.add))
                        if q < TT:
                            for hf in range(2):
                                v.wait_ge(S("Pn").sem, 2 * 4 * q + hf + 1)
                                S("Pn_out").on(v.tensor_copy(pr("e", hf), bank(3 + 3 * hf)))
                            for i in range(3):
                                for hf in range(2):
                                    v.wait_ge(S("X").sem, 2 * (3 * q + i) + hf + 1)
                                    S("IX_out").on(v.tensor_tensor(pr("f", hf), mid(C("ident", n, n), 4),
                                                                   bank(2 + 3 * hf), ALU.subtract))
                                for hf in range(2):
                                    v.wait_ge(S("Pn").sem, 2 * (4 * q + 1 + i) + hf + 1)
                                    S("Pn_out").on(v.tensor_copy(pr("de"[i % 2], hf), bank(3 + 3 * hf)))
                        for hf in range(2):
                            v.wait_ge(S("wu").sem, 2 * q + hf + 1)
                            S("u0_out").on(v.tensor_copy(u0[0:n, 4 * hf:4 * hf + 4, :],
                                                         ps[0:n, 2 + 3 * hf, 0:4 * HD].rearrange("p (h d) -> p h d", h=4)))

                    for q in range(TT):
                        prepare(q)
                        for half in range(2):
                            n = 2 * q + half
                            r = slice(HD * half, HD * half + HD)
                            v.wait_ge(S("wS").sem, n + 1)
                            v.wait_ge(S("u0_out").sem, 2 * (q + 1))
                            done("v_step", v.tensor_tensor(
                                u[r].rearrange("p (a b) d -> p a b d", b=2), u0[r].rearrange("p (a b) d -> p a b d", b=2),
                                ps[r, 0:2, 0:4 * HD].rearrange("p b (a d) -> p a b d", a=4), ALU.subtract))
                            S("u_out").on(v.tensor_tensor(u[r], u[r], bc(sig[r, q, 0:NH], HD), ALU.mult))
                            v.wait_ge(S("stmp_ready").sem, n + 1)
                            v.wait_ge(S("dS").sem, n + 1)
                            S("state").on(v.tensor_tensor(St[:], ps[:, 4, 0:4 * HD].rearrange("p (a e) -> p a e", a=4),
                                                          Stmp[:], ALU.add))
                            v.wait_ge(S("oS_out").sem, n + 1)
                            v.wait_ge(S("oU").sem, n + 1)
                            o = mixT[:, 0:4, HD * n:HD * (n + 1)]
                            S("oT_out").on(v.tensor_tensor(o, ps[:, 3, 0:4 * HD].rearrange("p (a i) -> p a i", a=4), o,
                                                           ALU.add))
                    prepare(TT)

                    v.wait_ge(S("sample_mm").sem, 1)
                    done("sample_dve", v.tensor_copy(xuT[:], ps[:, 0, 0:256].rearrange("p (a s i) -> p a s i", a=4, s=2)))
                    v.wait_ge(S("sample_mm").sem, 2)
                    v.wait_ge(S("u0_out").sem, 2 * (TT + 1))
                    done("v_step", v.tensor_tensor(u[0:NS], u0[0:NS], ps[0:NS, 1, :].rearrange("p (h d) -> p h d", h=NH),
                                                   ALU.subtract))
                    S("sample_dve").on(v.tensor_tensor(u[0:NS], u[0:NS], bc(sig[0:NS, TT, 0:NH], HD), ALU.mult))
                    v.wait_ge(S("sample_mm").sem, 3)
                    S("sample_dve").on(v.tensor_tensor(mixT[:, 0:4, SEQ:TOK], ps[:, 2, 0:4 * NS].rearrange("p (a i) -> p a i", a=4),
                                                   xuT[:, :, 1, :], ALU.add))
                    for hp in range(4):
                        v.wait_ge(S("sdS").sem, hp + 1)
                        v.wait_ge(S("sadd_out").sem, hp + 1)
                        S("sdS_out").on(v.tensor_tensor(Ss[:, :, hp, :], ps[:, 3 + hp, :].rearrange("p (b e) -> p b e", b=NB),
                                                        sadd[:, hp % 2], ALU.add))
                    for hp in range(4):
                        v.wait_ge(S("o_sum").sem, hp + 1)
                        S("o_mean").on(v.tensor_scalar(halves(qkv[:, 8 + hp, :]), whole(hp), 1.0 / HD, EPS,
                                                       ALU.mult, ALU.add))
                    for hp in range(4):
                        v.wait_ge(S("o_root").sem, hp + 1)
                        done("v_step", v.reciprocal(qkv[:, 8 + hp, :], qkv[:, 8 + hp, :]))
                        done("v_step", v.scalar_tensor_tensor(mixT[:, hp, :], mixT[:, hp, :], ggdn[:, 0:1],
                                                              qkv[:, 8 + hp, :], ALU.mult, ALU.mult))
                        S("gdn_mixed").on(v.tensor_tensor(mixT[:, hp, :], mixT[:, hp, :], zT[:, hp, :], ALU.mult))

                    for i, n in enumerate(ROPED):
                        v.wait_ge(S("rot").sem, i + 1)
                        if i:
                            v.wait_ge(S("rope_done").sem, i)
                        done("rope_sin", v.tensor_tensor(halves(rs[:]), whole(i % 4), halves(C("sin")), ALU.mult))
                        v.wait_ge(S("rope_cos").sem, i + 1)
                        S("rope_done").on(v.tensor_tensor(nsaT[:, n, :], nsaT[:, n, :], rs[:], ALU.add))
                    for i in range(2 * NB):
                        b, bank = i // 2, 6 + i % 2
                        if i % 2 == 0:
                            v.wait_ge(S("kpast_turned").sem, i + 1)
                            v.tensor_copy(kselT[:, b, 0:PAST], ps[:, bank, 0:PAST])
                            S("kpast_out").on(v.tensor_copy(kwinT[:, b, 0:PAST], ps[:, bank, PAST:2 * PAST]))
                        else:
                            v.wait_ge(S("kpast_turned").sem, i + 1)
                            S("kpast_out").on(v.tensor_copy(cmpT[:, :, b, :],
                                                            ps[:, bank, :].rearrange("p (s t) -> p s t", s=2)))
                    for s in range(2):
                        v.wait_ge(S("cmp").sem, s + 1)
                        done("v_step", v.tensor_copy(ckT[:, s, :], ps[:, s, 0:NCA + 1]))
                        S("ck_out").on(v.tensor_scalar(ckT[:, s, 0:NCA], ckT[:, s, 0:NCA], ckT[:, s, NCA:NCA + 1], None,
                                                       ALU.add))
                    v.wait_ge(S("ck_rot").sem, 1)
                    v.wait_ge(S("rope_done").sem, len(ROPED))
                    done("v_step", v.tensor_tensor(rs[:, 0:NCA], ps[:, 2, 0:NCA], C("sinc"), ALU.mult))
                    v.wait_ge(S("ck_cos").sem, 1)
                    S("ck_done").on(v.tensor_tensor(ckr[:], ckr[:], rs[:, 0:NCA], ALU.add))

                    def gates(q):
                        return sig[:, q, NH:4 * NH].rearrange("p (h r) -> p h r", r=3)

                    def compressed(q):
                        v.wait_ge(S("cs").sem, q + 1)
                        s_ps = ps[:, 0:2, 0:GQA * NCP].rearrange("p b (j n) -> p b j n", j=GQA)
                        late = C("cmpneg")[:, NCP * q:NCP * (q + 1)].unsqueeze(1).unsqueeze(1).to_broadcast([P, 2, GQA, NCP])
                        st = stat[:, 40:40 + NH]
                        done("v_step", v.tensor_tensor(pc[:].rearrange("p (b j) n -> p b j n", b=2), s_ps, late, ALU.add))
                        done("v_step", v.tensor_reduce(st, pc[:], AX.X, ALU.max))
                        done("v_step", v.tensor_scalar(st, st, FLOOR, None, ALU.max))
                        done("c_max", v.tensor_tensor(pc[:], pc[:], bc(st, NCP), ALU.subtract))
                        v.wait_ge(S("c_exp").sem, q + 1)
                        done("v_step", v.tensor_reduce(st, pc[:], AX.X, ALU.add))
                        done("v_step", v.tensor_scalar(st, st, 1e-30, None, ALU.max))
                        done("v_step", v.reciprocal(st, st))
                        done("v_step", v.tensor_tensor(st, st, gates(q)[:, :, 0], ALU.mult))
                        S("pc_ready").on(v.tensor_tensor(pc[:], pc[:], bc(st, NCP), ALU.mult))

                    def scores(uu):
                        q, z = uu // NH, uu % 2
                        n = P * (q + 1)
                        v.wait_ge(S("score").sem, uu + 1)
                        both = ps[:, 2 * z:2 * z + 2, :]
                        diag = both[:, :, P * q:P * (q + 1)]
                        done("v_step", v.tensor_tensor(diag, diag, mid(C("causal"), 2), ALU.add))
                        if uu >= 2:
                            v.wait_ge(S("p_exp").sem, 2 * (uu - 1))
                        done("v_step", v.tensor_reduce(stat[:, 8 * z:8 * z + 2], both[:, :, 0:n], AX.X, ALU.max))
                        done("p_max", v.tensor_scalar(stat[:, 8 * z + 2:8 * z + 4], stat[:, 8 * z:8 * z + 2], -SCALE, None,
                                                      ALU.mult))

                    def weigh(uu):
                        (q, h), z = divmod(uu, NH), uu % 2
                        n = P * (q + 1)
                        st, r = stat[:, 8 * z + 4:8 * z + 6], stat[:, 8 * z + 6:8 * z + 8]
                        v.wait_ge(S("p_exp").sem, 2 * (uu + 1))
                        if uu >= 2:
                            v.wait_ge(S("p_scaled").sem, 2 * (uu - 1))
                        done("v_step", v.tensor_scalar(st, st, 1e-30, None, ALU.max))
                        done("v_step", v.reciprocal(r, st))
                        S("p_rs").on(v.tensor_tensor(r, r, gates(q)[:, h, 1:3], ALU.mult))
                        v.wait_ge(S("pT").sem, 2 * uu + 2)
                        if uu:
                            v.wait_ge(S("nsa").sem, uu)
                        S("pT_out1").on(v.tensor_copy(attT[:, 1, 0:n], ps[:, 5, 0:n]))

                    for what, i in SCHEDULE:
                        {"c": compressed, "s": scores, "w": weigh}[what](i)

                    for g in range(2):
                        v.wait_ge(S("ss").sem, g + 1)
                        both = ps[:, 0:2, :]
                        new = both[:, :, PAST:PAST + NT]
                        if g:
                            v.wait_ge(S("sp_ready").sem, 3 * g)
                        done("v_step", v.tensor_tensor(new, new, mid(C("newneg"), 2), ALU.add))
                        v.tensor_reduce(stat[:, 24:25], ps[:, 2, 0:NCS], AX.X, ALU.max)
                        done("v_step", v.tensor_reduce(stat[:, 25:27], both[:, :, 0:PAST + NT], AX.X, ALU.max))
                        done("s_max", v.tensor_scalar(stat[:, 27:30], stat[:, 24:27], -SCALE, None, ALU.mult))
                        done("v_step", v.tensor_tensor(stat[:, 64:64 + 3 * NH].rearrange("p (h r) -> p h r", r=3),
                                                       ps[:, 3, 0:3 * NH].rearrange("p (h r) -> p h r", r=3),
                                                       bc(C("rowhead"), 3), ALU.mult))
                        done("v_step", v.tensor_reduce(stat[:, 33:36], stat[:, 64:64 + 3 * NH].rearrange(
                            "p (h r) -> p r h", r=3), AX.X, ALU.add))
                        v.wait_ge(S("s_exp").sem, g + 1)
                        done("v_step", v.tensor_scalar(stat[:, 30:33], stat[:, 30:33], 1e-30, None, ALU.max))
                        done("v_step", v.reciprocal(stat[:, 36:39], stat[:, 30:33]))
                        done("v_step", v.tensor_tensor(stat[:, 36:39], stat[:, 36:39], stat[:, 33:36], ALU.mult))
                        S("sp_ready").on(v.tensor_scalar(att[:, 1, 0, 0:NCS], att[:, 1, 0, 0:NCS], stat[:, 36:37], None,
                                                         ALU.mult))
                        for s in range(2):
                            S("sp_ready").on(v.tensor_scalar(att[:, 0, s, 0:PAST + NT], att[:, 0, s, 0:PAST + NT],
                                                             stat[:, 37 + s:38 + s], None, ALU.mult))
                    v.wait_ge(S("so_att").sem, 2)
                    for g in range(KVH):
                        r = slice(HD * g, HD * (g + 1))
                        src = ps[r, 7, 0:8 * 32].rearrange("p (b k j t) -> p k j b t", b=NB, k=KVH, j=GQA)[:, g]
                        S("nsa_mixed").on(v.tensor_copy(mixT[r, 4:8, SEQ:TOK].rearrange("p j (b t) -> p j b t", b=NB), src))

                    for d in range(KT):
                        v.wait_ge(S("res").sem, d + 1)
                        S("res_added").on(v.tensor_tensor(halves(xT[:, d, :]), whole(d % 4), halves(xT[:, d, :]), ALU.add))
                    v.wait_ge(S("res_added").sem, KT)
                    norm_vector(v, "norm2", gmlp, hT, "h2_ready")
                    with v.Fori(0, NGROUP) as m:
                        for d in range(KT):
                            v.wait_ge(S("res").sem, m * 8 + (KT + d + 1))
                            v.tensor_tensor(halves(xT[:, d, :]), whole(d % 4), halves(xT[:, d, :]),
                                            ALU.add).then_inc(S("res_added").sem, 1)

                @block.gpsimd
                def _(g_):
                    g = g_

                    def done(sem, instruction):
                        S(sem).on(instruction)
                        g.wait_ge(S(sem).sem, S(sem).n)

                    for n in range(12):
                        g.wait_ge(S("pre_out").sem, n + 1)
                        g.tensor_copy(xs[:, n, :, 3:7], pre[:, n % 3, SEQ:TOK].rearrange("p (b t) -> p b t", b=NB))
                        S("tail_out").on(g.tensor_copy(ctail[:, n, 0:3], pre[:, n % 3, SEQ - 3:SEQ]))
                    g.wait_ge(S("tail_out").sem, 12)
                    g.wait_ge(S("conv_state_in").sem, 16)
                    S("tail_out").on(g.tensor_copy(ctail[:, :, 3:].rearrange("p n (b t) -> p n b t", b=NB), xs[:, :, :, 4:7]))
                    g.wait_ge(S("proj_out").sem, 12)
                    for i in range(CONV - 1):
                        w = convw[:, :, i:i + 1].to_broadcast([P, 12, NS])
                        for b in range(NB):
                            x = g.tensor_tensor(cmul[:, :, NT * b:NT * (b + 1)], xs[:, :, b, i:i + NT],
                                                w[:, :, 0:NT], ALU.mult)
                        done("g_step", x)
                        done("sconv_done" if i == CONV - 2 else "g_step",
                             g.tensor_tensor(qkv[:, :, SEQ:TOK], qkv[:, :, SEQ:TOK], cmul[:], ALU.add))

                    def prepare(q):
                        n = tile_len(q)

                        def pr(name, hf):
                            return prep[name][0:n, hf, :, 0:n]

                        neg = C("negp" if q < TT else "negs", n, n)
                        cum = C("cump" if q < TT else "cums", n, n)
                        g.wait_ge(S("g_ready").sem, 1)
                        g.wait_ge(S("kv_turned").sem, q + 1)
                        for hf in range(2):
                            S("gU_ready").on(g.tensor_tensor(pr("d", hf), mid(cum, 4),
                                                             bc(gtok[0:n, q, 4 * hf:4 * hf + 4], n), ALU.mult))
                        for hf in range(2):
                            g.wait_ge(S("G_diff").sem, 2 * q + hf + 1)
                            S("G_masked").on(g.tensor_tensor(pr("a", hf), pr("a", hf), mid(neg, 4), ALU.add))
                        g.wait_ge(S("gram").sem, 2 * q + 2)
                        g.wait_ge(S("Eg_out").sem, TT + 1)
                        if q < TT:
                            S("qe_out").on(g.tensor_tensor(qkv[:, 0:4, cols(q)], qkv[:, 0:4, cols(q)], Eg[:, :, cols(q)],
                                                           ALU.mult))
                        else:
                            S("qe_out").on(g.tensor_tensor(wqT[:, 1, :, 0:NS], qkv[:, 0:4, cols(q)], Eg[:, :, cols(q)],
                                                           ALU.mult))
                        for hf in range(2):
                            g.wait_ge(S("GE_out").sem, 2 * q + hf + 1)
                            S("B_ready").on(g.tensor_tensor(pr("b", hf), pr("b", hf), bc(sig[0:n, q, 4 * hf:4 * hf + 4], n),
                                                            ALU.mult))
                        for hf in range(2):
                            g.wait_ge(S("A_out").sem, 2 * q + hf + 1)
                            S("AD_ready").on(g.tensor_tensor(pr("c", hf), pr("a", hf), mid(C("lower", n, n), 4), ALU.mult))
                        for hf in range(2):
                            g.wait_ge(S("D2T_out").sem, 2 * q + hf + 1)
                            S("ID2T_out").on(g.tensor_tensor(pr("c", hf), pr("b", hf), mid(C("ident", n, n), 4), ALU.add))
                        if q < TT:
                            for hf in range(2):
                                for lev in LEVELS:
                                    x = g.tensor_tensor(pr("m" + str(lev), hf), pr("a", hf),
                                                        mid(C("low" + str(lev), n, n), 4), ALU.mult)
                                S("M_ready").on(x)
                            for half in range(2):
                                c = 2 * q + half
                                g.wait_ge(S("state").sem, c + 1)
                                last = Eg[:, :, HD * c + HD - 1:HD * c + HD].to_broadcast([P, 4, HD])
                                S("stmp_ready").on(g.tensor_tensor(Stmp[:], St[:], last, ALU.mult))

                    for q in range(TT + 1):
                        prepare(q)
                    g.wait_ge(S("states_in").sem, 16)
                    g.wait_ge(S("sample_dve").sem, 2)
                    for h in range(NH):
                        S("um_out").on(g.tensor_tensor(um[:, h], mid(u[0:NS, h, :], NB), bc(C("seqof", NS), HD), ALU.mult))
                    for hp in range(4):
                        if hp >= 2:
                            g.wait_ge(S("sdS_out").sem, hp - 1)
                        last = Eg[:, hp, SEQ:TOK].rearrange("p (b t) -> p b t", b=NB)[:, :, NT - 1:NT].to_broadcast([P, NB, HD])
                        S("sadd_out").on(g.tensor_tensor(sadd[:, hp % 2], Ss[:, :, hp, :], last, ALU.mult))

                    g.wait_ge(S("proj_out").sem, N_TILES)
                    S("qs_ready").on(g.memset(qs[:], 0.0))
                    for i, n in enumerate(ROPED):
                        g.wait_ge(S("rot").sem, i + 1)
                        S("rope_cos").on(g.tensor_tensor(nsaT[:, n, :], nsaT[:, n, :], C("cos"), ALU.mult))
                    g.wait_ge(S("qs_ready").sem, 1)
                    g.wait_ge(S("rope_done").sem, len(ROPED))
                    for k in range(KVH):
                        r = slice(HD * k, HD * (k + 1))
                        done("qs_ready", g.tensor_copy(qs[r, :, k, :, :], nsaT[r, 0:4, SEQ:TOK].rearrange(
                            "p j (b t) -> p b j t", b=NB)))
                    for n, kT in ((6, kselT), (8, kwinT)):
                        S("knew_out").on(g.tensor_copy(kT[:, :, PAST:PAST + NT],
                                                       nsaT[:, n, SEQ:TOK].rearrange("p (b t) -> p b t", b=NB)))
                    g.wait_ge(S("ck_out").sem, 1)
                    S("ck_cos").on(g.tensor_tensor(ckr[:], ckT[:, 0, 0:NCA], C("cosc"), ALU.mult))
                    for uu in range(UNITS):
                        q, z = uu // NH, uu % 2
                        n = P * (q + 1)
                        g.wait_ge(S("p_rs").sem, uu + 1)
                        for s in range(2):
                            S("p_scaled").on(g.tensor_scalar(att[:, z, s, 0:n], att[:, z, s, 0:n],
                                                             stat[:, 8 * z + 6 + s:8 * z + 7 + s], None, ALU.mult))

            nums = sorted(x.sem.num for x in signals.values())
            assert setup.num not in range(nums[0], nums[-1] + 1)
            nc.gpsimd.sem_clear(range(nums[0], nums[-1] + 1))
            nc.all_engine_barrier()
            for x in signals.values():
                x.n = 0

        last = [ctx.enter_context(nc.semaphore("stored"))]
        with nc.Block() as block:
            @block.tensor
            def _(t):
                norm_tensor(t, "norm1", lambda k: mixT[:, k, :])

            @block.scalar
            def _(act):
                norm_scalar(act, "norm1", lambda k: mixT[:, k, :], KT)

            @block.vector
            def _(v):
                norm_vector(v, "norm1", gfin, hT, "h_ready")

            @block.sync
            def _(sp):
                sp.wait_ge(S("h_ready").sem, KT)
                sp.dma_start(O["yT"], hT[:]).then_inc(last[0], 16)
                sp.wait_ge(last[0], 16)


def kernel(x_prompt, x_sample, cache_kv, page_table, state_win, state_gdn, state_conv, norm_mix, w_in, conv_w,
           a_log, dt_bias, gdn_norm, cmp_pe_k, cmp_w_k, cmp_pe_v, cmp_w_v, w_out, norm_mlp, w_up, w_down,
           norm_final):
    import concourse.bacc as bacc
    from concourse.bass_utils import run_bass_kernel_spmd

    def tiled(a, axis=-1):
        a = np.moveaxis(np.asarray(a), axis, 0)
        return np.moveaxis(a.reshape((a.shape[0] // P, P) + a.shape[1:]), 1, 0)

    L = DEPTH
    x = np.concatenate([np.asarray(x_prompt)[0], np.asarray(x_sample).reshape(NS, D)], 0)
    arrays = {
        "xT": tiled(x),
        "norm_final": tiled(norm_final),
        "norm_mix": np.stack([tiled(a) for a in np.asarray(norm_mix)]),
        "norm_mlp": np.stack([tiled(a) for a in np.asarray(norm_mlp)]),
        "gdn_norm": np.concatenate([np.asarray(gdn_norm)] * 2, 1)[:, :, None],
        "conv_w": np.stack([np.moveaxis(tiled(a), 2, 2) for a in np.asarray(conv_w)]),
        "state_conv": np.stack([tiled(a) for a in np.asarray(state_conv)]),
        "state_gdn": np.asarray(state_gdn).reshape(L, NB, 4, 2, HD, HD).transpose(0, 3, 4, 1, 2, 5).reshape(
            L, P, NB, 4, HD),
        "page_table": np.asarray(page_table).reshape(1, NPG),
        "cmp_pe_k": np.asarray(cmp_pe_k).transpose(0, 2, 1),
        "cmp_pe_v": np.asarray(cmp_pe_v).transpose(0, 2, 1),
        "consts": CONST_TABLE,
        "cache_kv": cache_kv, "state_win": state_win, "w_in": w_in, "a_log": a_log, "dt_bias": dt_bias,
        "cmp_w_k": cmp_w_k, "cmp_w_v": cmp_w_v, "w_out": w_out, "w_up": w_up, "w_down": w_down,
    }
    arrays = {k: np.ascontiguousarray(np.asarray(a)) for k, a in arrays.items()}
    shapes = {
        "yT": (P, KT, TOK), "rows_T": (L, P, 6, TOK), "win_past": (L, NB, PAST - NT, 2, KVH, HD),
        "gdn_p": (L, P, 4, HD), "gdn_s": (L, P, NB, 4, HD), "conv_T": (L, P, 12, 3 + 3 * NB),
    }
    nc = bacc.Bacc("TRN2", target_bir_lowering=False, num_devices=1)
    A = {k: nc.dram_tensor("in_" + k, a.shape, mybir.dt.from_np(a.dtype), kind="ExternalInput").ap()
         for k, a in arrays.items()}
    O = {k: nc.dram_tensor("out_" + k, s, F32, kind="ExternalOutput").ap() for k, s in shapes.items()}
    build(nc, A, O)
    r = run_bass_kernel_spmd(nc, [{"in_" + k: a for k, a in arrays.items()}], core_ids=[0]).results[0]
    o = {k: np.asarray(r["out_" + k]) for k in shapes}

    y = o["yT"].transpose(2, 1, 0).reshape(TOK, D)
    rows = o["rows_T"].reshape(L, KVH, HD, 6, TOK).transpose(0, 1, 4, 3, 2)
    rows_p = rows[:, None, :, 0:SEQ, 0:4]
    rows_s = rows[:, :, SEQ:, 0:4].reshape(L, KVH, NB, NT, 4, HD).transpose(0, 2, 1, 3, 4, 5)
    win_new = rows[:, :, :, 4:6].transpose(0, 2, 3, 1, 4)
    win_p = win_new[:, None, 0:SEQ]
    win_s = np.concatenate([o["win_past"], win_new[:, SEQ:].reshape(L, NB, NT, 2, KVH, HD)], 2)
    gdn_p = o["gdn_p"].reshape(L, 2, HD, 4, HD).transpose(0, 3, 1, 2, 4).reshape(L, 1, NH, HD, HD)
    gdn_s = o["gdn_s"].reshape(L, 2, HD, NB, 4, HD).transpose(0, 3, 4, 1, 2, 5).reshape(L, NB, NH, HD, HD)
    conv = o["conv_T"].transpose(0, 3, 2, 1).reshape(L, 3 + 3 * NB, C_QKV)
    conv_p = conv[:, None, 0:3]
    conv_s = conv[:, 3:].reshape(L, NB, 3, C_QKV)
    return tuple(np.ascontiguousarray(a) for a in (
        y[None, 0:SEQ], y[SEQ:].reshape(NB, NT, D), rows_p, rows_s, win_p, win_s, gdn_p, gdn_s, conv_p, conv_s))
```

```python
from contextlib import ExitStack

import numpy as np

import concourse.bass as bass
from concourse import mybir

F32 = mybir.dt.float32
F32R = mybir.dt.float32r
I32 = mybir.dt.int32
ALU = mybir.AluOpType
ACT = mybir.ActivationFunctionType
AX = mybir.AxisListType

P = 128
D = 1024
SEQ = 512
DEPTH = 2
NB = 8
NT = 4
NS = NB * NT
TOK = SEQ + NS
HALF = TOK // 2
PAST = 256
PAGE = 128
HD = 64
NH = 8
KVH = 2
GQA = NH // KVH
KT = D // P
CONV = 4
CHUNK = 64
CMP = 32
SEL = 64
TOP_K = 16
WINDOW = 512
DFF = 4 * D
EPS = 1e-6
THETA = 10000.0
NEG = -1e30
FLOOR = -1e25
N_POOL = NB * (PAST // PAGE) * 5 // 4
C_QKV = 3 * NH * HD
O_Z = C_QKV
O_AB = O_Z + NH * HD
O_Q = O_AB + 2 * NH
O_KV = O_Q + NH * HD
O_GATE = O_KV + 6 * KVH * HD
D_PROJ = O_GATE + 3 * NH
assert SEQ // SEL <= TOP_K and PAST // SEL + 1 <= TOP_K
assert SEQ <= WINDOW and PAST + NT <= WINDOW
TT = SEQ // P
NCP = SEQ // CMP
NCS = PAST // CMP
assert (PAST + NT) // CMP == NCS
NCA = NCP + NB * NCS
SLOT = 256
NSLOT = 4
GROUP = 1024
NGROUP = DFF // GROUP
BASE = 8
NPG = NB * (PAST // PAGE)
LEVELS = [16, 32, 64]
SCALE = HD ** -0.5
FRONT = 20
SMALLW = 2 * NH + 3 * NH

CONSTS = {}


def _consts():
    k = np.arange(P)[:, None]
    i = np.arange(P)[None, :]
    t = {}
    t["ident"] = (k == i)
    t["ones"] = np.ones((P, P))
    t["headones"] = (k // HD == i // HD)
    for name, c in (("p", CHUNK), ("s", NT)):
        same = k // c == i // c
        t["cum" + name] = same & (k <= i)
        t["seg" + name] = same
        t["neg" + name] = np.where(same & (k <= i), 0.0, NEG)
    t["upper"] = (k // BASE == i // BASE) & (k < i)
    t["lower"] = (k // BASE == i // BASE) & (k > i)
    b = BASE
    while b < CHUNK:
        t["low" + str(2 * b)] = (k // (2 * b) == i // (2 * b)) & (k // b != i // b) & (k > i)
        b *= 2
    t["causal"] = np.where(i <= k, 0.0, NEG)
    end = (np.arange(NCP) + 1) * CMP - 1
    t["cmpneg"] = np.concatenate([np.where(end[None, :] <= k + P * q, 0.0, NEG) for q in range(TT)], 1)
    new = np.arange(NT)[None, :]
    t["newneg"] = np.where(new <= k % NT, 0.0, NEG)
    d, e = k % HD, i % HD
    t["rot"] = (k // HD == i // HD) * ((d == e + HD // 2) * -1.0 + (d == e - HD // 2) * 1.0)
    inv = np.float32(THETA) ** (-np.arange(HD // 2, dtype=np.float32) / np.float32(HD // 2))
    pos = np.concatenate([np.arange(SEQ), np.tile(PAST + np.arange(NT), NB)]).astype(np.float32)
    cpos = np.concatenate([end, np.tile(end[:NCS], NB)]).astype(np.float32)
    freq = inv[np.arange(P) % (HD // 2)].astype(np.float32)
    for name, x in (("", pos), ("c", cpos)):
        ang = (x[None, :] * freq[:, None]).astype(np.float32)
        t["cos" + name] = np.cos(ang)
        t["sin" + name] = np.sin(ang)
    row_b, row_h, row_t = np.arange(P) // 32, np.arange(P) % 32 // NT, np.arange(P) % NT
    for g in range(2):
        t["pick" + str(g)] = (k == ((4 * g + row_b) * NT + row_t)[None, :])
    t["rowhead"] = (row_h[:, None] == np.arange(NH)[None, :])
    of_row = (k // NCP) % KVH * GQA + k // NCP // KVH
    t["cmphead"] = (of_row == np.arange(NH)[None, :])
    t["seqof"] = (k // NT == np.arange(NB)[None, :])
    at, cols = 0, []
    for name, v in t.items():
        v = np.asarray(v, dtype=np.float32)
        CONSTS[name] = (at, v.shape[1])
        at += v.shape[1]
        cols.append(v)
    return np.ascontiguousarray(np.concatenate(cols, 1))


CONST_TABLE = _consts()
NCONST = CONST_TABLE.shape[1]


class Signal:

    def __init__(self, sem):
        self.sem, self.n = sem, 0

    def on(self, instruction):
        instruction.then_inc(self.sem, 1)
        self.n += 1
        return self.n


def build(nc, A, O):
    ctx = ExitStack()
    with ctx:
        def sb(name, shape, dt=F32, into=ctx):
            return into.enter_context(nc.sbuf_tensor(name, shape, dt))

        def sb2(name, shape, into=ctx):
            with ExitStack() as first:
                plain = sb(name, shape, F32, first)
            return plain, sb(name + "_r", shape, F32R, into)

        def F(ap):
            return ap.bitcast(F32)

        signals = {}

        def S(name):
            if name not in signals:
                signals[name] = Signal(ctx.enter_context(nc.semaphore(name)))
            return signals[name]

        setup = ctx.enter_context(nc.semaphore("setup_loaded"))
        ps = ctx.enter_context(nc.psum_tensor("ps", [P, 8, 512], F32))

        xT = sb("xT_sb", [P, KT, TOK])
        hT, hT_r = sb2("hT", [P, KT, TOK])
        mixT, mixT_r = sb2("mixT", [P, KT, TOK])
        wring, wring_r = sb2("wring", [P, NSLOT, KT * SLOT])
        cst = sb("cst", [P, NCONST])
        pages = sb("pages", [1, NPG], I32)
        gmix = sb("gmix", [P, KT])
        gmlp = sb("gmlp", [P, KT])
        gfin = sb("gfin", [P, KT])
        ggdn = sb("ggdn", [P, 1])
        convw = sb("convw", [P, 12, CONV])
        dtb = sb("dtb", [P, NH])
        alog = sb("alog", [P, NH])
        tok_small = sb("tok_small", [P, TT + 1, SMALLW])
        sig = sb("sig", [P, TT + 1, 4 * NH])
        rs = sb("rs", [P, TOK])
        Eg = mixT[:, 4:8, :]
        osq = mixT[:, 4:8, :]

        def C(name, rows=P, cols=None):
            at, n = CONSTS[name]
            return cst[0:rows, at:at + (cols or n)]

        def bc(ap, n):
            return ap.unsqueeze(2).to_broadcast([ap.shape[0], ap.shape[1], n])

        def mid(ap, n):
            return ap.unsqueeze(1).to_broadcast([ap.shape[0], n, ap.shape[1]])

        with ExitStack() as gdn_ctx:
            h_hi = sb("h_hi", [P, KT, TOK], F32R, gdn_ctx)
            qkv = sb("qkv", [P, 12, TOK], into=gdn_ctx)
            zT = sb("zT", [P, 4, TOK], into=gdn_ctx)
            xs = sb("xs", [P, 12, NB, CONV - 1 + NT], into=gdn_ctx)
            ctail = sb("ctail", [P, 12, 3 + NB * 3], into=gdn_ctx)
            St = sb("St", [P, 4, HD], into=gdn_ctx)
            Stmp = sb("Stmp", [P, 4, HD], into=gdn_ctx)
            gtok = sb("gtok", [P, TT + 1, NH], into=gdn_ctx)
            gt2 = sb("gt2", [P, TT + 1, NH], into=gdn_ctx)
            gt3 = sb("gt3", [P, TT + 1, NH], into=gdn_ctx)
            gcum = sb("gcum", [P, TT + 1, NH], into=gdn_ctx)
            egc = sb("egc", [P, TT + 1, NH], into=gdn_ctx)
            edec = sb("edec", [P, TT + 1, NH], into=gdn_ctx)
            qkm = sb("qkm", [P, NH, P], into=gdn_ctx)
            kdec = sb("kdec", [P, NH, HD], into=gdn_ctx)
            kb = sb("kb", [P, NH, HD], into=gdn_ctx)
            vtok = sb("vtok", [P, NH, HD], into=gdn_ctx)
            u0 = sb("u0", [P, NH, HD], into=gdn_ctx)
            wqT = sb("wqT", [P, 2, 4, P], into=gdn_ctx)
            u = sb("u", [P, NH, HD], into=gdn_ctx)
            with ExitStack() as prep_ctx:
                names = ["a", "b", "c", "d", "e", "f", "m"]
                prep = {n: sb("prep_" + n, [P, 2, 4, P], into=prep_ctx) for n in names}
            with ExitStack() as conv_ctx:
                pre = sb("pre", [P, 3, TOK], into=conv_ctx)
                sq = sb("sq", [P, 4, TOK], into=conv_ctx)
                cmul = sb("cmul", [P, 12, NS], into=conv_ctx)
                r_a = sb("r_a", [P, 4, TOK], into=conv_ctx)
            with ExitStack() as sample_ctx:
                Ss = sb("Ss", [P, NB, 4, HD], into=sample_ctx)
                um = sb("um", [NS, NH, NB, HD], into=sample_ctx)
                xuT = sb("xuT", [P, 4, 2, NS], into=sample_ctx)
                sadd = sb("sadd", [P, 2, NB, HD], into=sample_ctx)
        with ExitStack() as nsa_ctx:
            past_keys = sb("past_keys", [P, KT * TOK], into=nsa_ctx)
            kselT, kwinT = (past_keys[:, NB * (PAST + NT) * i:NB * (PAST + NT) * (i + 1)].rearrange(
                "p (b t) -> p b t", b=NB) for i in range(2))
            nsaT = sb("nsaT", [P, 10, TOK], into=nsa_ctx)
            rows = sb("rows", [P, 2, 2, NB, 2, P], into=nsa_ctx)
            krows = rows[:, 0].rearrange("p s b g e -> p (s b g e)")
            kz = krows[:, 0:4 * SEQ].rearrange("p (s g n) -> p s g n", s=2, g=KVH)
            pc = krows[:, 4 * SEQ:5 * SEQ].rearrange("p (q h n) -> p q h n", q=TT, h=NH)
            pcT = krows[:, 5 * SEQ:6 * SEQ].rearrange("p (q n) -> p q n", q=TT)
            cvb = krows[:, 6 * SEQ:7 * SEQ].rearrange("p (h d) -> p h d", h=NH)
            cvrep = krows[:, 7 * SEQ:7 * SEQ + P]
            ckz = krows[:, 7 * SEQ + P:7 * SEQ + P + KVH * NCP].rearrange("p (g n) -> p g n", g=KVH)
            cstat = krows[:, 7 * SEQ + 2 * P:7 * SEQ + 2 * P + TT * NH]
            values, values_r = sb2("values", [P, 2 * (TT + NB) * P], nsa_ctx)
            vtp = values[:, 0:2 * TT * P].rearrange("p (s q e) -> p s q e", s=2, q=TT)
            vnew = values[0:NT, 2 * TT * P:].rearrange("p (s b e) -> p s b e", s=2, b=NB)
            ckT = sb("ckT", [P, 2, NCA + 1], into=nsa_ctx)
            ckr = sb("ckr", [P, NCA], into=nsa_ctx)
            cvs = sb("cvs", [NCS, NB, P], into=nsa_ctx)
            pe = sb("pe", [P, 2, CMP], into=nsa_ctx)
            qs = sb("qs", [P, NB, KVH, GQA, NT], into=nsa_ctx)
            stat = sb("stat", [P, 96], into=nsa_ctx)
            att = sb("att", [P, 2, 2, 512], into=nsa_ctx)
            h_flat = hT[:, :, :].rearrange("p a b -> p (a b)")
            attT = h_flat[:, 0:1024].rearrange("p (s n) -> p s n", s=2)
            osum = h_flat[:, 1024:2048].rearrange("p (a j g d) -> p a j g d", a=2, j=GQA, g=KVH)
            scaled = h_flat[:, 2048:2048 + 6 * HD].rearrange("p (a s d) -> p a s d", a=2, s=3)
        with ExitStack() as mlp_ctx:
            mix_hi = sb("mix_hi", [P, KT, TOK], F32R, mlp_ctx)
            uT, uT_r = sb2("uT", [P, 8, TOK], mlp_ctx)
            u_hi = sb("u_hi", [P, 8, TOK], F32R, mlp_ctx)
            w_hi_mlp = sb("w_hi_mlp", [P, 4, KT * P], F32R, mlp_ctx)
        cmp_rows = att[:, :, :, :].rearrange("p a b c -> p (a b c)").rearrange(
            "p (b g s e) -> p b g s e", b=4, g=2, s=2)
        cmpT = hT[:, :, :].rearrange("p a b -> p (a b)")[:, 0:2 * NB * PAST].rearrange(
            "p (s b t) -> p s b t", s=2, b=NB)

        def whole(pair, rows=P):
            return ps[0:rows, 2 * pair:2 * pair + 2, 0:HALF]

        def halves(ap):
            return ap.rearrange("p (a b) -> p a b", a=2)

        def heads4(ap, n):
            return ap.rearrange("p (h i) -> p h i", h=4)[:, :, 0:n]

        def tile_len(q):
            return P if q < TT else NS

        def cols(q):
            return slice(P * q, P * q + tile_len(q))

        def par(h):
            return slice(HD * (h % 2), HD * (h % 2) + HD)

        def high_slots(flat, n):
            return [flat[:, KT * P * i:KT * P * (i + 1)].rearrange("p (k n) -> p k n", k=KT) for i in range(n)]

        w_hi_gdn = high_slots(mixT_r[:, :, :].rearrange("p k n -> p (k n)"), 4)
        w_hi_nsa = high_slots(values_r, 3)
        w_hi_mlp = high_slots(w_hi_mlp[:, :, :].rearrange("p a b -> p (a b)"), 4)

        def wslot(c, ring=wring):
            return ring[:, c % NSLOT, :].rearrange("p (k n) -> p k n", k=KT)

        def front_chunks(l):
            w_in = A["w_in"][l].rearrange("(k p) n -> p k n", p=P)
            w_out = A["w_out"][l]
            out = {}
            for c in range(6):
                out[c] = [(wslot(c), w_in[:, :, SLOT * c:SLOT * (c + 1)])]
            for c in range(2):
                out[6 + c] = [(wslot(6 + c), w_in[:, :, O_Z + SLOT * c:O_Z + SLOT * (c + 1)])]
            out[8] = [(wslot(8)[:, :, 0:2 * NH], w_in[:, :, O_AB:O_AB + 2 * NH]),
                      (wslot(8)[:, :, 2 * NH:SMALLW], w_in[:, :, O_GATE:O_GATE + 3 * NH])]
            for c in range(2):
                out[9 + c] = [(wslot(9 + c)[:, :, P * j + HD * g:P * j + HD * (g + 1)],
                               w_in[:, :, O_Q + HD * (GQA * g + 2 * c + j):O_Q + HD * (GQA * g + 2 * c + j + 1)])
                              for j in range(2) for g in range(KVH)]
            for c in range(3):
                out[11 + c] = [(wslot(11 + c), w_in[:, :, O_KV + SLOT * c:O_KV + SLOT * (c + 1)])]
            for c, name in enumerate(("cmp_w_k", "cmp_w_v")):
                dst = wring[:, (14 + c) % NSLOT, :].rearrange("p (c e) -> p c e", c=CMP)
                src = A[name][l].rearrange("c d e -> d c e")
                out[14 + c] = [(dst[HD * g:HD * (g + 1)], src) for g in range(KVH)]
            for c in range(4):
                n0, n1 = SLOT * c, SLOT * (c + 1)
                gdn = w_out[0:NH * HD, n0:n1].rearrange("(k p) n -> p k n", p=P)
                out[16 + c] = [(wslot(16 + c)[:, 0:4, :], gdn)]
                for g in range(KVH):
                    rows = w_out[(NH + GQA * g) * HD:(NH + GQA * (g + 1)) * HD, n0:n1]
                    out[16 + c].append((wslot(16 + c)[HD * g:HD * (g + 1), 4:8, :],
                                        rows.rearrange("(j d) n -> d j n", d=HD)))
            return out

        parts = {c: len(v) for c, v in front_chunks(0).items()}
        ld = [S(f"weights_in_slot{s}") for s in range(NSLOT)]

        def landed(c):
            return 16 * sum(parts[x] for x in range(c % NSLOT, c + 1, NSLOT))

        front_total = [landed(FRONT - NSLOT + s) for s in range(NSLOT)]

        def used(c):
            if c <= 8:
                return S("proj").sem, min(2 * (c + 1), 17)
            if c <= 13:
                return S("proj").sem, 17 + 2 * (c - 8)
            if c <= 15:
                return S("cmp").sem, c - 13
            return S("res").sem, 2 * (c - 15)

        tiles = [(c, P * j, P) for c in range(8) for j in range(2)] + [(8, 0, SMALLW)]
        tiles += [(c, P * j, P) for c in range(9, 14) for j in range(2)]
        N_GDN = 17
        N_TILES = len(tiles)
        tiles += [(16 + d // 2, P * (d % 2), P) for d in range(KT)]
        N_FRONT = len(tiles)

        def high(n):
            if n < N_GDN:
                slots, first = w_hi_gdn, 0
            elif n < N_TILES:
                slots, first = w_hi_nsa, N_GDN
            else:
                slots, first = w_hi_mlp, N_TILES
            at = (n - first) % len(slots)
            return slots[at], (n - len(slots) if n - first >= len(slots) else None)

        def tile_used(n):
            return (S("proj").sem, n + 1) if n < N_TILES else (S("res").sem, n - N_TILES + 1)

        def split_high(act, n):
            c, col, M = tiles[n]
            slot, before = high(n)
            act.wait_ge(ld[c % NSLOT].sem, landed(c))
            if before is not None:
                act.wait_ge(*tile_used(before))
            S("w_high").on(nc.scalar.activation(slot[:, :, 0:M], wslot(c)[:, :, col:col + M], ACT.Copy))

        def split_low(v, n):
            c, col, M = tiles[n]
            v.wait_ge(S("w_high").sem, n + 1)
            S("w_low").on(v.tensor_tensor(wslot(c, wring_r)[:, :, col:col + M], wslot(c)[:, :, col:col + M],
                                          F(high(n)[0][:, :, 0:M]), ALU.subtract))
        ROPED = (0, 1, 2, 3, 6, 8)
        UNITS = TT * NH
        SCHEDULE = [("s", 0), ("s", 1)]
        for uu in range(UNITS):
            SCHEDULE.append(("t", uu))
            if uu + 2 < UNITS:
                SCHEDULE.append(("s", uu + 2))
            SCHEDULE.append(("v", uu))
            if uu >= NH and uu % NH == 0:
                SCHEDULE.append(("o", uu // NH - 1))
        SCHEDULE.append(("o", TT - 1))

        def mlp_split_high(act, m, i):
            c, col = i // 2, P * (i % 2)
            act.wait_ge(ld[c % NSLOT].sem, m * 32 + (front_total[c % NSLOT] + 16 * (c // 4 + 1)))
            if i < 4:
                act.wait_ge(S("res").sem, m * 8 + (5 + i))
            elif i < 12:
                act.wait_ge(S("up").sem, m * 8 + (i - 3))
            else:
                act.wait_ge(S("res").sem, m * 8 + (8 + i - 11))
            nc.scalar.activation(w_hi_mlp[i % 4], wslot(c)[:, :, col:col + P], ACT.Copy).then_inc(
                S("w_high").sem, 1)

        def mlp_split_low(v, m, i):
            col = P * (i % 2)
            v.wait_ge(S("w_high").sem, m * 16 + (N_FRONT + i + 1))
            v.tensor_tensor(wslot(i // 2, wring_r)[:, :, col:col + P], wslot(i // 2)[:, :, col:col + P],
                            F(w_hi_mlp[i % 4]), ALU.subtract).then_inc(S("w_low").sem, 1)

        AHEAD = 2

        def mlp_split_ahead(split, engine, m, i, last):
            if i + AHEAD < 16:
                split(engine, m, i + AHEAD)
            elif not last:
                split(engine, m + 1, i + AHEAD - 16)

        with nc.Block() as block:
            @block.sync
            def _(sp):
                sp.dma_start(cst[:], A["consts"]).then_inc(setup, 16)
                sp.dma_start(xT[:], A["xT"]).then_inc(setup, 16)
                sp.dma_start(pages[:], A["page_table"]).then_inc(setup, 16)
                sp.dma_start(gfin[:], A["norm_final"]).then_inc(setup, 16)
                sp.wait_ge(setup, 64)

        def norm_tensor(t, use, sq_of):
            for k in range(KT):
                t.wait_ge(S("norm_square").sem, use * KT + k + 1)
                for h in range(2):
                    x = t.matmul(ps[:, h, 0:HALF], C("ones"), sq_of(k)[:, HALF * h:HALF * (h + 1)],
                                 start=(k == 0), stop=(k == KT - 1), skip_group_check=True)
                S("norm_sum").on(x)

        def norm_scalar(act, use, sq_of, ring, between=()):
            for k in range(KT):
                if k >= ring:
                    act.wait_ge(S("norm_sum").sem, use * KT + k - ring + 1)
                S("norm_square").on(nc.scalar.activation(sq_of(k), xT[:, k, :], ACT.Square))
            for split in between:
                split(act)
            act.wait_ge(S("norm_mean").sem, use + 1)
            S("norm_root").on(nc.scalar.activation(rs[:], rs[:], ACT.Sqrt))

        def norm_vector(v, use, g, out, high=None, between=()):
            v.wait_ge(S("norm_sum").sem, (use + 1) * KT)
            S("norm_mean").on(v.tensor_scalar(halves(rs[:]), whole(0), 1.0 / D, EPS, ALU.mult, ALU.add))
            for split in between:
                split(v)
            v.wait_ge(S("norm_root").sem, use + 1)
            S("v_step").on(v.reciprocal(rs[:], rs[:]))
            v.wait_ge(S("v_step").sem, S("v_step").n)

            def low(k):
                v.wait_ge(S("h_high").sem, use * KT + k + 1)
                S("h_ready").on(v.tensor_tensor(hT_r[:, k, :], out[:, k, :], F(high[:, k, :]), ALU.subtract))

            for k in range(KT):
                x = v.scalar_tensor_tensor(out[:, k, :], xT[:, k, :], g[:, k:k + 1], rs[:], ALU.mult, ALU.mult)
                S("h_full").on(x)
                if high is not None and k:
                    low(k - 1)
            if high is not None:
                low(KT - 1)

        def norm_high(act, use, high):
            for k in range(KT):
                act.wait_ge(S("h_full").sem, use * KT + k + 1)
                S("h_high").on(nc.scalar.activation(high[:, k, :], hT[:, k, :], ACT.Copy))

        with nc.Fori(0, DEPTH) as l:
            with nc.Block() as block:

                @block.sync
                def _(sp):
                    for dst, name in ((gmix, "norm_mix"), (gmlp, "norm_mlp"), (ggdn, "gdn_norm"), (convw, "conv_w")):
                        sp.dma_start(dst[:], A[name][l]).then_inc(S("params").sem, 16)
                    for dst, name in ((dtb, "dt_bias"), (alog, "a_log")):
                        sp.dma_start(dst[:], A[name][l].partition_broadcast(P)).then_inc(S("params").sem, 16)
                    chunks = front_chunks(l)

                    def load(c):
                        if c >= NSLOT:
                            sp.wait_ge(*used(c - NSLOT))
                        for dst, src in chunks[c]:
                            sp.dma_start(dst, src).then_inc(ld[c % NSLOT].sem, 16)

                    load(0)
                    sp.dma_start(xs[:, :, :, 0:3], A["state_conv"][l]).then_inc(S("conv_state_in").sem, 16)
                    for c in range(1, NSLOT):
                        load(c)
                    sp.dma_start(O["win_past"][l], A["state_win"][l][:, NT:PAST]).then_inc(S("window_kept").sem, 16)
                    for c in range(NSLOT, 13):
                        load(c)
                    sp.wait_ge(S("u0_out").sem, 2 * (TT + 1))
                    sp.wait_ge(S("wT_out").sem, 2 * (TT + 1))
                    sp.dma_start(Ss[:], A["state_gdn"][l]).then_inc(S("states_in").sem, 16)
                    sp.wait_ge(S("tail_out").sem, 13)
                    sp.dma_start(O["conv_T"][l], ctail[:]).then_inc(S("gdn_stored").sem, 16)
                    sp.wait_ge(S("state").sem, 2 * TT + 1)
                    sp.dma_start(O["gdn_p"][l], St[:]).then_inc(S("gdn_stored").sem, 16)
                    sp.wait_ge(S("sdS_out").sem, 4)
                    sp.dma_start(O["gdn_s"][l], Ss[:]).then_inc(S("gdn_stored").sem, 16)
                    sp.wait_ge(S("gdn_stored").sem, 48)
                    sp.wait_ge(S("gdn_mixed").sem, 4)
                    load(13)
                    for s, name in enumerate(("cmp_pe_k", "cmp_pe_v")):
                        for g in range(KVH):
                            sp.dma_start(pe[HD * g:HD * (g + 1), s, :], A[name][l]).then_inc(S("pe_in").sem, 16)
                    win = A["state_win"][l].rearrange("b (g p) s h d -> p b g (s h d)", p=P)
                    for b in range(NB):
                        for kv in range(2):
                            sp.dma_start(rows[:, kv, 1, b], win[:, b][:, :, P * kv:P * (kv + 1)]).then_inc(
                                S("window_in").sem, 16)
                    for b in range(NB):
                        if b == 4:
                            sp.wait_ge(S("kpast_turned").sem, 2 * 4)
                        for pg in range(2):
                            i = 2 * b + pg
                            phys = sp.value_load(pages[0:1, i:i + 1], min_val=0, max_val=N_POOL - 1)
                            page = A["cache_kv"][l, bass.ds(phys, 1)]
                            for g in range(KVH):
                                src = page[0, g]
                                cc = slice(HD * g, HD * (g + 1))
                                sp.dma_start(rows[:, :, 0, b, pg, cc], src[:, 2:4, :]).then_inc(S("pages_in").sem, 16)
                                sp.dma_start(cmp_rows[:, b % 4, pg, :, cc], src[:, 0:2, :]).then_inc(S("pages_in").sem, 16)
                    for c in range(14, FRONT):
                        load(c)
                    sp.wait_ge(S("rope_done").sem, len(ROPED))
                    sp.dma_start(O["rows_T"][l], nsaT[:, 4:10, :]).then_inc(S("rows_stored").sem, 16)
                    with sp.Fori(0, NGROUP) as m:
                        up = A["w_up"][l].rearrange("(k p) n -> p k n", p=P)
                        down = A["w_down"][l].rearrange("(m k p) n -> m p k n", p=P, k=8)[m]
                        for c in range(8):
                            if c < 4:
                                sp.wait_ge(S("res").sem, m * 8 + 2 * (c + 1))
                                src = up[:, :, bass.ds(m * GROUP + c * SLOT, SLOT)]
                            else:
                                sp.wait_ge(S("up").sem, m * 8 + 2 * (c - 3))
                                src = down[:, :, (c - 4) * SLOT:(c - 3) * SLOT]
                            sp.dma_start(wslot(c), src).then_inc(ld[c % NSLOT].sem, 16)
                    sp.wait_ge(S("window_kept").sem, 16)
                    sp.wait_ge(S("rows_stored").sem, 16)

                @block.tensor
                def _(t):
                    def mm(out, lhsT, rhs, start=True, stop=True):
                        return t.matmul(out, lhsT, rhs, start=start, stop=stop, skip_group_check=True)

                    def dense(pair, w_high, w_low, x_high, x_low, M=P, ready=None):
                        for k in range(KT):
                            if ready:
                                t.wait_ge(*ready(k))
                            for i, (w, src) in enumerate(((w_high, x_high), (w_high, x_low), (w_low, x_high))):
                                for h in range(2):
                                    x = mm(ps[0:M, 2 * pair + h, 0:HALF], w[:, k, :],
                                           src[:, k, HALF * h:HALF * (h + 1)],
                                           start=(k == 0 and i == 0), stop=(k == KT - 1 and i == 2))
                        return x

                    norm_tensor(t, 0, lambda k: sq[:, k % 4, :])

                    def project(n):
                        c, col, M = tiles[n]
                        t.wait_ge(S("w_low").sem, n + 1)
                        if n >= 4:
                            t.wait_ge(S("proj_out").sem, n - 3)
                        S("proj").on(dense(n % 4, high(n)[0][:, :, 0:M], wslot(c, wring_r)[:, :, col:col + M], h_hi, hT_r, M,
                                           ready=(lambda k: (S("h_ready").sem, k + 1)) if n == 0 else None))

                    for n in range(N_GDN):
                        project(n)

                    for n in range(8):
                        t.wait_ge(S("l2_square").sem, n + 1)
                        t.wait_ge(S("proj_out").sem, N_GDN)
                        if n >= 4:
                            t.wait_ge(S("l2_out").sem, n - 3)
                        for h in range(2):
                            x = mm(ps[:, 2 * (n % 4) + h, 0:HALF], C("headones"),
                                   sq[:, n % 4, HALF * h:HALF * (h + 1)])
                        S("l2_sum").on(x)

                    t.wait_ge(S("l2_out").sem, 8)
                    for q in range(TT + 1):
                        n = tile_len(q)
                        x = t.transpose(ps[0:n, 0, SMALLW * q:SMALLW * (q + 1)],
                                        rs[0:SMALLW, P * q:P * q + n], C("ident", SMALLW, SMALLW))
                    S("decay_tensor").on(x)

                    t.wait_ge(S("decay_vector").sem, 2)
                    for j, m in enumerate(("cum", "seg")):
                        mm(ps[:, 1, 64 * j:64 * j + TT * NH], C(m + "p"),
                           gtok[:, 0:TT, :].rearrange("p a b -> p (a b)"))
                        x = mm(ps[0:NS, 1, 64 * j + TT * NH:64 * j + (TT + 1) * NH], C(m + "s", NS, NS),
                               gtok[0:NS, TT, :])
                    S("decay_tensor").on(x)
                    for q in range(TT + 1):
                        n = tile_len(q)
                        for h in range(NH):
                            x = mm(ps[par(h), 2 + q, P * (h // 2):P * (h // 2) + n],
                                   gtok[0:n, q, h:h + 1].to_broadcast([n, HD]),
                                   C("cump" if q < TT else "cums", n, n))
                        S("gchan_sum").on(x)

                    def prepare(q):
                        n = tile_len(q)
                        if q == 0:
                            t.wait_ge(S("Eg_out").sem, TT + 1)
                            t.wait_ge(S("gates_act").sem, 7)
                            t.wait_ge(S("l2_done").sem, 8)
                        else:
                            t.wait_ge(S("state").sem, 2 * q + 1)
                            t.wait_ge(S("oT_out").sem, 2 * q)
                        for s in range(2):
                            for hp in range(4):
                                x = t.transpose(ps[0:n, s, P * hp:P * (hp + 1)], qkv[:, 4 + 4 * s + hp, cols(q)],
                                                C("ident"))
                        S("kv_turned").on(x)
                        for hf in range(2):
                            b0 = 2 + 3 * hf
                            for h in range(4):
                                hh = 4 * hf + h
                                for s in range(2):
                                    at = 2 * P * s + P * (h // 2)
                                    x = mm(ps[0:n, b0 + h % 2, at:at + n], qkv[par(hh), 4 + hh // 2, cols(q)],
                                           qkv[par(hh), 4 - 4 * s + hh // 2, cols(q)])
                            S("gram").on(x)
                            t.wait_ge(S("gU_ready").sem, 2 * q + hf + 1)
                            S("grow").on(mm(heads4(ps[0:n, b0 + 2, :], n), C("ones", n, n),
                                            prep["d"][0:n, hf, :, 0:n]))

                        def each(bank, lhsT, rhs, hf):
                            for h in range(4):
                                x = mm(ps[0:n, bank, P * h:P * h + n], prep[lhsT][0:n, hf, h, 0:n],
                                       prep[rhs][0:n, hf, h, 0:n])
                            return x

                        def turn(bank, name, hf):
                            for h in range(4):
                                x = t.transpose(ps[0:n, bank, P * h:P * h + n], prep[name][0:n, hf, h, 0:n],
                                                C("ident", n, n))
                            return x

                        for hf in range(2):
                            t.wait_ge(S("B_ready").sem, 2 * q + hf + 1)
                            S("A_turned").on(turn(2 + 3 * hf, "b", hf))
                        for hf in range(2):
                            t.wait_ge(S("D_ready").sem, 2 * q + hf + 1)
                            t.wait_ge(S("AD_ready").sem, 2 * q + hf + 1)
                            S("D2").on(each(3 + 3 * hf, "c", "d", hf))
                        for hf in range(2):
                            t.wait_ge(S("D2_out").sem, 2 * q + hf + 1)
                            S("D2T").on(turn(2 + 3 * hf, "f", hf))
                        for hf in range(2):
                            t.wait_ge(S("ID2T_out").sem, 2 * q + hf + 1)
                            S("P1").on(each(3 + 3 * hf, "c", "e", hf))
                            if q < TT:
                                S("D4").on(each(4 + 3 * hf, "b", "f", hf))
                        if q < TT:
                            for hf in range(2):
                                t.wait_ge(S("ID4_out").sem, 2 * q + hf + 1)
                                S("ID4T").on(turn(2 + 3 * hf, "f", hf))
                            for hf in range(2):
                                t.wait_ge(S("ID4T_out").sem, 2 * q + hf + 1)
                                t.wait_ge(S("P1_out").sem, 2 * q + hf + 1)
                                S("Pn").on(each(3 + 3 * hf, "b", "d", hf))
                            for i, lev in enumerate(LEVELS):
                                cur = "ed"[i % 2]
                                for hf in range(2):
                                    t.wait_ge(S("Pn_out").sem, 2 * (4 * q + i) + hf + 1)
                                    t.wait_ge(S("M_ready").sem, 2 * (3 * q + i) + hf + 1)
                                    S("X").on(each(2 + 3 * hf, "m", cur, hf))
                                    S("PT").on(turn(4 + 3 * hf, cur, hf))
                                for hf in range(2):
                                    t.wait_ge(S("IX_out").sem, 2 * (3 * q + i) + hf + 1)
                                    t.wait_ge(S("PT_out").sem, 2 * (3 * q + i) + hf + 1)
                                    S("Pn").on(each(3 + 3 * hf, "b", "f", hf))
                        t.wait_ge(S("kb_out").sem, 2 * q + 2)
                        t.wait_ge(S("v_out").sem, q + 1)
                        for hf in range(2):
                            if q < TT:
                                t.wait_ge(S("Pn_out").sem, 2 * (4 * q + 3) + hf + 1)
                            else:
                                t.wait_ge(S("P1_out").sem, 2 * q + hf + 1)
                            for h in range(4):
                                hh = 4 * hf + h
                                mm(ps[0:n, 2 + 3 * hf, HD * h:HD * (h + 1)], prep["d"][0:n, hf, h, 0:n],
                                   vtok[0:n, hh, :])
                                x = mm(ps[par(hh), 4 + 3 * hf, P * (h // 2):P * (h // 2) + n],
                                       kb[0:n, hh, :], prep["d"][0:n, hf, h, 0:n])
                            S("wu").on(x)

                    def scan(q):
                        for half in range(2):
                            n = 2 * q + half
                            rows = slice(HD * half, HD * half + HD)
                            t.wait_ge(S("u0_out").sem, 2 * (q + 1))
                            t.wait_ge(S("wT_out").sem, 2 * (q + 1))
                            t.wait_ge(S("state").sem, n + 1)
                            t.wait_ge(S("qe_out").sem, q + 1)
                            for h in range(NH):
                                x = mm(ps[rows, h % 2, HD * (h // 2):HD * (h // 2 + 1)], wqT[par(h), 0, h // 2, rows],
                                       St[par(h), h // 2, :])
                            S("wS").on(x)
                            if n:
                                t.wait_ge(S("oT_out").sem, n)
                            for h in range(NH):
                                x = mm(ps[par(h), 2, HD * (h // 2):HD * (h // 2 + 1)], St[par(h), h // 2, :],
                                       qkv[par(h), h // 2, P * q + HD * half:P * q + HD * (half + 1)])
                            S("oS").on(x)
                            t.wait_ge(S("u_out").sem, n + 1)
                            for h in range(NH):
                                x = mm(ps[par(h), 4, HD * (h // 2):HD * (h // 2 + 1)], kdec[rows, h, :], u[rows, h, :])
                            S("dS").on(x)
                            for h in range(NH):
                                x = mm(ps[par(h), 3, HD * (h // 2):HD * (h // 2 + 1)], u[rows, h, :], qkm[rows, h, rows])
                            S("oU").on(x)

                    for q in range(TT):
                        prepare(q)
                        scan(q)
                    prepare(TT)

                    t.wait_ge(S("u0_out").sem, 2 * (TT + 1))
                    t.wait_ge(S("wT_out").sem, 2 * (TT + 1))
                    t.wait_ge(S("qe_out").sem, TT + 1)
                    t.wait_ge(S("states_in").sem, 16)
                    for b in range(NB):
                        for h in range(NH):
                            out = ps[par(h), 0, 64 * (h // 2):64 * (h // 2 + 1)].rearrange("p (s i) -> p s i", s=2)
                            x = mm(out[:, :, NT * b:NT * (b + 1)], Ss[par(h), b, h // 2, :],
                                   wqT[par(h), :, h // 2, NT * b:NT * (b + 1)])
                    S("sample_mm").on(x)
                    t.wait_ge(S("sample_dve").sem, 1)
                    for hp in range(4):
                        x = t.transpose(ps[0:NS, 1, P * hp:P * (hp + 1)], xuT[:, hp, 0, :], C("ident"))
                    S("sample_mm").on(x)
                    t.wait_ge(S("sample_dve").sem, 2)
                    for h in range(NH):
                        x = mm(ps[par(h), 2, NS * (h // 2):NS * (h // 2 + 1)], u[0:NS, h, :], qkm[0:NS, h, 0:NS])
                    S("sample_mm").on(x)
                    for hp in range(4):
                        for h in (2 * hp, 2 * hp + 1):
                            t.wait_ge(S("um_out").sem, h + 1)
                            x = mm(ps[par(h), 3 + hp, :], kdec[0:NS, h, :], um[:, h, :, :].rearrange("p b e -> p (b e)"))
                        S("sdS").on(x)

                    t.wait_ge(S("sdS_out").sem, 4)
                    for hp in range(4):
                        t.wait_ge(S("o_square").sem, hp + 1)
                        for h in range(2):
                            x = mm(ps[:, 2 * hp + h, 0:HALF], C("headones"), osq[:, hp, HALF * h:HALF * (h + 1)])
                        S("o_sum").on(x)

                    t.wait_ge(S("gdn_mixed").sem, 4)
                    for n in range(N_GDN, N_TILES):
                        project(n)
                    t.wait_ge(S("proj_out").sem, N_TILES)
                    for i, n in enumerate(ROPED):
                        if i >= 4:
                            t.wait_ge(S("rope_sin").sem, i - 3)
                        for h in range(2):
                            x = mm(ps[:, 2 * (i % 4) + h, 0:HALF], C("rot"), nsaT[:, n, HALF * h:HALF * (h + 1)])
                        S("rot").on(x)
                    t.wait_ge(S("rope_sin").sem, len(ROPED))
                    for s in range(2):
                        for q in range(TT):
                            x = t.transpose(ps[:, s, P * q:P * (q + 1)], nsaT[:, 7 + 2 * s, P * q:P * (q + 1)],
                                            C("ident"))
                        S("v_turned").on(x)
                    for s in range(2):
                        for b in range(NB):
                            x = t.transpose(ps[0:NT, 2 + 2 * s + b // 4, P * (b % 4):P * (b % 4 + 1)],
                                            nsaT[:, 7 + 2 * s, SEQ + NT * b:SEQ + NT * (b + 1)], C("ident"))
                        S("v_turned").on(x)
                    t.wait_ge(S("window_in").sem, 32 * NB)
                    for i in range(2 * NB):
                        b = i // 2
                        if i % 2 == 0:
                            t.wait_ge(S("pages_in").sem, 16 * 32 if b < 4 else 16 * 64)
                        if i >= 2:
                            t.wait_ge(S("kpast_out").sem, i - 1)
                        bank = 6 + i % 2
                        if i % 2 == 0:
                            for pg in range(2):
                                t.transpose(ps[:, bank, P * pg:P * (pg + 1)], rows[:, 0, 0, b, pg, :], C("ident"))
                                x = t.transpose(ps[:, bank, P * (2 + pg):P * (3 + pg)], rows[:, 0, 1, b, pg, :], C("ident"))
                            S("kpast_turned").on(x)
                        else:
                            for s in range(2):
                                for pg in range(2):
                                    x = t.transpose(ps[:, bank, P * (2 * s + pg):P * (2 * s + pg + 1)],
                                                    cmp_rows[:, b % 4, pg, s, :], C("ident"))
                            S("kpast_turned").on(x)
                    t.wait_ge(S("kpast_out").sem, 2 * NB)
                    t.wait_ge(S("pe_in").sem, 64)
                    t.wait_ge(S("v_copied").sem, 2)
                    for s in range(2):
                        t.wait_ge(ld[(14 + s) % NSLOT].sem, landed(14 + s))
                        w = wring[:, (14 + s) % NSLOT, :].rearrange("p (c e) -> p c e", c=CMP)
                        for g in range(KVH):
                            r = slice(HD * g, HD * (g + 1))
                            for c in range(CMP):
                                mm(ps[r, s, 0:NCP], w[r, c, :],
                                   nsaT[r, 4 + s, 0:SEQ].rearrange("p (n c) -> p n c", c=CMP)[:, :, c],
                                   start=(c == 0), stop=(c == CMP - 1))
                                mm(ps[r, s, NCP:NCA], w[r, c, :],
                                   cmpT[r, s, :, :].rearrange("p b (n c) -> p (b n) c", c=CMP)[:, :, c],
                                   start=False, stop=(c == CMP - 1))
                                x = mm(ps[r, s, NCA:NCA + 1], w[r, c, :], pe[r, s, c:c + 1],
                                       start=False, stop=(c == CMP - 1))
                        S("cmp").on(x)
                    t.wait_ge(S("ck_out").sem, 2)
                    t.wait_ge(S("v_copied").sem, 4)
                    S("ck_rot").on(mm(ps[:, 2, 0:NCA], C("rot"), ckT[:, 0, 0:NCA]))
                    t.wait_ge(S("cvrep_ready").sem, 1)
                    t.transpose(ps[:, 3, 0:P], cvrep, C("ident"))
                    for b in range(NB):
                        x = t.transpose(ps[0:NCS, 4 + b // 4, P * (b % 4):P * (b % 4 + 1)],
                                        ckT[:, 1, NCP + NCS * b:NCP + NCS * (b + 1)], C("ident"))
                    S("cv_turned").on(x)

                    t.wait_ge(S("compressed_vector").sem, 1)
                    t.wait_ge(S("rope_done").sem, len(ROPED))
                    for q in range(TT):
                        for j in range(GQA):
                            at = KVH * NCP * (GQA * q + j)
                            x = mm(ps[:, 6, at:at + KVH * NCP], nsaT[:, j, P * q:P * (q + 1)],
                                   ckz.rearrange("p g n -> p (g n)"))
                    S("compressed_tensor").on(x)

                    def scores(uu):
                        q, h = divmod(uu, NH)
                        if uu == 0:
                            t.wait_ge(S("cv_out").sem, 1)
                            t.wait_ge(S("kz_ready").sem, 4)
                            t.wait_ge(S("compressed_vector").sem, 2)
                        if uu >= 2:
                            t.wait_ge(S("p_exp").sem, 2 * (uu - 1))
                        for s in range(2):
                            x = mm(ps[:, 2 * (uu % 2) + s, 0:P * (q + 1)], nsaT[:, h % GQA, P * q:P * (q + 1)],
                                   kz[:, s, h // GQA, 0:P * (q + 1)])
                        S("score").on(x)

                    def turn(uu):
                        q, h = divmod(uu, NH)
                        if h == 1 and q:
                            t.wait_ge(S("o_out").sem, q)
                        for s in range(2):
                            t.wait_ge(S("p_exp").sem, 2 * uu + s + 1)
                            if uu:
                                t.wait_ge(S(f"pT_out{s}").sem, uu)
                            for kt in range(q + 1):
                                x = t.transpose(ps[:, 4 + s, P * kt:P * (kt + 1)],
                                                att[:, uu % 2, s, P * kt:P * (kt + 1)], C("ident"))
                            S("pT").on(x)

                    def values_of(uu):
                        q, h = divmod(uu, NH)
                        g = h // GQA
                        if uu == 0:
                            t.wait_ge(S("compressed_scalar").sem, 2)
                            t.wait_ge(S("compressed_vector").sem, 2)
                        if uu >= 2:
                            t.wait_ge(S("o_scaled").sem, uu - 1)
                        out = ps[:, 6 + uu % 2, :]
                        for s in range(2):
                            t.wait_ge(S(f"pT_out{s}").sem, uu + 1)
                            for kt in range(q + 1):
                                mm(out[:, HD * s:HD * (s + 1)], attT[:, s, P * kt:P * (kt + 1)],
                                   vtp[:, s, kt, HD * g:HD * (g + 1)], start=(kt == 0), stop=(kt == q))
                        S("nsa").on(mm(out[:, 2 * HD:3 * HD], pcT[:, q, :], cvb[:, h, :]))

                    def outputs(q):
                        t.wait_ge(S("o_added").sem, NH * (q + 1))
                        t.wait_ge(S("pT_out0").sem, min(NH * (q + 1) + 1, UNITS))
                        for j in range(GQA):
                            x = t.transpose(ps[:, 4, P * j:P * (j + 1)],
                                            osum[:, q % 2, j, :, :].rearrange("p g d -> p (g d)"), C("ident"))
                        S("o_turned").on(x)

                    for what, i in SCHEDULE[:2]:
                        scores(i)
                    t.wait_ge(S("compressed_vector").sem, 4)
                    for q in range(TT):
                        x = t.transpose(ps[:, 7, P * q:P * (q + 1)], pc[:, q].rearrange("p h n -> p (h n)"), C("ident"))
                    S("compressed_tensor").on(x)
                    for what, i in SCHEDULE[2:]:
                        {"s": scores, "t": turn, "v": values_of, "o": outputs}[what](i)
                    t.wait_ge(S("o_out").sem, TT)
                    t.wait_ge(S("o_scaled").sem, UNITS)

                    t.wait_ge(S("qs_ready").sem, 3)
                    t.wait_ge(S("knew_out").sem, 2)
                    for g in range(2):
                        for b4 in range(4):
                            b = 4 * g + b4
                            q32 = qs[:, b, :, :, :].rearrange("p a b c -> p (a b c)")
                            r = slice(32 * b4, 32 * b4 + 32)
                            mm(ps[r, 0, 0:PAST + NT], q32, kselT[:, b, :])
                            mm(ps[r, 1, 0:PAST + NT], q32, kwinT[:, b, :])
                            mm(ps[r, 2, 0:NCS], q32, ckr[:, NCP + NCS * b:NCP + NCS * (b + 1)])
                        S("ss").on(mm(ps[:, 3, 0:3 * NH], C("pick" + str(g), NS), sig[0:NS, TT, NH:4 * NH]))
                        t.wait_ge(S("sp_ready").sem, 3 * (g + 1))
                        for s in range(2):
                            for i, (a, n) in enumerate(((0, P), (P, P), (PAST, NT))):
                                t.transpose(ps[0:n, 4 + s, P * i:P * (i + 1)], att[:, 0, s, a:a + n], C("ident"))
                        x = t.transpose(ps[0:NCS, 6, 0:P], att[:, 1, 0, 0:NCS], C("ident"))
                        S("spT").on(x)
                        t.wait_ge(S("spT_out").sem, 5 * (g + 1))
                        for b4 in range(4):
                            b = 4 * g + b4
                            c = slice(32 * b4, 32 * b4 + 32)
                            out = ps[:, 7, 32 * b:32 * b + 32]
                            mm(out, cvs[:, b, :], att[0:NCS, 1, 1, c], stop=False)
                            for s in range(2):
                                for pg in range(2):
                                    v = rows[:, 1, s, b, pg, :]
                                    mm(out, v, attT[:, s, P * pg + 32 * b4:P * pg + 32 * b4 + 32], start=False, stop=False)
                                x = mm(out, vnew[:, s, b, :], attT[0:NT, s, 2 * P + 32 * b4:2 * P + 32 * b4 + 32],
                                       start=False, stop=(s == 1))
                        S("so_att").on(x)

                    for d in range(KT):
                        n = N_TILES + d
                        c, col, _ = tiles[n]
                        t.wait_ge(S("w_low").sem, n + 1)
                        if d >= 4:
                            t.wait_ge(S("res_added").sem, d - 3)
                        S("res").on(dense(d % 4, high(n)[0], wslot(c, wring_r)[:, :, col:col + P], mix_hi, mixT_r,
                                          ready=(lambda k: (S("mix_low").sem, k + 1)) if d == 0 else None))
                    t.wait_ge(S("res_added").sem, KT)

                    norm_tensor(t, 1, lambda k: mixT[:, k, :])

                    def mlp_group(m):
                        for i in range(16):
                            c, col = i // 2, P * (i % 2)
                            t.wait_ge(S("w_low").sem, m * 16 + (N_FRONT + i + 1))
                            if i < 4:
                                t.wait_ge(S("res_added").sem, m * 8 + (5 + i))
                            elif i < 12:
                                t.wait_ge(S("relu_done").sem, m * 8 + (i - 3))
                            else:
                                t.wait_ge(S("res_added").sem, m * 8 + (8 + i - 11))
                            up, first = i < 8, i in (0, 8)
                            ready = (lambda k: (S("h_ready").sem, KT + k + 1)) if up else (
                                lambda k: (S("u_ready").sem, m * 8 + (k + 1)))
                            x = dense(i % 4, w_hi_mlp[i % 4], wslot(c, wring_r)[:, :, col:col + P], mix_hi if up else u_hi,
                                      hT_r if up else uT_r, ready=ready if first else None)
                            x.then_inc(S("up" if up else "res").sem, 1)

                    with t.Fori(0, NGROUP - 1) as m:
                        mlp_group(m)
                    mlp_group(NGROUP - 1)

                @block.scalar
                def _(act):
                    A1 = nc.scalar.activation
                    norm_scalar(act, 0, lambda k: sq[:, k % 4, :], 4,
                                [lambda e, n=n: split_high(e, n) for n in range(AHEAD)])
                    norm_high(act, 0, h_hi)
                    act.wait_ge(S("params").sem, 16 * 6)

                    def out_of(n, rows=P):
                        if n + AHEAD < N_GDN or N_GDN <= n < N_TILES - AHEAD:
                            split_high(act, n + AHEAD)
                        act.wait_ge(S("proj").sem, n + 1)
                        return whole(n % 4, rows)

                    for n in range(12):
                        src = out_of(n)
                        if n >= 3:
                            act.wait_ge(S("conv_done").sem, n - 2)
                            act.wait_ge(S("tail_out").sem, n - 2)
                        S("pre_out").on(A1(halves(pre[:, n % 3, :]), src, ACT.Copy))
                        S("proj_out").on(A1(halves(qkv[:, n, :]), src, ACT.Copy, scale=convw[:, n, CONV - 1:CONV]))
                    for n in range(12, 16):
                        S("proj_out").on(A1(halves(zT[:, n - 12, :]), out_of(n), ACT.Silu))
                    act.wait_ge(S("h_ready").sem, KT)
                    S("proj_out").on(A1(halves(rs[0:SMALLW, :]), out_of(16, SMALLW), ACT.Copy))
                    act.wait_ge(S("conv_done").sem, 12)
                    act.wait_ge(S("sconv_done").sem, 1)
                    for n in range(12):
                        S("silu").on(A1(qkv[:, n, :], qkv[:, n, :], ACT.Silu))

                    def l2_square(n):
                        if n >= 4:
                            act.wait_ge(S("l2_sum").sem, n - 3)
                        act.wait_ge(S("silu").sem, n + 1)
                        S("l2_square").on(A1(sq[:, n % 4, :], qkv[:, n, :], ACT.Square))

                    for n in range(4):
                        l2_square(n)
                    for n in range(8):
                        if n + 4 < 8:
                            l2_square(n + 4)
                        act.wait_ge(S("l2_out").sem, n + 1)
                        S("l2_root").on(A1(r_a[:, n % 4, :], r_a[:, n % 4, :], ACT.Sqrt))

                    act.wait_ge(S("decay_tensor").sem, 1)
                    act.wait_ge(S("zeroed").sem, 4)
                    W4 = TT * SMALLW
                    A1(tok_small[:, 0:TT, :].rearrange("p a b -> p (a b)"), ps[:, 0, 0:W4], ACT.Copy)
                    S("gates_act").on(A1(tok_small[0:NS, TT, :], ps[0:NS, 0, W4:W4 + SMALLW], ACT.Copy))
                    S("gates_act").on(A1(alog[:], alog[:], ACT.Exp))
                    act.wait_ge(S("gates_act").sem, 1)
                    S("gates_act").on(A1(sig[:], tok_small[:, :, NH:SMALLW], ACT.Exp, scale=-1.0))
                    act.wait_ge(S("decay_vector").sem, 1)
                    S("gates_act").on(A1(gt3[:], gt3[:], ACT.Exp, scale=-1.0))
                    act.wait_ge(S("gates_act").sem, 4)
                    S("gates_act").on(A1(gt3[:], gt3[:], ACT.Ln, bias=1.0))
                    act.wait_ge(S("decay_vector").sem, 3)
                    S("gates_act").on(A1(egc[:], gcum[:], ACT.Exp))
                    act.wait_ge(S("decay_vector").sem, 4)
                    S("gates_act").on(A1(edec[:], edec[:], ACT.Exp))
                    for q in range(TT + 1):
                        n = tile_len(q)
                        act.wait_ge(S("gchan_sum").sem, q + 1)
                        S("Eg_out").on(A1(Eg[:, :, cols(q)], heads4(ps[:, 2 + q, :], n), ACT.Exp))

                    def prepare(q):
                        n = tile_len(q)

                        def out(sem, name, hf, bank, wait):
                            act.wait_ge(S(wait).sem, S(sem).n + 1)
                            S(sem).on(A1(prep[name][0:n, hf, :, 0:n], heads4(ps[0:n, bank, :], n), ACT.Copy))

                        act.wait_ge(S("kv_turned").sem, q + 1)
                        S("v_out").on(A1(vtok[0:n].rearrange("p h d -> p (h d)"), ps[0:n, 1, :], ACT.Copy))
                        for hf in range(2):
                            act.wait_ge(S("G_masked").sem, 2 * q + hf + 1)
                            S("E_ready").on(A1(prep["a"][0:n, hf, :, 0:n], prep["a"][0:n, hf, :, 0:n], ACT.Exp))
                        for hf in range(2):
                            out("A_out", "a", hf, 2 + 3 * hf, "A_turned")
                        for hf in range(2):
                            out("D2_out", "f", hf, 3 + 3 * hf, "D2")
                        for hf in range(2):
                            out("D2T_out", "b", hf, 2 + 3 * hf, "D2T")
                        if q < TT:
                            for hf in range(2):
                                out("ID4T_out", "b", hf, 2 + 3 * hf, "ID4T")
                            for i in range(3):
                                for hf in range(2):
                                    out("PT_out", "b", hf, 4 + 3 * hf, "PT")
                        for hf in range(2):
                            act.wait_ge(S("wu").sem, 2 * q + hf + 1)
                            S("wT_out").on(A1(wqT[:, 0, 2 * hf:2 * hf + 2, 0:n],
                                              ps[:, 4 + 3 * hf, 0:2 * P].rearrange("p (a i) -> p a i", a=2)[:, :, 0:n],
                                              ACT.Copy))

                    for q in range(TT):
                        prepare(q)
                        for half in range(2):
                            n = 2 * q + half
                            act.wait_ge(S("oS").sem, n + 1)
                            S("oS_out").on(A1(mixT[:, 0:4, HD * n:HD * (n + 1)],
                                              ps[:, 2, 0:4 * HD].rearrange("p (a i) -> p a i", a=4), ACT.Copy))
                    prepare(TT)

                    act.wait_ge(S("sample_dve").sem, 3)
                    act.wait_ge(S("sadd_out").sem, 4)
                    act.wait_ge(S("oT_out").sem, 2 * TT)
                    for hp in range(4):
                        S("o_square").on(A1(osq[:, hp, :], mixT[:, hp, :], ACT.Square))
                    for hp in range(4):
                        act.wait_ge(S("o_mean").sem, hp + 1)
                        S("o_root").on(A1(qkv[:, 8 + hp, :], qkv[:, 8 + hp, :], ACT.Sqrt))

                    act.wait_ge(S("gdn_stored").sem, 48)
                    for n in range(N_GDN, N_GDN + AHEAD):
                        split_high(act, n)
                    for n in range(N_GDN, N_TILES):
                        S("proj_out").on(A1(halves(nsaT[:, n - N_GDN, :]), out_of(n), ACT.Copy))
                    for s in range(2):
                        act.wait_ge(S("v_turned").sem, s + 1)
                        S("v_copied").on(A1(vtp[:, s].rearrange("p a b -> p (a b)"), ps[:, s, :], ACT.Copy))
                    for s in range(2):
                        act.wait_ge(S("v_turned").sem, s + 3)
                        S("v_copied").on(A1(vnew[:, s].rearrange("p (a b) e -> p a (b e)", a=2),
                                          ps[0:NT, 2 + 2 * s:4 + 2 * s, :], ACT.Copy))
                    act.wait_ge(S("cv_turned").sem, 1)
                    S("cv_out").on(A1(cvs[:].rearrange("p (a b) e -> p a (b e)", a=2), ps[0:NCS, 4:6, :], ACT.Copy))
                    act.wait_ge(S("kz_zeroed").sem, 1)
                    act.wait_ge(S("rope_done").sem, len(ROPED))
                    for s in range(2):
                        for g in range(KVH):
                            r = slice(HD * g, HD * (g + 1))
                            S("kz_ready").on(A1(kz[r, s, g, :], nsaT[r, 6 + 2 * s, 0:SEQ], ACT.Copy))
                    act.wait_ge(S("compressed_vector").sem, 3)
                    S("compressed_scalar").on(A1(pc, pc, ACT.Exp, scale=SCALE))

                    def softmax(uu):
                        q, n, z = uu // NH, P * (uu // NH + 1), uu % 2
                        act.wait_ge(S("p_max").sem, uu + 1)
                        if uu >= 2:
                            act.wait_ge(S("pT").sem, 2 * (uu - 1))
                            act.wait_ge(S("r_ready").sem, uu - 1)
                        for s in range(2):
                            S("p_exp").on(A1(att[:, z, s, 0:n], ps[:, 2 * z + s, 0:n], ACT.Exp,
                                             bias=stat[:, 8 * z + 2 + s:8 * z + 3 + s], scale=SCALE,
                                             accum_out=stat[:, 8 * z + 4 + s:8 * z + 5 + s]))

                    def turned(uu):
                        n = P * (uu // NH + 1)
                        act.wait_ge(S("pT").sem, 2 * uu + 1)
                        if uu:
                            act.wait_ge(S("nsa").sem, uu)
                        S("pT_out0").on(A1(attT[:, 0, 0:n], ps[:, 4, 0:n], ACT.Copy))

                    def outputs(q):
                        act.wait_ge(S("o_turned").sem, q + 1)
                        S("o_out").on(A1(mixT[:, 4:8, cols(q)], heads4(ps[:, 4, :], P), ACT.Copy))

                    for what, i in SCHEDULE[:2]:
                        softmax(i)
                    act.wait_ge(S("compressed_tensor").sem, 2)
                    S("compressed_scalar").on(A1(pcT.rearrange("p q n -> p (q n)"), ps[:, 7, :], ACT.Copy))
                    for what, i in SCHEDULE[2:]:
                        if what != "v":
                            {"s": softmax, "t": turned, "o": outputs}[what](i)

                    for g in range(2):
                        act.wait_ge(S("s_max").sem, g + 1)
                        A1(att[:, 1, 0, 0:NCS], ps[:, 2, 0:NCS], ACT.Exp, bias=stat[:, 27:28], scale=SCALE,
                           accum_out=stat[:, 30:31])
                        for s in range(2):
                            x = A1(att[:, 0, s, 0:PAST + NT], ps[:, s, 0:PAST + NT], ACT.Exp,
                                   bias=stat[:, 28 + s:29 + s], scale=SCALE, accum_out=stat[:, 31 + s:32 + s])
                        S("s_exp").on(x)
                        act.wait_ge(S("spT").sem, g + 1)
                        S("spT_out").on(A1(att[0:NCS, 1, 1, 0:P], ps[0:NCS, 6, 0:P], ACT.Copy))
                        for s in range(2):
                            S("spT_out").on(A1(attT[:, s, 0:2 * P], ps[:, 4 + s, 0:2 * P], ACT.Copy))
                            S("spT_out").on(A1(attT[0:NT, s, 2 * P:3 * P], ps[0:NT, 4 + s, 2 * P:3 * P], ACT.Copy))

                    act.wait_ge(S("rows_stored").sem, 16)
                    act.wait_ge(S("nsa_mixed").sem, 2)
                    for n in range(N_TILES, N_TILES + AHEAD):
                        split_high(act, n)
                    for k in range(KT):
                        S("mix_high").on(A1(mix_hi[:, k, :], mixT[:, k, :], ACT.Copy))
                    for n in range(N_TILES + AHEAD, N_FRONT):
                        split_high(act, n)

                    act.wait_ge(S("res_added").sem, KT)
                    norm_scalar(act, 1, lambda k: mixT[:, k, :], KT,
                                [lambda e, i=i: mlp_split_high(e, 0, i) for i in range(AHEAD)])
                    norm_high(act, 1, mix_hi)

                    def mlp_group(m, last):
                        for i in range(16):
                            mlp_split_ahead(mlp_split_high, act, m, i, last)
                            if i < 8:
                                act.wait_ge(S("up").sem, m * 8 + (i + 1))
                                A1(halves(uT[:, i, :]), whole(i % 4), ACT.Relu).then_inc(S("relu_done").sem, 1)
                            if 1 <= i < 9:
                                act.wait_ge(S("u_square").sem, m * 8 + i)
                                A1(u_hi[:, i - 1, :], uT[:, i - 1, :], ACT.Copy).then_inc(S("u_high").sem, 1)

                    with act.Fori(0, NGROUP - 1) as m:
                        mlp_group(m, False)
                    mlp_group(NGROUP - 1, True)

                @block.vector
                def _(v):
                    def done(sem, instruction):
                        S(sem).on(instruction)
                        v.wait_ge(S(sem).sem, S(sem).n)

                    S("zeroed").on(v.memset(tok_small[:], 0.0))
                    S("zeroed").on(v.memset(gcum[:], 0.0))
                    S("zeroed").on(v.memset(edec[:], 0.0))
                    S("zeroed").on(v.memset(gt2[:], 0.0))
                    S("state").on(v.memset(St[:], 0.0))
                    v.wait_ge(S("params").sem, 16 * 6)
                    norm_vector(v, 0, gmix, hT, h_hi, [lambda e, n=n: split_low(e, n) for n in range(AHEAD)])

                    for n in range(12):
                        split_low(v, n + AHEAD)
                        v.wait_ge(S("pre_out").sem, n + 1)
                        v.wait_ge(S("proj_out").sem, n + 1)
                        for s in range(1, CONV):
                            x = v.scalar_tensor_tensor(qkv[:, n, s:SEQ], pre[:, n % 3, 0:SEQ - s],
                                                       convw[:, n, CONV - 1 - s:CONV - s], qkv[:, n, s:SEQ],
                                                       ALU.mult, ALU.add)
                            done("v_step" if s < CONV - 1 else "conv_done", x)

                    for n in range(12 + AHEAD, N_GDN):
                        split_low(v, n)

                    def l2_sum(n):
                        v.wait_ge(S("l2_sum").sem, n + 1)
                        if n >= 4:
                            v.wait_ge(S("l2_done").sem, n - 3)
                        S("l2_out").on(v.tensor_scalar(halves(r_a[:, n % 4, :]), whole(n % 4), EPS, None, ALU.add))

                    def l2_scale(n):
                        v.wait_ge(S("l2_root").sem, n + 1)
                        done("v_step", v.reciprocal(r_a[:, n % 4, :], r_a[:, n % 4, :]))
                        S("l2_done").on(v.scalar_tensor_tensor(qkv[:, n, :], qkv[:, n, :], SCALE if n < 4 else 1.0,
                                                               r_a[:, n % 4, :], ALU.mult, ALU.mult))

                    for n in range(9):
                        if n < 8:
                            l2_sum(n)
                        if n:
                            l2_scale(n - 1)

                    v.wait_ge(S("gates_act").sem, 1)
                    done("v_step", v.tensor_tensor(gt2[:], tok_small[:, :, 0:NH], mid(dtb[:], TT + 1), ALU.add))
                    done("v_step", v.tensor_scalar(gt3[:], gt2[:], -1.0, None, ALU.mult))
                    done("decay_vector", v.tensor_tensor(gt3[:], gt3[:], gt2[:], ALU.max))
                    v.wait_ge(S("gates_act").sem, 3)
                    done("v_step", v.tensor_scalar(sig[:], sig[:], 1.0, None, ALU.add))
                    done("v_step", v.reciprocal(sig[:], sig[:]))
                    v.wait_ge(S("gates_act").sem, 5)
                    done("v_step", v.scalar_tensor_tensor(gt2[:], gt2[:], 0.0, gt3[:], ALU.max, ALU.add))
                    v.wait_ge(S("gates_act").sem, 2)
                    done("v_step", v.tensor_tensor(gtok[:], gt2[:], mid(alog[:], TT + 1), ALU.mult))
                    done("decay_vector", v.tensor_scalar(gtok[:], gtok[:], -1.0, None, ALU.mult))
                    v.wait_ge(S("decay_tensor").sem, 2)
                    NG = TT * NH

                    def flat(ap):
                        return ap.rearrange("p a b -> p (a b)")

                    v.tensor_copy(flat(gcum[:, 0:TT, :]), ps[:, 1, 0:NG])
                    done("decay_vector", v.tensor_copy(gcum[0:NS, TT, :], ps[0:NS, 1, NG:NG + NH]))
                    v.tensor_tensor(flat(edec[:, 0:TT, :]), ps[:, 1, 64:64 + NG], flat(gcum[:, 0:TT, :]), ALU.subtract)
                    done("decay_vector", v.tensor_tensor(edec[0:NS, TT, :], ps[0:NS, 1, 64 + NG:64 + NG + NH],
                                                  gcum[0:NS, TT, :], ALU.subtract))

                    def prepare(q):
                        n = tile_len(q)

                        def pr(name, hf):
                            return prep[name][0:n, hf, :, 0:n]

                        def bank(b):
                            return heads4(ps[0:n, b, :], n)

                        v.wait_ge(S("kv_turned").sem, q + 1)
                        v.wait_ge(S("gates_act").sem, 7)
                        k_ps = ps[0:n, 0, :].rearrange("p (h d) -> p h d", h=NH)
                        S("kb_out").on(v.tensor_tensor(kb[0:n], k_ps, bc(egc[0:n, q, :], HD), ALU.mult))
                        S("kb_out").on(v.tensor_tensor(kdec[0:n], k_ps, bc(edec[0:n, q, :], HD), ALU.mult))
                        for hf in range(2):
                            v.wait_ge(S("grow").sem, 2 * q + hf + 1)
                            S("G_diff").on(v.tensor_tensor(pr("a", hf), bank(4 + 3 * hf),
                                                           bc(gcum[0:n, q, 4 * hf:4 * hf + 4], n), ALU.subtract))
                        for hf in range(2):
                            v.wait_ge(S("E_ready").sem, 2 * q + hf + 1)
                            b0 = 2 + 3 * hf

                            def gram(s):
                                return ps[0:n, b0:b0 + 2, 2 * P * s:2 * P * (s + 1)].rearrange(
                                    "p b (a i) -> p a b i", a=2)[:, :, :, 0:n]

                            def pairs(ap):
                                return ap.rearrange("p (a b) i -> p a b i", b=2)

                            v.tensor_tensor(pairs(qkm[0:n, 4 * hf:4 * hf + 4, 0:n]), gram(1), pairs(pr("a", hf)), ALU.mult)
                            S("GE_out").on(v.tensor_tensor(pairs(pr("b", hf)), gram(0), pairs(pr("a", hf)), ALU.mult))
                        for hf in range(2):
                            v.wait_ge(S("B_ready").sem, 2 * q + hf + 1)
                            done("v_step", v.tensor_tensor(pr("d", hf), pr("b", hf), mid(C("upper", n, n), 4), ALU.mult))
                            S("D_ready").on(v.tensor_tensor(pr("e", hf), mid(C("ident", n, n), 4), pr("d", hf),
                                                            ALU.subtract))
                        for hf in range(2):
                            v.wait_ge(S("P1").sem, 2 * q + hf + 1)
                            v.wait_ge(S("D_ready").sem, 2 * q + 2)
                            S("P1_out").on(v.tensor_copy(pr("d", hf), bank(3 + 3 * hf)))
                            if q < TT:
                                v.wait_ge(S("D4").sem, 2 * q + hf + 1)
                                S("ID4_out").on(v.tensor_tensor(pr("f", hf), bank(4 + 3 * hf),
                                                                mid(C("ident", n, n), 4), ALU.add))
                        if q < TT:
                            for hf in range(2):
                                v.wait_ge(S("Pn").sem, 2 * 4 * q + hf + 1)
                                S("Pn_out").on(v.tensor_copy(pr("e", hf), bank(3 + 3 * hf)))
                            for i in range(3):
                                for hf in range(2):
                                    v.wait_ge(S("X").sem, 2 * (3 * q + i) + hf + 1)
                                    S("IX_out").on(v.tensor_tensor(pr("f", hf), mid(C("ident", n, n), 4),
                                                                   bank(2 + 3 * hf), ALU.subtract))
                                for hf in range(2):
                                    v.wait_ge(S("Pn").sem, 2 * (4 * q + 1 + i) + hf + 1)
                                    S("Pn_out").on(v.tensor_copy(pr("de"[i % 2], hf), bank(3 + 3 * hf)))
                        for hf in range(2):
                            v.wait_ge(S("wu").sem, 2 * q + hf + 1)
                            S("u0_out").on(v.tensor_copy(u0[0:n, 4 * hf:4 * hf + 4, :],
                                                         ps[0:n, 2 + 3 * hf, 0:4 * HD].rearrange("p (h d) -> p h d", h=4)))

                    for q in range(TT):
                        prepare(q)
                        for half in range(2):
                            n = 2 * q + half
                            r = slice(HD * half, HD * half + HD)
                            v.wait_ge(S("wS").sem, n + 1)
                            v.wait_ge(S("u0_out").sem, 2 * (q + 1))
                            done("v_step", v.tensor_tensor(
                                u[r].rearrange("p (a b) d -> p a b d", b=2), u0[r].rearrange("p (a b) d -> p a b d", b=2),
                                ps[r, 0:2, 0:4 * HD].rearrange("p b (a d) -> p a b d", a=4), ALU.subtract))
                            S("u_out").on(v.tensor_tensor(u[r], u[r], bc(sig[r, q, 0:NH], HD), ALU.mult))
                            v.wait_ge(S("stmp_ready").sem, n + 1)
                            v.wait_ge(S("dS").sem, n + 1)
                            S("state").on(v.tensor_tensor(St[:], ps[:, 4, 0:4 * HD].rearrange("p (a e) -> p a e", a=4),
                                                          Stmp[:], ALU.add))
                            v.wait_ge(S("oS_out").sem, n + 1)
                            v.wait_ge(S("oU").sem, n + 1)
                            o = mixT[:, 0:4, HD * n:HD * (n + 1)]
                            S("oT_out").on(v.tensor_tensor(o, ps[:, 3, 0:4 * HD].rearrange("p (a i) -> p a i", a=4), o,
                                                           ALU.add))
                    prepare(TT)

                    v.wait_ge(S("sample_mm").sem, 1)
                    done("sample_dve", v.tensor_copy(xuT[:], ps[:, 0, 0:256].rearrange("p (a s i) -> p a s i", a=4, s=2)))
                    v.wait_ge(S("sample_mm").sem, 2)
                    v.wait_ge(S("u0_out").sem, 2 * (TT + 1))
                    done("v_step", v.tensor_tensor(u[0:NS], u0[0:NS], ps[0:NS, 1, :].rearrange("p (h d) -> p h d", h=NH),
                                                   ALU.subtract))
                    S("sample_dve").on(v.tensor_tensor(u[0:NS], u[0:NS], bc(sig[0:NS, TT, 0:NH], HD), ALU.mult))
                    v.wait_ge(S("sample_mm").sem, 3)
                    S("sample_dve").on(v.tensor_tensor(mixT[:, 0:4, SEQ:TOK], ps[:, 2, 0:4 * NS].rearrange("p (a i) -> p a i", a=4),
                                                   xuT[:, :, 1, :], ALU.add))
                    for hp in range(4):
                        v.wait_ge(S("sdS").sem, hp + 1)
                        v.wait_ge(S("sadd_out").sem, hp + 1)
                        S("sdS_out").on(v.tensor_tensor(Ss[:, :, hp, :], ps[:, 3 + hp, :].rearrange("p (b e) -> p b e", b=NB),
                                                        sadd[:, hp % 2], ALU.add))
                    for hp in range(4):
                        v.wait_ge(S("o_sum").sem, hp + 1)
                        S("o_mean").on(v.tensor_scalar(halves(qkv[:, 8 + hp, :]), whole(hp), 1.0 / HD, EPS,
                                                       ALU.mult, ALU.add))
                    for hp in range(4):
                        v.wait_ge(S("o_root").sem, hp + 1)
                        done("v_step", v.reciprocal(qkv[:, 8 + hp, :], qkv[:, 8 + hp, :]))
                        done("v_step", v.scalar_tensor_tensor(mixT[:, hp, :], mixT[:, hp, :], ggdn[:, 0:1],
                                                              qkv[:, 8 + hp, :], ALU.mult, ALU.mult))
                        S("gdn_mixed").on(v.tensor_tensor(mixT[:, hp, :], mixT[:, hp, :], zT[:, hp, :], ALU.mult))

                    for n in range(N_GDN, N_TILES):
                        split_low(v, n)

                    for i, n in enumerate(ROPED):
                        v.wait_ge(S("rot").sem, i + 1)
                        if i:
                            v.wait_ge(S("rope_done").sem, i)
                        done("rope_sin", v.tensor_tensor(halves(rs[:]), whole(i % 4), halves(C("sin")), ALU.mult))
                        v.wait_ge(S("rope_cos").sem, i + 1)
                        S("rope_done").on(v.tensor_tensor(nsaT[:, n, :], nsaT[:, n, :], rs[:], ALU.add))
                    for i in range(2 * NB):
                        b, bank = i // 2, 6 + i % 2
                        if i % 2 == 0:
                            v.wait_ge(S("kpast_turned").sem, i + 1)
                            v.tensor_copy(kselT[:, b, 0:PAST], ps[:, bank, 0:PAST])
                            S("kpast_out").on(v.tensor_copy(kwinT[:, b, 0:PAST], ps[:, bank, PAST:2 * PAST]))
                        else:
                            v.wait_ge(S("kpast_turned").sem, i + 1)
                            S("kpast_out").on(v.tensor_copy(cmpT[:, :, b, :],
                                                            ps[:, bank, :].rearrange("p (s t) -> p s t", s=2)))
                    for s in range(2):
                        v.wait_ge(S("cmp").sem, s + 1)
                        done("v_step", v.tensor_copy(ckT[:, s, :], ps[:, s, 0:NCA + 1]))
                        S("ck_out").on(v.tensor_scalar(ckT[:, s, 0:NCA], ckT[:, s, 0:NCA], ckT[:, s, NCA:NCA + 1], None,
                                                       ALU.add))
                    v.wait_ge(S("ck_rot").sem, 1)
                    v.wait_ge(S("rope_done").sem, len(ROPED))
                    done("v_step", v.tensor_tensor(rs[:, 0:NCA], ps[:, 2, 0:NCA], C("sinc"), ALU.mult))
                    v.wait_ge(S("ck_cos").sem, 1)
                    done("v_step", v.tensor_tensor(ckr[:], ckr[:], rs[:, 0:NCA], ALU.add))
                    v.wait_ge(S("kz_zeroed").sem, 1)
                    for g in range(KVH):
                        r = slice(HD * g, HD * (g + 1))
                        x = v.tensor_copy(ckz[r, g, :], ckr[r, 0:NCP])
                    S("compressed_vector").on(x)
                    v.wait_ge(S("cv_turned").sem, 1)
                    S("compressed_vector").on(v.tensor_tensor(
                        cvb.rearrange("p (g j) d -> p g j d", g=KVH),
                        ps[:, 3, 0:P].rearrange("p (g d) -> p g d", g=KVH).unsqueeze(2).to_broadcast([P, KVH, GQA, HD]),
                        C("cmphead").rearrange("p (g j) -> p g j", g=KVH).unsqueeze(3).to_broadcast([P, KVH, GQA, HD]),
                        ALU.mult))

                    def gates(q):
                        return sig[:, q, NH:4 * NH].rearrange("p (h r) -> p h r", r=3)

                    v.wait_ge(S("compressed_tensor").sem, 1)
                    late = C("cmpneg").rearrange("p (q n) -> p q n", q=TT).unsqueeze(2).to_broadcast([P, TT, NH, NCP])
                    pc3 = pc.rearrange("p q h n -> p (q h) n")
                    done("v_step", v.tensor_tensor(pc, ps[:, 6, :].rearrange("p (q h n) -> p q h n", q=TT, h=NH), late,
                                                   ALU.add))
                    done("v_step", v.tensor_reduce(cstat, pc3, AX.X, ALU.max))
                    done("v_step", v.tensor_scalar(cstat, cstat, FLOOR, None, ALU.max))
                    done("compressed_vector", v.tensor_tensor(pc3, pc3, bc(cstat, NCP), ALU.subtract))

                    def compressed_sums():
                        v.wait_ge(S("compressed_scalar").sem, 1)
                        done("v_step", v.tensor_reduce(cstat, pc3, AX.X, ALU.add))
                        done("v_step", v.tensor_scalar(cstat, cstat, 1e-30, None, ALU.max))
                        done("v_step", v.reciprocal(cstat, cstat))
                        c4 = cstat.rearrange("p (q j g) -> p q j g", q=TT, j=GQA)
                        for q in range(TT):
                            x = v.tensor_tensor(c4[:, q], c4[:, q], sig[:, q, NH:4 * NH].rearrange(
                                "p (g j r) -> p r j g", g=KVH, j=GQA)[:, 0], ALU.mult)
                        done("v_step", x)
                        S("compressed_vector").on(v.tensor_tensor(pc3, pc3, bc(cstat, NCP), ALU.mult))

                    def maxima(uu):
                        q, z = uu // NH, uu % 2
                        n = P * (q + 1)
                        v.wait_ge(S("score").sem, uu + 1)
                        both = ps[:, 2 * z:2 * z + 2, :]
                        diag = both[:, :, P * q:P * (q + 1)]
                        done("v_step", v.tensor_tensor(diag, diag, mid(C("causal"), 2), ALU.add))
                        if uu >= 2:
                            v.wait_ge(S("p_exp").sem, 2 * (uu - 1))
                        done("v_step", v.tensor_reduce(stat[:, 8 * z:8 * z + 2], both[:, :, 0:n], AX.X, ALU.max))
                        S("p_max").on(v.tensor_scalar(stat[:, 8 * z + 2:8 * z + 4], stat[:, 8 * z:8 * z + 2], -SCALE, None,
                                                      ALU.mult))

                    def turned(uu):
                        n = P * (uu // NH + 1)
                        v.wait_ge(S("pT").sem, 2 * uu + 2)
                        if uu:
                            v.wait_ge(S("nsa").sem, uu)
                        S("pT_out1").on(v.tensor_copy(attT[:, 1, 0:n], ps[:, 5, 0:n]))
                        (q, h), z = divmod(uu, NH), uu % 2
                        st = stat[:, 8 * z + 4:8 * z + 6]
                        v.wait_ge(S("p_exp").sem, 2 * (uu + 1))
                        done("v_step", v.tensor_scalar(st, st, 1e-30, None, ALU.max))
                        done("v_step", v.reciprocal(st, st))
                        S("r_ready").on(v.tensor_tensor(stat[:, 48 + 3 * z:50 + 3 * z], gates(q)[:, h, 1:3], st,
                                                        ALU.mult))

                    def scale(uu):
                        z = uu % 2
                        v.wait_ge(S("nsa").sem, uu + 1)
                        v.wait_ge(S("r_ready").sem, uu + 1)
                        if uu >= 2:
                            v.wait_ge(S("o_added").sem, uu - 1)
                        S("o_scaled").on(v.tensor_tensor(
                            scaled[:, z], ps[:, 6 + z, 0:3 * HD].rearrange("p (s d) -> p s d", s=3),
                            bc(stat[:, 48 + 3 * z:51 + 3 * z], HD), ALU.mult))

                    done("v_step", v.memset(stat[:, 48:54], 1.0))
                    maxima(0)
                    maxima(1)
                    compressed_sums()
                    for what, i in SCHEDULE[2:]:
                        if what != "o":
                            {"s": maxima, "t": turned, "v": scale}[what](i)

                    for g in range(2):
                        v.wait_ge(S("ss").sem, g + 1)
                        both = ps[:, 0:2, :]
                        new = both[:, :, PAST:PAST + NT]
                        if g:
                            v.wait_ge(S("sp_ready").sem, 3 * g)
                        done("v_step", v.tensor_tensor(new, new, mid(C("newneg"), 2), ALU.add))
                        v.tensor_reduce(stat[:, 24:25], ps[:, 2, 0:NCS], AX.X, ALU.max)
                        done("v_step", v.tensor_reduce(stat[:, 25:27], both[:, :, 0:PAST + NT], AX.X, ALU.max))
                        done("s_max", v.tensor_scalar(stat[:, 27:30], stat[:, 24:27], -SCALE, None, ALU.mult))
                        done("v_step", v.tensor_tensor(stat[:, 64:64 + 3 * NH].rearrange("p (h r) -> p h r", r=3),
                                                       ps[:, 3, 0:3 * NH].rearrange("p (h r) -> p h r", r=3),
                                                       bc(C("rowhead"), 3), ALU.mult))
                        done("v_step", v.tensor_reduce(stat[:, 33:36], stat[:, 64:64 + 3 * NH].rearrange(
                            "p (h r) -> p r h", r=3), AX.X, ALU.add))
                        v.wait_ge(S("s_exp").sem, g + 1)
                        done("v_step", v.tensor_scalar(stat[:, 30:33], stat[:, 30:33], 1e-30, None, ALU.max))
                        done("v_step", v.reciprocal(stat[:, 36:39], stat[:, 30:33]))
                        done("v_step", v.tensor_tensor(stat[:, 36:39], stat[:, 36:39], stat[:, 33:36], ALU.mult))
                        S("sp_ready").on(v.tensor_scalar(att[:, 1, 0, 0:NCS], att[:, 1, 0, 0:NCS], stat[:, 36:37], None,
                                                         ALU.mult))
                        for s in range(2):
                            S("sp_ready").on(v.tensor_scalar(att[:, 0, s, 0:PAST + NT], att[:, 0, s, 0:PAST + NT],
                                                             stat[:, 37 + s:38 + s], None, ALU.mult))
                    v.wait_ge(S("so_att").sem, 2)
                    for g in range(KVH):
                        r = slice(HD * g, HD * (g + 1))
                        src = ps[r, 7, 0:8 * 32].rearrange("p (b k j t) -> p k j b t", b=NB, k=KVH, j=GQA)[:, g]
                        S("nsa_mixed").on(v.tensor_copy(mixT[r, 4:8, SEQ:TOK].rearrange("p j (b t) -> p j b t", b=NB), src))

                    v.wait_ge(S("nsa_mixed").sem, 2)
                    for n in range(N_TILES, N_TILES + AHEAD):
                        split_low(v, n)
                    for k in range(KT):
                        v.wait_ge(S("mix_high").sem, k + 1)
                        S("mix_low").on(v.tensor_tensor(mixT_r[:, k, :], mixT[:, k, :], F(mix_hi[:, k, :]), ALU.subtract))
                    for d in range(KT):
                        if d + AHEAD < KT:
                            split_low(v, N_TILES + d + AHEAD)
                        v.wait_ge(S("res").sem, d + 1)
                        S("res_added").on(v.tensor_tensor(halves(xT[:, d, :]), whole(d % 4), halves(xT[:, d, :]), ALU.add))
                    v.wait_ge(S("res_added").sem, KT)
                    norm_vector(v, 1, gmlp, hT, mix_hi, [lambda e, i=i: mlp_split_low(e, 0, i) for i in range(AHEAD)])

                    def mlp_group(m, last):
                        for i in range(16):
                            mlp_split_ahead(mlp_split_low, v, m, i, last)
                            if i < 8:
                                v.wait_ge(S("relu_done").sem, m * 8 + (i + 1))
                                v.tensor_tensor(uT[:, i, :], uT[:, i, :], uT[:, i, :], ALU.mult).then_inc(
                                    S("u_square").sem, 1)
                            if 1 <= i < 9:
                                v.wait_ge(S("u_high").sem, m * 8 + i)
                                v.tensor_tensor(uT_r[:, i - 1, :], uT[:, i - 1, :], F(u_hi[:, i - 1, :]), ALU.subtract).then_inc(
                                    S("u_ready").sem, 1)
                            if i >= 8:
                                d = i - 8
                                v.wait_ge(S("res").sem, m * 8 + (KT + d + 1))
                                v.tensor_tensor(halves(xT[:, d, :]), whole(d % 4), halves(xT[:, d, :]),
                                                ALU.add).then_inc(S("res_added").sem, 1)

                    with v.Fori(0, NGROUP - 1) as m:
                        mlp_group(m, False)
                    mlp_group(NGROUP - 1, True)

                @block.gpsimd
                def _(g_):
                    g = g_

                    def done(sem, instruction):
                        S(sem).on(instruction)
                        g.wait_ge(S(sem).sem, S(sem).n)

                    for n in range(12):
                        g.wait_ge(S("pre_out").sem, n + 1)
                        g.tensor_copy(xs[:, n, :, 3:7], pre[:, n % 3, SEQ:TOK].rearrange("p (b t) -> p b t", b=NB))
                        S("tail_out").on(g.tensor_copy(ctail[:, n, 0:3], pre[:, n % 3, SEQ - 3:SEQ]))
                    g.wait_ge(S("tail_out").sem, 12)
                    g.wait_ge(S("conv_state_in").sem, 16)
                    S("tail_out").on(g.tensor_copy(ctail[:, :, 3:].rearrange("p n (b t) -> p n b t", b=NB), xs[:, :, :, 4:7]))
                    g.wait_ge(S("proj_out").sem, 12)
                    for i in range(CONV - 1):
                        w = convw[:, :, i:i + 1].to_broadcast([P, 12, NS])
                        for b in range(NB):
                            x = g.tensor_tensor(cmul[:, :, NT * b:NT * (b + 1)], xs[:, :, b, i:i + NT],
                                                w[:, :, 0:NT], ALU.mult)
                        done("g_step", x)
                        done("sconv_done" if i == CONV - 2 else "g_step",
                             g.tensor_tensor(qkv[:, :, SEQ:TOK], qkv[:, :, SEQ:TOK], cmul[:], ALU.add))

                    def prepare(q):
                        n = tile_len(q)

                        def pr(name, hf):
                            return prep[name][0:n, hf, :, 0:n]

                        neg = C("negp" if q < TT else "negs", n, n)
                        cum = C("cump" if q < TT else "cums", n, n)
                        g.wait_ge(S("decay_vector").sem, 2)
                        g.wait_ge(S("kv_turned").sem, q + 1)
                        for hf in range(2):
                            S("gU_ready").on(g.tensor_tensor(pr("d", hf), mid(cum, 4),
                                                             bc(gtok[0:n, q, 4 * hf:4 * hf + 4], n), ALU.mult))
                        for hf in range(2):
                            g.wait_ge(S("G_diff").sem, 2 * q + hf + 1)
                            S("G_masked").on(g.tensor_tensor(pr("a", hf), pr("a", hf), mid(neg, 4), ALU.add))
                        g.wait_ge(S("gram").sem, 2 * q + 2)
                        g.wait_ge(S("Eg_out").sem, TT + 1)
                        if q < TT:
                            S("qe_out").on(g.tensor_tensor(qkv[:, 0:4, cols(q)], qkv[:, 0:4, cols(q)], Eg[:, :, cols(q)],
                                                           ALU.mult))
                        else:
                            S("qe_out").on(g.tensor_tensor(wqT[:, 1, :, 0:NS], qkv[:, 0:4, cols(q)], Eg[:, :, cols(q)],
                                                           ALU.mult))
                        for hf in range(2):
                            g.wait_ge(S("GE_out").sem, 2 * q + hf + 1)
                            S("B_ready").on(g.tensor_tensor(pr("b", hf), pr("b", hf), bc(sig[0:n, q, 4 * hf:4 * hf + 4], n),
                                                            ALU.mult))
                        for hf in range(2):
                            g.wait_ge(S("A_out").sem, 2 * q + hf + 1)
                            S("AD_ready").on(g.tensor_tensor(pr("c", hf), pr("a", hf), mid(C("lower", n, n), 4), ALU.mult))
                        for hf in range(2):
                            g.wait_ge(S("D2T_out").sem, 2 * q + hf + 1)
                            S("ID2T_out").on(g.tensor_tensor(pr("c", hf), pr("b", hf), mid(C("ident", n, n), 4), ALU.add))
                        if q < TT:
                            for hf in range(2):
                                S("M_ready").on(g.tensor_tensor(pr("m", hf), pr("a", hf),
                                                                mid(C("low16", n, n), 4), ALU.mult))
                            for i, lev in enumerate(LEVELS[1:]):
                                for hf in range(2):
                                    g.wait_ge(S("X").sem, 2 * (3 * q + i) + hf + 1)
                                    S("M_ready").on(g.tensor_tensor(pr("m", hf), pr("a", hf),
                                                                    mid(C("low" + str(lev), n, n), 4), ALU.mult))
                            for half in range(2):
                                c = 2 * q + half
                                g.wait_ge(S("state").sem, c + 1)
                                last = Eg[:, :, HD * c + HD - 1:HD * c + HD].to_broadcast([P, 4, HD])
                                S("stmp_ready").on(g.tensor_tensor(Stmp[:], St[:], last, ALU.mult))

                    for q in range(TT + 1):
                        prepare(q)
                    g.wait_ge(S("states_in").sem, 16)
                    g.wait_ge(S("sample_dve").sem, 2)
                    for h in range(NH):
                        S("um_out").on(g.tensor_tensor(um[:, h], mid(u[0:NS, h, :], NB), bc(C("seqof", NS), HD), ALU.mult))
                    for hp in range(4):
                        if hp >= 2:
                            g.wait_ge(S("sdS_out").sem, hp - 1)
                        last = Eg[:, hp, SEQ:TOK].rearrange("p (b t) -> p b t", b=NB)[:, :, NT - 1:NT].to_broadcast([P, NB, HD])
                        S("sadd_out").on(g.tensor_tensor(sadd[:, hp % 2], Ss[:, :, hp, :], last, ALU.mult))

                    g.wait_ge(S("proj_out").sem, N_TILES)
                    S("qs_ready").on(g.memset(qs[:], 0.0))
                    for i, n in enumerate(ROPED):
                        g.wait_ge(S("rot").sem, i + 1)
                        S("rope_cos").on(g.tensor_tensor(nsaT[:, n, :], nsaT[:, n, :], C("cos"), ALU.mult))
                    g.wait_ge(S("qs_ready").sem, 1)
                    g.wait_ge(S("rope_done").sem, len(ROPED))
                    for k in range(KVH):
                        r = slice(HD * k, HD * (k + 1))
                        done("qs_ready", g.tensor_copy(qs[r, :, k, :, :], nsaT[r, 0:4, SEQ:TOK].rearrange(
                            "p j (b t) -> p b j t", b=NB)))
                    for n, kT in ((6, kselT), (8, kwinT)):
                        S("knew_out").on(g.tensor_copy(kT[:, :, PAST:PAST + NT],
                                                       nsaT[:, n, SEQ:TOK].rearrange("p (b t) -> p b t", b=NB)))
                    g.wait_ge(S("kpast_turned").sem, 2 * NB)
                    g.memset(ckz, 0.0)
                    S("kz_zeroed").on(g.memset(kz, 0.0))
                    g.wait_ge(S("ck_out").sem, 1)
                    S("ck_cos").on(g.tensor_tensor(ckr[:], ckT[:, 0, 0:NCA], C("cosc"), ALU.mult))
                    g.wait_ge(S("ck_out").sem, 2)
                    S("cvrep_ready").on(g.tensor_copy(cvrep.rearrange("p (h n) -> p h n", h=NH),
                                                      mid(ckT[:, 1, 0:NCP], NH)))

                    def add(uu):
                        (q, h), z = divmod(uu, NH), uu % 2
                        out = osum[:, q % 2, h % GQA, h // GQA, :]
                        g.wait_ge(S("o_scaled").sem, uu + 1)
                        if q >= 2:
                            g.wait_ge(S("o_turned").sem, q - 1)
                        done("g_step", g.tensor_tensor(out, scaled[:, z, 0], scaled[:, z, 1], ALU.add))
                        S("o_added").on(g.tensor_tensor(out, out, scaled[:, z, 2], ALU.add))

                    for uu in range(UNITS):
                        add(uu)

            nums = sorted(x.sem.num for x in signals.values())
            assert setup.num not in range(nums[0], nums[-1] + 1)
            nc.gpsimd.sem_clear(range(nums[0], nums[-1] + 1))
            nc.all_engine_barrier()
            for x in signals.values():
                x.n = 0

        last = [ctx.enter_context(nc.semaphore("stored"))]
        with nc.Block() as block:
            @block.tensor
            def _(t):
                norm_tensor(t, 0, lambda k: mixT[:, k, :])

            @block.scalar
            def _(act):
                norm_scalar(act, 0, lambda k: mixT[:, k, :], KT)

            @block.vector
            def _(v):
                norm_vector(v, 0, gfin, hT)

            @block.sync
            def _(sp):
                sp.wait_ge(S("h_full").sem, KT)
                sp.dma_start(O["yT"], hT[:]).then_inc(last[0], 16)
                sp.wait_ge(last[0], 16)


def kernel(x_prompt, x_sample, cache_kv, page_table, state_win, state_gdn, state_conv, norm_mix, w_in, conv_w,
           a_log, dt_bias, gdn_norm, cmp_pe_k, cmp_w_k, cmp_pe_v, cmp_w_v, w_out, norm_mlp, w_up, w_down,
           norm_final):
    import concourse.bacc as bacc
    from concourse.bass_utils import run_bass_kernel_spmd

    def tiled(a, axis=-1):
        a = np.moveaxis(np.asarray(a), axis, 0)
        return np.moveaxis(a.reshape((a.shape[0] // P, P) + a.shape[1:]), 1, 0)

    L = DEPTH
    x = np.concatenate([np.asarray(x_prompt)[0], np.asarray(x_sample).reshape(NS, D)], 0)
    arrays = {
        "xT": tiled(x),
        "norm_final": tiled(norm_final),
        "norm_mix": np.stack([tiled(a) for a in np.asarray(norm_mix)]),
        "norm_mlp": np.stack([tiled(a) for a in np.asarray(norm_mlp)]),
        "gdn_norm": np.concatenate([np.asarray(gdn_norm)] * 2, 1)[:, :, None],
        "conv_w": np.stack([np.moveaxis(tiled(a), 2, 2) for a in np.asarray(conv_w)]),
        "state_conv": np.stack([tiled(a) for a in np.asarray(state_conv)]),
        "state_gdn": np.asarray(state_gdn).reshape(L, NB, 4, 2, HD, HD).transpose(0, 3, 4, 1, 2, 5).reshape(
            L, P, NB, 4, HD),
        "page_table": np.asarray(page_table).reshape(1, NPG),
        "cmp_pe_k": np.asarray(cmp_pe_k).transpose(0, 2, 1),
        "cmp_pe_v": np.asarray(cmp_pe_v).transpose(0, 2, 1),
        "consts": CONST_TABLE,
        "cache_kv": cache_kv, "state_win": state_win, "w_in": w_in, "a_log": a_log, "dt_bias": dt_bias,
        "cmp_w_k": cmp_w_k, "cmp_w_v": cmp_w_v, "w_out": w_out, "w_up": w_up, "w_down": w_down,
    }
    arrays = {k: np.ascontiguousarray(np.asarray(a)) for k, a in arrays.items()}
    shapes = {
        "yT": (P, KT, TOK), "rows_T": (L, P, 6, TOK), "win_past": (L, NB, PAST - NT, 2, KVH, HD),
        "gdn_p": (L, P, 4, HD), "gdn_s": (L, P, NB, 4, HD), "conv_T": (L, P, 12, 3 + 3 * NB),
    }
    nc = bacc.Bacc("TRN2", target_bir_lowering=False, num_devices=1)
    A = {k: nc.dram_tensor("in_" + k, a.shape, mybir.dt.from_np(a.dtype), kind="ExternalInput").ap()
         for k, a in arrays.items()}
    O = {k: nc.dram_tensor("out_" + k, s, F32, kind="ExternalOutput").ap() for k, s in shapes.items()}
    build(nc, A, O)
    r = run_bass_kernel_spmd(nc, [{"in_" + k: a for k, a in arrays.items()}], core_ids=[0]).results[0]
    o = {k: np.asarray(r["out_" + k]) for k in shapes}

    y = o["yT"].transpose(2, 1, 0).reshape(TOK, D)
    rows = o["rows_T"].reshape(L, KVH, HD, 6, TOK).transpose(0, 1, 4, 3, 2)
    rows_p = rows[:, None, :, 0:SEQ, 0:4]
    rows_s = rows[:, :, SEQ:, 0:4].reshape(L, KVH, NB, NT, 4, HD).transpose(0, 2, 1, 3, 4, 5)
    win_new = rows[:, :, :, 4:6].transpose(0, 2, 3, 1, 4)
    win_p = win_new[:, None, 0:SEQ]
    win_s = np.concatenate([o["win_past"], win_new[:, SEQ:].reshape(L, NB, NT, 2, KVH, HD)], 2)
    gdn_p = o["gdn_p"].reshape(L, 2, HD, 4, HD).transpose(0, 3, 1, 2, 4).reshape(L, 1, NH, HD, HD)
    gdn_s = o["gdn_s"].reshape(L, 2, HD, NB, 4, HD).transpose(0, 3, 4, 1, 2, 5).reshape(L, NB, NH, HD, HD)
    conv = o["conv_T"].transpose(0, 3, 2, 1).reshape(L, 3 + 3 * NB, C_QKV)
    conv_p = conv[:, None, 0:3]
    conv_s = conv[:, 3:].reshape(L, NB, 3, C_QKV)
    return tuple(np.ascontiguousarray(a) for a in (
        y[None, 0:SEQ], y[SEQ:].reshape(NB, NT, D), rows_p, rows_s, win_p, win_s, gdn_p, gdn_s, conv_p, conv_s))
```

```python
from contextlib import ExitStack

import numpy as np

import concourse.bass as bass
from concourse import mybir

F32 = mybir.dt.float32
F32R = mybir.dt.float32r
I32 = mybir.dt.int32
ALU = mybir.AluOpType
ACT = mybir.ActivationFunctionType
AX = mybir.AxisListType

P = 128
D = 1024
SEQ = 512
DEPTH = 2
NB = 8
NT = 4
NS = NB * NT
TOK = SEQ + NS
HALF = TOK // 2
PAST = 256
PAGE = 128
HD = 64
NH = 8
KVH = 2
GQA = NH // KVH
KT = D // P
CONV = 4
CHUNK = 64
CMP = 32
SEL = 64
TOP_K = 16
WINDOW = 512
DFF = 4 * D
EPS = 1e-6
THETA = 10000.0
NEG = -1e30
FLOOR = -1e25
N_POOL = NB * (PAST // PAGE) * 5 // 4
C_QKV = 3 * NH * HD
O_Z = C_QKV
O_AB = O_Z + NH * HD
O_Q = O_AB + 2 * NH
O_KV = O_Q + NH * HD
O_GATE = O_KV + 6 * KVH * HD
assert SEQ // SEL <= TOP_K and PAST // SEL + 1 <= TOP_K
assert SEQ <= WINDOW and PAST + NT <= WINDOW
TT = SEQ // P
NCP = SEQ // CMP
NCS = PAST // CMP
assert (PAST + NT) // CMP == NCS
NCA = NCP + NB * NCS
SHORT = NT + NCS + NT
SROW = 2 * PAST + SHORT
SLOT = 256
NSLOT = 4
GROUP = 1024
NGROUP = DFF // GROUP
BASE = 8
NPG = NB * (PAST // PAGE)
LEVELS = [16, 32, 64]
SCALE = HD ** -0.5
FRONT = 20
SMALLW = 2 * NH + 3 * NH

CONSTS = {}


def _consts():
    k = np.arange(P)[:, None]
    i = np.arange(P)[None, :]
    t = {}
    t["ident"] = (k == i)
    t["ones"] = np.ones((P, P))
    t["headsum"] = (k // HD == i)[:, 0:32]
    t["headspread"] = (k % 32 == i // HD)
    for name, c in (("p", CHUNK), ("s", NT)):
        same = k // c == i // c
        t["cum" + name] = same & (k <= i)
        t["seg" + name] = same
        t["neg" + name] = np.where(same & (k <= i), 0.0, NEG)
    t["upper"] = (k // BASE == i // BASE) & (k < i)
    t["lower"] = (k // BASE == i // BASE) & (k > i)
    b = BASE
    while b < CHUNK:
        t["low" + str(2 * b)] = (k // (2 * b) == i // (2 * b)) & (k // b != i // b) & (k > i)
        b *= 2
    t["causal"] = np.where(i <= k, 0.0, NEG)
    end = (np.arange(NCP) + 1) * CMP - 1
    t["cmpneg"] = np.concatenate([np.where(end[None, :] <= k + P * q, 0.0, NEG) for q in range(TT)], 1)
    new = np.arange(NT)[None, :]
    t["newneg"] = np.where(new <= k % NT, 0.0, NEG)
    d, e = k % HD, i % HD
    t["rot"] = (k // HD == i // HD) * ((d == e + HD // 2) * -1.0 + (d == e - HD // 2) * 1.0)
    inv = np.float32(THETA) ** (-np.arange(HD // 2, dtype=np.float32) / np.float32(HD // 2))
    pos = np.concatenate([np.arange(SEQ), np.tile(PAST + np.arange(NT), NB)]).astype(np.float32)
    cpos = np.concatenate([end, np.tile(end[:NCS], NB)]).astype(np.float32)
    freq = inv[np.arange(P) % (HD // 2)].astype(np.float32)
    for name, x in (("", pos), ("c", cpos)):
        ang = (x[None, :] * freq[:, None]).astype(np.float32)
        t["cos" + name] = np.cos(ang)
        t["sin" + name] = np.sin(ang)
    row_b, row_h, row_t = np.arange(P) // 32, np.arange(P) % 32 // NT, np.arange(P) % NT
    for g in range(2):
        t["pick" + str(g)] = (k == ((4 * g + row_b) * NT + row_t)[None, :])
    t["rowhead"] = (row_h[:, None] == np.arange(NH)[None, :])
    of_row = (k // NCP) % KVH * GQA + k // NCP // KVH
    t["cmphead"] = (of_row == np.arange(NH)[None, :])
    t["seqof"] = (k // NT == np.arange(NB)[None, :])
    at, cols = 0, []
    for name, v in t.items():
        v = np.asarray(v, dtype=np.float32)
        CONSTS[name] = (at, v.shape[1])
        at += v.shape[1]
        cols.append(v)
    return np.ascontiguousarray(np.concatenate(cols, 1))


CONST_TABLE = _consts()
NCONST = CONST_TABLE.shape[1]


class Signal:

    def __init__(self, sem):
        self.sem, self.n = sem, 0

    def on(self, instruction):
        instruction.then_inc(self.sem, 1)
        self.n += 1
        return self.n


def build(nc, A, O):
    ctx = ExitStack()
    with ctx:
        def sb(name, shape, dt=F32, into=ctx):
            return into.enter_context(nc.sbuf_tensor(name, shape, dt))

        def sb2(name, shape, into=ctx):
            with ExitStack() as first:
                plain = sb(name, shape, F32, first)
            return plain, sb(name + "_r", shape, F32R, into)

        def F(ap):
            return ap.bitcast(F32)

        signals = {}

        def S(name):
            if name not in signals:
                signals[name] = Signal(ctx.enter_context(nc.semaphore(name)))
            return signals[name]

        setup = ctx.enter_context(nc.semaphore("setup_loaded"))
        x_loaded = ctx.enter_context(nc.semaphore("x_loaded"))
        ps = ctx.enter_context(nc.psum_tensor("ps", [P, 8, 512], F32))

        xT = sb("xT_sb", [P, KT, TOK])
        hT, hT_r = sb2("hT", [P, KT, TOK])
        mixT, mixT_r = sb2("mixT", [P, KT, TOK])
        wring, wring_r = sb2("wring", [P, NSLOT, KT * SLOT])
        cst = sb("cst", [P, NCONST])
        pages = sb("pages", [1, NPG], I32)
        gmix = sb("gmix", [P, KT])
        gmlp = sb("gmlp", [P, KT])
        gfin = sb("gfin", [P, KT])
        ggdn = sb("ggdn", [P, 1])
        convw = sb("convw", [P, 12, CONV])
        dtb = sb("dtb", [P, NH])
        alog = sb("alog", [P, NH])
        tok_small = sb("tok_small", [P, TT + 1, SMALLW])
        sig = sb("sig", [P, TT + 1, 4 * NH])
        rs = sb("rs", [P, TOK])
        Eg = mixT[:, 4:8, :]
        osq = mixT[:, 4:8, :]

        def C(name, rows=P, cols=None):
            at, n = CONSTS[name]
            return cst[0:rows, at:at + (cols or n)]

        def bc(ap, n):
            return ap.unsqueeze(2).to_broadcast([ap.shape[0], ap.shape[1], n])

        def mid(ap, n):
            return ap.unsqueeze(1).to_broadcast([ap.shape[0], n, ap.shape[1]])

        with ExitStack() as gdn_ctx:
            h_hi = sb("h_hi", [P, KT, TOK], F32R, gdn_ctx)
            qkv = sb("qkv", [P, 12, TOK], into=gdn_ctx)
            zT = sb("zT", [P, 4, TOK], into=gdn_ctx)
            ctail = sb("ctail", [P, 12, 3 + NB * 3], into=gdn_ctx)
            St = sb("St", [P, 4, HD], into=gdn_ctx)
            Stmp = sb("Stmp", [P, 4, HD], into=gdn_ctx)
            gtok = sb("gtok", [P, TT + 1, NH], into=gdn_ctx)
            gt2 = sb("gt2", [P, TT + 1, NH], into=gdn_ctx)
            gt3 = sb("gt3", [P, TT + 1, NH], into=gdn_ctx)
            gcum = sb("gcum", [P, TT + 1, NH], into=gdn_ctx)
            egc = sb("egc", [P, TT + 1, NH], into=gdn_ctx)
            edec = sb("edec", [P, TT + 1, NH], into=gdn_ctx)
            qkm = sb("qkm", [P, 2, NH, P], into=gdn_ctx)
            kdec = sb("kdec", [P, 2, NH, HD], into=gdn_ctx)
            kb = sb("kb", [P, NH, HD], into=gdn_ctx)
            vtok = sb("vtok", [P, NH, HD], into=gdn_ctx)
            u0 = sb("u0", [P, NH, HD], into=gdn_ctx)
            wqT = sb("wqT", [P, 2, 4, P], into=gdn_ctx)
            u = sb("u", [P, NH, HD], into=gdn_ctx)
            with ExitStack() as prep_ctx:
                names = ["a", "b", "c", "d", "e", "f"]
                prep = {n: sb("prep_" + n, [P, 2, 4, P], into=prep_ctx) for n in names}
            with ExitStack() as conv_ctx:
                xs = sb("xs", [P, 12, NB, CONV - 1 + NT], into=conv_ctx)
                pre = sb("pre", [P, 3, TOK], into=conv_ctx)
                sq = sb("sq", [P, 4, TOK], into=conv_ctx)
                cmul = sb("cmul", [P, 12, NS], into=conv_ctx)
                r_a = sb("r_a", [P, 2, TOK], into=conv_ctx)
            with ExitStack() as sample_ctx:
                um = sb("um", [NS, NH, NB, HD], into=sample_ctx)
                xuT = sb("xuT", [P, 4, 2, NS], into=sample_ctx)
                sadd = qkm[:, (TT - 1) % 2].rearrange("p a b -> p (a b)").rearrange("p (a b d) -> p a b d", a=2, b=NB)
        with ExitStack() as nsa_ctx:
            past_keys = sb("past_keys", [P, KT * TOK], into=nsa_ctx)
            kselT, kwinT = (past_keys[:, NB * (PAST + NT) * i:NB * (PAST + NT) * (i + 1)].rearrange(
                "p (b t) -> p b t", b=NB) for i in range(2))
            nsaT = sb("nsaT", [P, 10, TOK], into=nsa_ctx)
            rows = sb("rows", [P, 2, 2, NB, 2, P], into=nsa_ctx)
            krows = rows[:, 0].rearrange("p s b g e -> p (s b g e)")
            kz = krows[:, 0:4 * SEQ].rearrange("p (s g n) -> p s g n", s=2, g=KVH)
            pc = krows[:, 4 * SEQ:5 * SEQ].rearrange("p (q h n) -> p q h n", q=TT, h=NH)
            pcT = krows[:, 5 * SEQ:6 * SEQ].rearrange("p (q n) -> p q n", q=TT)
            cvb = krows[:, 6 * SEQ:7 * SEQ].rearrange("p (h d) -> p h d", h=NH)
            cvrep = krows[:, 7 * SEQ:7 * SEQ + P]
            ckz = krows[:, 7 * SEQ + P:7 * SEQ + P + KVH * NCP].rearrange("p (g n) -> p g n", g=KVH)
            vsrc = krows[:, 7 * SEQ + 3 * P:7 * SEQ + 4 * P].rearrange("p (b n) -> p b n", b=NB)
            cstat = krows[:, 7 * SEQ + 2 * P:7 * SEQ + 2 * P + TT * NH]
            values, values_r = sb2("values", [P, 2 * (TT + NB) * P], nsa_ctx)
            vtp = values[:, 0:2 * TT * P].rearrange("p (s q e) -> p s q e", s=2, q=TT)
            vshort = values[0:SHORT, 2 * TT * P:2 * TT * P + NB * P].rearrange("p (b e) -> p b e", b=NB)
            ckT = sb("ckT", [P, 2, NCA + 1], into=nsa_ctx)
            ckr = sb("ckr", [P, NCA], into=nsa_ctx)
            pe = sb("pe", [P, 2, CMP], into=nsa_ctx)
            qs = sb("qs", [P, NB, KVH, GQA, NT], into=nsa_ctx)
            stat = sb("stat", [P, 96], into=nsa_ctx)
            sstat = sb("sstat", [P, 2, 48], into=nsa_ctx)
            cmp_rows = sb("cmp_rows", [P, NB, 2, 2, P], into=nsa_ctx)
            att = cmp_rows[:, 0:4].rearrange("p b g s e -> p (b g s e)").rearrange("p (a s n) -> p a s n", a=2, s=2)
            satt = cmp_rows[:, 4:8].rearrange("p b g s e -> p (b g s e)").rearrange("p (a n) -> p a n", a=2)
            h_flat = hT[:, :, :].rearrange("p a b -> p (a b)")
            attT = h_flat[:, 0:1024].rearrange("p (s n) -> p s n", s=2)
            osum = h_flat[:, 1024:2048].rearrange("p (a j g d) -> p a j g d", a=2, j=GQA, g=KVH)
            scaled = h_flat[:, 2048:2048 + 6 * HD].rearrange("p (a s d) -> p a s d", a=2, s=3)
        with ExitStack() as mlp_ctx:
            mix_hi = sb("mix_hi", [P, KT, TOK], F32R, mlp_ctx)
            w_hi_mlp = sb("w_hi_mlp", [P, 4, KT * P], F32R, mlp_ctx)
            uT, uT_r = sb2("uT", [P, 8, TOK], mlp_ctx)
            u_hi = sb("u_hi", [P, 8, TOK], F32R, mlp_ctx)
        cmp_in = [h_flat[:, 0:(NCA + 1) * CMP],
                  wring[:, 0:2, :].rearrange("p a b -> p (a b)")[:, 0:(NCA + 1) * CMP]]

        def whole(pair, rows=P):
            return ps[0:rows, 2 * pair:2 * pair + 2, 0:HALF]

        def halves(ap):
            return ap.rearrange("p (a b) -> p a b", a=2)

        def heads4(ap, n):
            return ap.rearrange("p (h i) -> p h i", h=4)[:, :, 0:n]

        def tile_len(q):
            return P if q < TT else NS

        def cols(q):
            return slice(P * q, P * q + tile_len(q))

        def par(h):
            return slice(HD * (h % 2), HD * (h % 2) + HD)

        Ss = wring[:, 0, :].rearrange("p (b h d) -> p b h d", b=NB, h=4)

        def high_slots(flat, n):
            return [flat[:, KT * P * i:KT * P * (i + 1)].rearrange("p (k n) -> p k n", k=KT) for i in range(n)]

        w_hi_gdn = high_slots(mixT_r[:, :, :].rearrange("p k n -> p (k n)"), 4)
        w_hi_nsa = high_slots(values_r, 3)
        w_hi_mlp = high_slots(w_hi_mlp[:, :, :].rearrange("p a b -> p (a b)"), 4)

        def wslot(c, ring=wring):
            return ring[:, c % NSLOT, :].rearrange("p (k n) -> p k n", k=KT)

        def front_chunks(l):
            w_in = A["w_in"][l].rearrange("(k p) n -> p k n", p=P)
            w_out = A["w_out"][l]
            out = {}
            for c in range(6):
                out[c] = [(wslot(c), w_in[:, :, SLOT * c:SLOT * (c + 1)])]
            for c in range(2):
                out[6 + c] = [(wslot(6 + c), w_in[:, :, O_Z + SLOT * c:O_Z + SLOT * (c + 1)])]
            out[8] = [(wslot(8)[:, :, 0:2 * NH], w_in[:, :, O_AB:O_AB + 2 * NH]),
                      (wslot(8)[:, :, 2 * NH:SMALLW], w_in[:, :, O_GATE:O_GATE + 3 * NH])]
            for c in range(2):
                out[9 + c] = [(wslot(9 + c)[:, :, P * j + HD * g:P * j + HD * (g + 1)],
                               w_in[:, :, O_Q + HD * (GQA * g + 2 * c + j):O_Q + HD * (GQA * g + 2 * c + j + 1)])
                              for j in range(2) for g in range(KVH)]
            for c in range(3):
                out[11 + c] = [(wslot(11 + c), w_in[:, :, O_KV + SLOT * c:O_KV + SLOT * (c + 1)])]
            for c, name in enumerate(("cmp_w_k", "cmp_w_v")):
                dst = wring[:, (14 + c) % NSLOT, :].rearrange("p (c e) -> p c e", c=CMP)
                src = A[name][l].rearrange("c d e -> d c e")
                out[14 + c] = [(dst[HD * g:HD * (g + 1)], src) for g in range(KVH)]
            for c in range(4):
                n0, n1 = SLOT * c, SLOT * (c + 1)
                gdn = w_out[0:NH * HD, n0:n1].rearrange("(k p) n -> p k n", p=P)
                out[16 + c] = [(wslot(16 + c)[:, 0:4, :], gdn)]
                for g in range(KVH):
                    rows = w_out[(NH + GQA * g) * HD:(NH + GQA * (g + 1)) * HD, n0:n1]
                    out[16 + c].append((wslot(16 + c)[HD * g:HD * (g + 1), 4:8, :],
                                        rows.rearrange("(j d) n -> d j n", d=HD)))
            return out

        parts = {c: len(v) for c, v in front_chunks(0).items()}
        ld = [S(f"weights_in_slot{s}") for s in range(NSLOT)]

        def landed(c):
            return 16 * sum(parts[x] for x in range(c % NSLOT, c + 1, NSLOT))

        front_total = [landed(FRONT - NSLOT + s) for s in range(NSLOT)]

        def used(c):
            if c <= 8:
                return S("proj").sem, min(2 * (c + 1), 17)
            if c <= 13:
                return S("proj").sem, 17 + 2 * (c - 8)
            if c <= 15:
                return S("cmp").sem, c - 13
            return S("res").sem, 2 * (c - 15)

        tiles = [(c, P * j, P) for c in range(8) for j in range(2)] + [(8, 0, SMALLW)]
        tiles += [(c, P * j, P) for c in range(9, 14) for j in range(2)]
        N_GDN = 17
        N_TILES = len(tiles)
        tiles += [(16 + d // 2, P * (d % 2), P) for d in range(KT)]
        N_FRONT = len(tiles)

        def high(n):
            if n < N_GDN:
                slots, first = w_hi_gdn, 0
            elif n < N_TILES:
                slots, first = w_hi_nsa, N_GDN
            else:
                slots, first = w_hi_mlp, N_TILES
            at = (n - first) % len(slots)
            return slots[at], (n - len(slots) if n - first >= len(slots) else None)

        def tile_used(n):
            return (S("proj").sem, n + 1) if n < N_TILES else (S("res").sem, n - N_TILES + 1)

        def split_high(act, n):
            c, col, M = tiles[n]
            slot, before = high(n)
            act.wait_ge(ld[c % NSLOT].sem, landed(c))
            if before is not None:
                act.wait_ge(*tile_used(before))
            S("w_high").on(nc.scalar.activation(slot[:, :, 0:M], wslot(c)[:, :, col:col + M], ACT.Copy))

        def split_low(v, n):
            c, col, M = tiles[n]
            v.wait_ge(S("w_high").sem, n + 1)
            S("w_low").on(v.tensor_tensor(wslot(c, wring_r)[:, :, col:col + M], wslot(c)[:, :, col:col + M],
                                          F(high(n)[0][:, :, 0:M]), ALU.subtract))
        ROPED = (0, 1, 2, 3, 6, 8)
        UNITS = TT * NH
        SCHEDULE = [("s", 0), ("s", 1)]
        for uu in range(UNITS):
            SCHEDULE.append(("t", uu))
            if uu + 2 < UNITS:
                SCHEDULE.append(("s", uu + 2))
            SCHEDULE.append(("v", uu))
            if uu >= NH and uu % NH == 0:
                SCHEDULE.append(("o", uu // NH - 1))
        SCHEDULE.append(("o", TT - 1))

        def mlp_split_high(act, m, i):
            c, col = i // 2, P * (i % 2)
            act.wait_ge(ld[c % NSLOT].sem, m * 32 + (front_total[c % NSLOT] + 16 * (c // 4 + 1)))
            if i < 4:
                act.wait_ge(S("res").sem, m * 8 + (5 + i))
            elif i < 12:
                act.wait_ge(S("up").sem, m * 8 + (i - 3))
            else:
                act.wait_ge(S("res").sem, m * 8 + (8 + i - 11))
            nc.scalar.activation(w_hi_mlp[i % 4], wslot(c)[:, :, col:col + P], ACT.Copy).then_inc(
                S("w_high").sem, 1)

        def mlp_split_low(v, m, i):
            col = P * (i % 2)
            v.wait_ge(S("w_high").sem, m * 16 + (N_FRONT + i + 1))
            v.tensor_tensor(wslot(i // 2, wring_r)[:, :, col:col + P], wslot(i // 2)[:, :, col:col + P],
                            F(w_hi_mlp[i % 4]), ALU.subtract).then_inc(S("w_low").sem, 1)

        AHEAD = 2

        def mlp_split_ahead(split, engine, m, i, last):
            if i + AHEAD < 16:
                split(engine, m, i + AHEAD)
            elif not last:
                split(engine, m + 1, i + AHEAD - 16)

        with nc.Block() as block:
            @block.sync
            def _(sp):
                sp.dma_start(xT[:], A["xT"]).then_inc(x_loaded, 16)
                sp.dma_start(cst[:], A["consts"]).then_inc(setup, 16)
                sp.dma_start(pages[:], A["page_table"]).then_inc(setup, 16)
                sp.dma_start(gfin[:], A["norm_final"]).then_inc(setup, 16)
                sp.wait_ge(x_loaded, 16)

        def norm_sum(t, use, sq_of, k):
            t.wait_ge(S("norm_square").sem, use * KT + k + 1)
            for h in range(2):
                x = t.matmul(ps[:, 6 * use + h, 0:HALF], C("ones"), sq_of(k)[:, HALF * h:HALF * (h + 1)],
                             start=(k == 0), stop=(k == KT - 1), skip_group_check=True)
            S("norm_sum").on(x)

        def norm_tensor(t, use, sq_of):
            for k in range(KT):
                norm_sum(t, use, sq_of, k)

        def norm_scalar(act, use, sq_of, ring, between=()):
            for k in range(KT):
                if use:
                    act.wait_ge(S("res_added").sem, k + 1)
                if k >= ring:
                    act.wait_ge(S("norm_sum").sem, use * KT + k - ring + 1)
                S("norm_square").on(nc.scalar.activation(sq_of(k), xT[:, k, :], ACT.Square))
                if use and N_TILES + AHEAD + 2 + k < N_FRONT:
                    split_high(act, N_TILES + AHEAD + 2 + k)
            for split in between:
                split(act)
            act.wait_ge(S("norm_mean").sem, use + 1)
            S("norm_root").on(nc.scalar.activation(rs[:], rs[:], ACT.Sqrt))

        def norm_vector(v, use, g, out, high=None, between=()):
            v.wait_ge(S("norm_sum").sem, (use + 1) * KT)
            S("norm_mean").on(v.tensor_scalar(halves(rs[:]), whole(3 * use), 1.0 / D, EPS, ALU.mult, ALU.add))
            for split in between:
                split(v)
            v.wait_ge(S("norm_root").sem, use + 1)
            S("v_step").on(v.reciprocal(rs[:], rs[:]))
            v.wait_ge(S("v_step").sem, S("v_step").n)

            def low(k):
                v.wait_ge(S("h_high").sem, use * KT + k + 1)
                S("h_ready").on(v.tensor_tensor(hT_r[:, k, :], out[:, k, :], F(high[:, k, :]), ALU.subtract))

            for k in range(KT):
                x = v.scalar_tensor_tensor(out[:, k, :], xT[:, k, :], g[:, k:k + 1], rs[:], ALU.mult, ALU.mult)
                S("h_full").on(x)
                if high is not None and k:
                    low(k - 1)
            if high is not None:
                low(KT - 1)

        def norm_high(act, use, high):
            for k in range(KT):
                act.wait_ge(S("h_full").sem, use * KT + k + 1)
                S("h_high").on(nc.scalar.activation(high[:, k, :], hT[:, k, :], ACT.Copy))

        with nc.Fori(0, DEPTH) as l:
            with nc.Block() as block:

                @block.sync
                def _(sp):
                    for dst, name in ((gmix, "norm_mix"), (gmlp, "norm_mlp"), (ggdn, "gdn_norm"), (convw, "conv_w")):
                        sp.dma_start(dst[:], A[name][l]).then_inc(S("params").sem, 16)
                    for dst, name in ((dtb, "dt_bias"), (alog, "a_log")):
                        sp.dma_start(dst[:], A[name][l].partition_broadcast(P)).then_inc(S("params").sem, 16)
                    chunks = front_chunks(l)

                    def load(c):
                        if c >= NSLOT:
                            sp.wait_ge(*used(c - NSLOT))
                        for dst, src in chunks[c]:
                            sp.dma_start(dst, src).then_inc(ld[c % NSLOT].sem, 16)

                    load(0)
                    sp.dma_start(xs[:, :, :, 0:3], A["state_conv"][l]).then_inc(S("conv_state_in").sem, 16)
                    for c in range(1, NSLOT):
                        load(c)
                    sp.dma_start(O["win_past"][l], A["state_win"][l][:, NT:PAST]).then_inc(S("window_kept").sem, 16)
                    for c in range(NSLOT, 12):
                        load(c)
                    sp.wait_ge(*used(8))
                    sp.dma_start(Ss, A["state_gdn"][l]).then_inc(S("states_in").sem, 16)
                    sp.wait_ge(S("tail_out").sem, 13)
                    sp.dma_start(O["conv_T"][l], ctail[:]).then_inc(S("gdn_stored").sem, 16)
                    sp.wait_ge(S("state").sem, 2 * TT + 1)
                    sp.dma_start(O["gdn_p"][l], St[:]).then_inc(S("gdn_stored").sem, 16)
                    sp.wait_ge(S("sdS_out").sem, 4)
                    sp.dma_start(O["gdn_s"][l], Ss).then_inc(S("gdn_stored").sem, 16)
                    sp.wait_ge(S("gdn_stored").sem, 48)
                    load(12)
                    sp.wait_ge(S("gdn_mixed").sem, 4)
                    load(13)
                    for s, name in enumerate(("cmp_pe_k", "cmp_pe_v")):
                        for g in range(KVH):
                            sp.dma_start(pe[HD * g:HD * (g + 1), s, :], A[name][l]).then_inc(S("pe_in").sem, 16)
                    sp.wait_ge(setup, 48)
                    for b in range(NB):
                        for pg in range(2):
                            i = 2 * b + pg
                            phys = sp.value_load(pages[0:1, i:i + 1], min_val=0, max_val=N_POOL - 1)
                            page = A["cache_kv"][l, bass.ds(phys, 1)]
                            for g in range(KVH):
                                src = page[0, g]
                                cc = slice(HD * g, HD * (g + 1))
                                sp.dma_start(rows[:, :, 0, b, pg, cc], src[:, 2:4, :]).then_inc(S("pages_in").sem, 16)
                                sp.dma_start(cmp_rows[:, b, pg, :, cc], src[:, 0:2, :]).then_inc(S("pages_in").sem, 16)
                    load(14)
                    load(15)
                    sp.wait_ge(S("rope_done").sem, len(ROPED))
                    sp.dma_start(O["rows_T"][l], nsaT[:, 4:10, :]).then_inc(S("rows_stored").sem, 16)
                    sp.wait_ge(S("cmp").sem, 2)
                    for c in range(16, FRONT):
                        load(c)
                    with sp.Fori(0, NGROUP) as m:
                        up = A["w_up"][l].rearrange("(k p) n -> p k n", p=P)
                        down = A["w_down"][l].rearrange("(m k p) n -> m p k n", p=P, k=8)[m]
                        for c in range(8):
                            if c < 4:
                                sp.wait_ge(S("res").sem, m * 8 + 2 * (c + 1))
                                src = up[:, :, bass.ds(m * GROUP + c * SLOT, SLOT)]
                            else:
                                sp.wait_ge(S("up").sem, m * 8 + 2 * (c - 3))
                                src = down[:, :, (c - 4) * SLOT:(c - 3) * SLOT]
                            sp.dma_start(wslot(c), src).then_inc(ld[c % NSLOT].sem, 16)
                    sp.wait_ge(S("window_kept").sem, 16)
                    sp.wait_ge(S("rows_stored").sem, 16)

                @block.tensor
                def _(t):
                    def mm(out, lhsT, rhs, start=True, stop=True):
                        return t.matmul(out, lhsT, rhs, start=start, stop=stop, skip_group_check=True)

                    def dense(pair, w_high, w_low, x_high, x_low, M=P, ready=None):
                        for k in range(KT):
                            if ready:
                                t.wait_ge(*ready(k))
                            for i, (w, src) in enumerate(((w_high, x_high), (w_high, x_low), (w_low, x_high))):
                                for h in range(2):
                                    x = mm(ps[0:M, 2 * pair + h, 0:HALF], w[:, k, :],
                                           src[:, k, HALF * h:HALF * (h + 1)],
                                           start=(k == 0 and i == 0), stop=(k == KT - 1 and i == 2))
                        return x

                    t.wait_ge(setup, 48)
                    norm_tensor(t, 0, lambda k: sq[:, k % 4, :])

                    def project(n):
                        c, col, M = tiles[n]
                        t.wait_ge(S("w_low").sem, n + 1)
                        if n >= 4:
                            t.wait_ge(S("proj_out").sem, n - 3)
                        S("proj").on(dense(n % 4, high(n)[0][:, :, 0:M], wslot(c, wring_r)[:, :, col:col + M], h_hi, hT_r, M,
                                           ready=(lambda k: (S("h_ready").sem, k + 1)) if n == 0 else None))

                    for n in range(N_GDN):
                        project(n)

                    def head_sum(i, pair, src):
                        for h in range(2):
                            x = mm(ps[32 * i:32 * i + 32, 2 * pair + h, 0:HALF], C("headsum"),
                                   src[:, HALF * h:HALF * (h + 1)])
                        return x

                    def head_spread(i, pair, src):
                        r = slice(32 * i, 32 * i + 32)
                        at, n = CONSTS["headspread"]
                        for h in range(2):
                            x = mm(ps[:, 2 * pair + h, 0:HALF], cst[r, at:at + n], src[r, HALF * h:HALF * (h + 1)])
                        return x

                    for n in range(8):
                        t.wait_ge(S("l2_square").sem, n + 1)
                        t.wait_ge(S("proj_out").sem, N_GDN)
                        S("l2_sum").on(head_sum(n % 4, n // 4, sq[:, n % 4, :]))

                    for q in range(TT + 1):
                        n = tile_len(q)
                        x = t.transpose(ps[0:n, 7, SMALLW * q:SMALLW * (q + 1)],
                                        rs[0:SMALLW, P * q:P * q + n], C("ident", SMALLW, SMALLW))
                    S("decay_tensor").on(x)

                    for n in range(8):
                        t.wait_ge(S("l2_inverse").sem, n // 4 + 1)
                        if n == 0:
                            t.wait_ge(S("l2_out").sem, 2)
                        if n >= 2:
                            t.wait_ge(S("l2_done").sem, n - 1)
                        S("l2_spread").on(head_spread(n % 4, 1 + n % 2, r_a[:, n // 4, :]))

                    t.wait_ge(S("decay_vector").sem, 2)
                    for j, m in enumerate(("cum", "seg")):
                        mm(ps[:, 6, 64 * j:64 * j + TT * NH], C(m + "p"),
                           gtok[:, 0:TT, :].rearrange("p a b -> p (a b)"))
                        x = mm(ps[0:NS, 6, 64 * j + TT * NH:64 * j + (TT + 1) * NH], C(m + "s", NS, NS),
                               gtok[0:NS, TT, :])
                    S("decay_tensor").on(x)
                    t.wait_ge(S("l2_done").sem, 8)
                    t.wait_ge(S("decay_vector").sem, 4)
                    for q in range(TT + 1):
                        n = tile_len(q)
                        for h in range(NH):
                            x = mm(ps[par(h), 2 + q, P * (h // 2):P * (h // 2) + n],
                                   gtok[0:n, q, h:h + 1].to_broadcast([n, HD]),
                                   C("cump" if q < TT else "cums", n, n))
                        S("gchan_sum").on(x)

                    def prepare(q):
                        n = tile_len(q)
                        if q == 0:
                            t.wait_ge(S("Eg_out").sem, TT + 1)
                            t.wait_ge(S("gates_act").sem, 7)
                            t.wait_ge(S("l2_done").sem, 8)
                        else:
                            t.wait_ge(S("u0_out").sem, 2 * q)
                            t.wait_ge(S("wT_out").sem, 2 * q)
                        for s in range(2):
                            for hp in range(4):
                                x = t.transpose(ps[0:n, 4 + 3 * s, P * hp:P * (hp + 1)], qkv[:, 4 + 4 * s + hp, cols(q)],
                                                C("ident"))
                        S("kv_turned").on(x)
                        for hf in range(2):
                            b0 = 2 + 3 * hf
                            for h in range(4):
                                hh = 4 * hf + h
                                for s in range(2):
                                    at = 2 * P * s + P * (h // 2)
                                    x = mm(ps[0:n, b0 + h % 2, at:at + n], qkv[par(hh), 4 + hh // 2, cols(q)],
                                           qkv[par(hh), 4 - 4 * s + hh // 2, cols(q)])
                            S("gram").on(x)
                            t.wait_ge(S("gU_ready").sem, 2 * q + hf + 1)
                            if hf == 0:
                                t.wait_ge(S("kb_out").sem, 2 * q + 2)
                            else:
                                t.wait_ge(S("v_out").sem, q + 1)
                            S("grow").on(mm(heads4(ps[0:n, b0 + 2, :], n), C("ones", n, n),
                                            prep["d"][0:n, hf, :, 0:n]))

                        def each(bank, lhsT, rhs, hf):
                            for h in range(4):
                                x = mm(ps[0:n, bank, P * h:P * h + n], prep[lhsT][0:n, hf, h, 0:n],
                                       prep[rhs][0:n, hf, h, 0:n])
                            return x

                        def turn(bank, name, hf):
                            for h in range(4):
                                x = t.transpose(ps[0:n, bank, P * h:P * h + n], prep[name][0:n, hf, h, 0:n],
                                                C("ident", n, n))
                            return x

                        if q:
                            scan_w(2 * q - 2)
                        for hf in range(2):
                            t.wait_ge(S("B_ready").sem, 2 * q + hf + 1)
                            S("A_turned").on(turn(2 + 3 * hf, "b", hf))
                        if q:
                            scan_state(2 * q - 2)
                        for hf in range(2):
                            t.wait_ge(S("D_ready").sem, 2 * q + hf + 1)
                            t.wait_ge(S("AD_ready").sem, 2 * q + hf + 1)
                            S("D2").on(each(3 + 3 * hf, "c", "d", hf))
                        if q:
                            scan_output(2 * q - 2)
                        for hf in range(2):
                            t.wait_ge(S("D2_out").sem, 2 * q + hf + 1)
                            S("D2T").on(turn(2 + 3 * hf, "f", hf))
                        if q:
                            scan_w(2 * q - 1)
                        for hf in range(2):
                            t.wait_ge(S("ID2T_out").sem, 2 * q + hf + 1)
                            S("P1").on(each(3 + 3 * hf, "c", "e", hf))
                            if q < TT:
                                S("D4").on(each(4 + 3 * hf, "b", "f", hf))
                        if q:
                            scan_state(2 * q - 1)
                        if q < TT:
                            for hf in range(2):
                                t.wait_ge(S("ID4_out").sem, 2 * q + hf + 1)
                                S("ID4T").on(turn(2 + 3 * hf, "f", hf))
                        if q:
                            scan_output(2 * q - 1)
                        if q < TT:
                            for hf in range(2):
                                t.wait_ge(S("ID4T_out").sem, 2 * q + hf + 1)
                                t.wait_ge(S("P1_out").sem, 2 * q + hf + 1)
                                S("Pn").on(each(3 + 3 * hf, "b", "d", hf))
                            for i, lev in enumerate(LEVELS):
                                cur = "ed"[i % 2]
                                for hf in range(2):
                                    t.wait_ge(S("Pn_out").sem, 2 * (4 * q + i) + hf + 1)
                                    t.wait_ge(S("M_ready").sem, 2 * (3 * q + i) + hf + 1)
                                    S("X").on(each(2 + 3 * hf, "c", cur, hf))
                                    S("PT").on(turn(4 + 3 * hf, cur, hf))
                                for hf in range(2):
                                    t.wait_ge(S("IX_out").sem, 2 * (3 * q + i) + hf + 1)
                                    t.wait_ge(S("PT_out").sem, 2 * (3 * q + i) + hf + 1)
                                    S("Pn").on(each(3 + 3 * hf, "b", "f", hf))
                        t.wait_ge(S("kb_out").sem, 2 * q + 2)
                        t.wait_ge(S("v_out").sem, q + 1)
                        for hf in range(2):
                            if q < TT:
                                t.wait_ge(S("Pn_out").sem, 2 * (4 * q + 3) + hf + 1)
                            else:
                                t.wait_ge(S("P1_out").sem, 2 * q + hf + 1)
                            for h in range(4):
                                hh = 4 * hf + h
                                mm(ps[0:n, 2 + 3 * hf, HD * h:HD * (h + 1)], prep["d"][0:n, hf, h, 0:n],
                                   vtok[0:n, hh, :])
                                x = mm(ps[par(hh), 4 + 3 * hf, P * (h // 2):P * (h // 2) + n],
                                       kb[0:n, hh, :], prep["d"][0:n, hf, h, 0:n])
                            S("wu").on(x)

                    def chunk(n):
                        return n // 2, slice(HD * (n % 2), HD * (n % 2) + HD)

                    def scan_w(n):
                        q, rows = chunk(n)
                        t.wait_ge(S("u0_out").sem, 2 * (q + 1))
                        t.wait_ge(S("wT_out").sem, 2 * (q + 1))
                        t.wait_ge(S("state").sem, n + 1)
                        if n:
                            t.wait_ge(S("oT_out").sem, n)
                        for h in range(NH):
                            x = mm(ps[rows, h % 2, HD * (h // 2):HD * (h // 2 + 1)], wqT[par(h), 0, h // 2, rows],
                                   St[par(h), h // 2, :])
                        S("wS").on(x)

                    def scan_state(n):
                        q, rows = chunk(n)
                        t.wait_ge(S("u_out").sem, n + 1)
                        t.wait_ge(S("qe_out").sem, q + 1)
                        for h in range(NH):
                            x = mm(ps[par(h), 0, HD * (h // 2):HD * (h // 2 + 1)], kdec[rows, q % 2, h, :], u[rows, h, :])
                        S("dS").on(x)
                        for h in range(NH):
                            x = mm(ps[par(h), 1, HD * (h // 2):HD * (h // 2 + 1)], St[par(h), h // 2, :],
                                   qkv[par(h), h // 2, HD * n:HD * (n + 1)])
                        S("oS").on(x)

                    def scan_output(n):
                        q, rows = chunk(n)
                        t.wait_ge(S("oS_out").sem, n + 1)
                        for h in range(NH):
                            x = mm(ps[par(h), 1, HD * (h // 2):HD * (h // 2 + 1)], u[rows, h, :], qkm[rows, q % 2, h, rows])
                        S("oU").on(x)

                    for q in range(TT + 1):
                        prepare(q)

                    t.wait_ge(S("u0_out").sem, 2 * (TT + 1))
                    t.wait_ge(S("wT_out").sem, 2 * (TT + 1))
                    t.wait_ge(S("qe_out").sem, TT + 1)
                    t.wait_ge(S("state").sem, 2 * TT + 1)
                    t.wait_ge(S("oT_out").sem, 2 * TT)
                    t.wait_ge(S("states_in").sem, 16)
                    for b in range(NB):
                        for h in range(NH):
                            out = ps[par(h), 0, 64 * (h // 2):64 * (h // 2 + 1)].rearrange("p (s i) -> p s i", s=2)
                            x = mm(out[:, :, NT * b:NT * (b + 1)], Ss[par(h), b, h // 2, :],
                                   wqT[par(h), :, h // 2, NT * b:NT * (b + 1)])
                    S("sample_mm").on(x)
                    t.wait_ge(S("sample_dve").sem, 1)
                    for hp in range(4):
                        x = t.transpose(ps[0:NS, 1, P * hp:P * (hp + 1)], xuT[:, hp, 0, :], C("ident"))
                    S("sample_mm").on(x)
                    t.wait_ge(S("sample_dve").sem, 2)
                    for h in range(NH):
                        x = mm(ps[par(h), 2, NS * (h // 2):NS * (h // 2 + 1)], u[0:NS, h, :], qkm[0:NS, TT % 2, h, 0:NS])
                    S("sample_mm").on(x)
                    for hp in range(4):
                        for h in (2 * hp, 2 * hp + 1):
                            t.wait_ge(S("um_odd" if h % 2 else "um_even").sem, h // 2 + 1)
                            x = mm(ps[par(h), 3 + hp, :], kdec[0:NS, TT % 2, h, :], um[:, h, :, :].rearrange("p b e -> p (b e)"))
                        S("sdS").on(x)

                    t.wait_ge(S("sdS_out").sem, 4)
                    for hp in range(4):
                        t.wait_ge(S("o_square").sem, hp + 1)
                        x = head_sum(hp, 0, osq[:, hp, :])
                    S("o_sum").on(x)
                    t.wait_ge(S("o_norm_vector").sem, 6)
                    for hp in range(4):
                        S("o_spread").on(head_spread(hp, (hp + 1) % 4, qkv[:, 8, :]))

                    t.wait_ge(S("gdn_mixed").sem, 4)
                    for n in range(N_GDN, N_TILES):
                        project(n)
                    t.wait_ge(S("proj_out").sem, N_TILES)
                    def rotate(i):
                        n = ROPED[i]
                        if i >= 3:
                            t.wait_ge(S("rope_sin").sem, i - 2)
                        for h in range(2):
                            x = mm(ps[:, 2 * (i % 3) + h, 0:HALF], C("rot"), nsaT[:, n, HALF * h:HALF * (h + 1)])
                        S("rot").on(x)

                    def turn_past(i):
                        b = i // 2
                        if i == 0:
                            t.wait_ge(S("window_in").sem, 32 * NB)
                            t.wait_ge(S("pages_in").sem, 16 * 64)
                        if i >= 2:
                            t.wait_ge(S("cpast_out" if i % 2 else "kpast_out").sem, i // 2)
                        if i % 2 == 0:
                            for pg in range(2):
                                t.transpose(ps[:, 6, P * pg:P * (pg + 1)], rows[:, 0, 0, b, pg, :], C("ident"))
                                x = t.transpose(ps[:, 6, P * (2 + pg):P * (3 + pg)], rows[:, 0, 1, b, pg, :], C("ident"))
                        else:
                            for s in range(2):
                                for pg in range(2):
                                    x = t.transpose(ps[:, 7, P * (2 * s + pg):P * (2 * s + pg + 1)],
                                                    cmp_rows[:, b, pg, s, :], C("ident"))
                        S("kpast_turned").on(x)

                    for i in range(len(ROPED)):
                        rotate(i)
                    for i in range(2 * NB):
                        turn_past(i)
                    t.wait_ge(S("kpast_out").sem, NB)
                    t.wait_ge(S("cpast_out").sem, NB)
                    t.wait_ge(S("rope_sin").sem, len(ROPED))
                    for s in range(2):
                        for q in range(TT):
                            x = t.transpose(ps[:, s, P * q:P * (q + 1)], nsaT[:, 7 + 2 * s, P * q:P * (q + 1)],
                                            C("ident"))
                        S("v_turned").on(x)
                    t.wait_ge(S("cmp_in_ready").sem, 4)
                    t.wait_ge(S("v_copied").sem, 2)
                    for s in range(2):
                        t.wait_ge(ld[(14 + s) % NSLOT].sem, landed(14 + s))
                        w = wring[:, (14 + s) % NSLOT, :].rearrange("p (c e) -> p c e", c=CMP)
                        for g in range(KVH):
                            r = slice(HD * g, HD * (g + 1))
                            for c in range(CMP):
                                x = mm(ps[r, s, 0:NCA + 1], w[r, c, :],
                                       cmp_in[s][r, :].rearrange("p (n c) -> p n c", c=CMP)[:, :, c],
                                       start=(c == 0), stop=(c == CMP - 1))
                        S("cmp").on(x)
                    t.wait_ge(S("ck_out").sem, 2)
                    S("ck_rot").on(mm(ps[:, 2, 0:NCA], C("rot"), ckT[:, 0, 0:NCA]))
                    t.wait_ge(S("compressed_pool").sem, 3)
                    t.transpose(ps[:, 3, 0:P], cvrep, C("ident"))
                    t.wait_ge(S("vsrc_ready").sem, 3)
                    for b in range(NB):
                        x = t.transpose(ps[0:SHORT, 4 + b // 4, P * (b % 4):P * (b % 4 + 1)], vsrc[:, b, :], C("ident"))
                    S("cv_turned").on(x)

                    t.wait_ge(S("compressed_vector").sem, 1)
                    t.wait_ge(S("rope_done").sem, len(ROPED))
                    for q in range(TT):
                        for j in range(GQA):
                            at = KVH * NCP * (GQA * q + j)
                            x = mm(ps[:, 6, at:at + KVH * NCP], nsaT[:, j, P * q:P * (q + 1)],
                                   ckz.rearrange("p g n -> p (g n)"))
                    S("compressed_tensor").on(x)

                    def scores(uu):
                        q, h = divmod(uu, NH)
                        if uu == 0:
                            t.wait_ge(S("cv_out").sem, 1)
                            t.wait_ge(S("kz_ready").sem, 4)
                            t.wait_ge(S("compressed_vector").sem, 2)
                        if uu >= 2:
                            t.wait_ge(S("p_exp").sem, 2 * (uu - 1))
                        for s in range(2):
                            x = mm(ps[:, 2 * (uu % 2) + s, 0:P * (q + 1)], nsaT[:, h % GQA, P * q:P * (q + 1)],
                                   kz[:, s, h // GQA, 0:P * (q + 1)])
                        S("score").on(x)

                    def turn(uu):
                        q, h = divmod(uu, NH)
                        if h == 1 and q:
                            t.wait_ge(S("o_out").sem, q)
                        for s in range(2):
                            t.wait_ge(S("p_exp").sem, 2 * uu + s + 1)
                            if uu:
                                t.wait_ge(S(f"pT_out{s}").sem, uu)
                            for kt in range(q + 1):
                                x = t.transpose(ps[:, 4 + s, P * kt:P * (kt + 1)],
                                                att[:, uu % 2, s, P * kt:P * (kt + 1)], C("ident"))
                            S("pT").on(x)

                    def values_of(uu):
                        q, h = divmod(uu, NH)
                        g = h // GQA
                        if uu == 0:
                            t.wait_ge(S("compressed_scalar").sem, 2)
                            t.wait_ge(S("compressed_vector").sem, 2)
                        if uu >= 2:
                            t.wait_ge(S("o_scaled").sem, uu - 1)
                        out = ps[:, 6 + uu % 2, :]
                        for s in range(2):
                            t.wait_ge(S(f"pT_out{s}").sem, uu + 1)
                            for kt in range(q + 1):
                                mm(out[:, HD * s:HD * (s + 1)], attT[:, s, P * kt:P * (kt + 1)],
                                   vtp[:, s, kt, HD * g:HD * (g + 1)], start=(kt == 0), stop=(kt == q))
                        S("nsa").on(mm(out[:, 2 * HD:3 * HD], pcT[:, q, :], cvb[:, h, :]))

                    def outputs(q):
                        t.wait_ge(S("o_added").sem, NH * (q + 1))
                        t.wait_ge(S("pT_out0").sem, min(NH * (q + 1) + 1, UNITS))
                        for j in range(GQA):
                            x = t.transpose(ps[:, 4, P * j:P * (j + 1)],
                                            osum[:, q % 2, j, :, :].rearrange("p g d -> p (g d)"), C("ident"))
                        S("o_turned").on(x)

                    for what, i in SCHEDULE[:2]:
                        scores(i)
                    t.wait_ge(S("compressed_vector").sem, 4)
                    for q in range(TT):
                        x = t.transpose(ps[:, 7, P * q:P * (q + 1)], pc[:, q].rearrange("p h n -> p (h n)"), C("ident"))
                    S("compressed_tensor").on(x)
                    for what, i in SCHEDULE[2:]:
                        {"s": scores, "t": turn, "v": values_of, "o": outputs}[what](i)
                    t.wait_ge(S("o_out").sem, TT)
                    t.wait_ge(S("o_scaled").sem, UNITS)

                    t.wait_ge(S("qs_ready").sem, 3)
                    t.wait_ge(S("knew_out").sem, 2)
                    for g in range(2):
                        for b4 in range(4):
                            b = 4 * g + b4
                            q32 = qs[:, b, :, :, :].rearrange("p a b c -> p (a b c)")
                            r = slice(32 * b4, 32 * b4 + 32)
                            mm(ps[r, 2 * g, 0:PAST + NT], q32, kselT[:, b, :])
                            mm(ps[r, 2 * g, PAST + NT:PAST + NT + NCS], q32, ckr[:, NCP + NCS * b:NCP + NCS * (b + 1)])
                            mm(ps[r, 2 * g + 1, 0:PAST + NT], q32, kwinT[:, b, :])
                        S("ss").on(mm(ps[:, 2 * g, 320:320 + 3 * NH], C("pick" + str(g), NS), sig[0:NS, TT, NH:4 * NH]))
                    for g in range(2):
                        t.wait_ge(S("sp_ready").sem, g + 1)
                        for i, at in enumerate((0, P, PAST + SHORT, PAST + SHORT + P)):
                            t.transpose(ps[:, 4 + g, P * i:P * (i + 1)], satt[:, g, at:at + P], C("ident"))
                        if g:
                            t.wait_ge(S("spT_out").sem, 2)
                        S("spT").on(t.transpose(ps[0:SHORT, 6, P * g:P * (g + 1)], satt[:, g, PAST:PAST + SHORT],
                                                C("ident")))
                    for g in range(2):
                        t.wait_ge(S("spT_out").sem, 2 * (g + 1))
                        for b4 in range(4):
                            b = 4 * g + b4
                            out = ps[:, 7, 32 * b:32 * b + 32]
                            mm(out, vshort[:, b, :], pcT[0:SHORT, g, 32 * b4:32 * b4 + 32], stop=False)
                            for i in range(4):
                                x = mm(out, rows[:, 1, i // 2, b, i % 2, :],
                                       attT[:, g, P * i + 32 * b4:P * i + 32 * b4 + 32], start=False, stop=(i == 3))
                        S("so_att").on(x)

                    for d in range(KT):
                        n = N_TILES + d
                        c, col, _ = tiles[n]
                        t.wait_ge(S("w_low").sem, n + 1)
                        if d >= 3:
                            t.wait_ge(S("res_added").sem, d - 2)
                        S("res").on(dense(d % 3, high(n)[0], wslot(c, wring_r)[:, :, col:col + P], mix_hi, mixT_r,
                                          ready=(lambda k: (S("mix_low").sem, k + 1)) if d == 0 else None))
                        if d >= 2:
                            norm_sum(t, 1, lambda k: uT[:, k, :], d - 2)
                    norm_sum(t, 1, lambda k: uT[:, k, :], KT - 2)
                    norm_sum(t, 1, lambda k: uT[:, k, :], KT - 1)


                    def mlp_group(m):
                        for i in range(16):
                            c, col = i // 2, P * (i % 2)
                            t.wait_ge(S("w_low").sem, m * 16 + (N_FRONT + i + 1))
                            if i < 4:
                                t.wait_ge(S("res_added").sem, m * 8 + (5 + i))
                            elif i < 12:
                                t.wait_ge(S("relu_done").sem, m * 8 + (i - 3))
                            else:
                                t.wait_ge(S("res_added").sem, m * 8 + (8 + i - 11))
                            up, first = i < 8, i in (0, 8)
                            ready = (lambda k: (S("h_ready").sem, KT + k + 1)) if up else (
                                lambda k: (S("u_ready").sem, m * 8 + (k + 1)))
                            x = dense(i % 4, w_hi_mlp[i % 4], wslot(c, wring_r)[:, :, col:col + P], mix_hi if up else u_hi,
                                      hT_r if up else uT_r, ready=ready if first else None)
                            x.then_inc(S("up" if up else "res").sem, 1)

                    with t.Fori(0, NGROUP - 1) as m:
                        mlp_group(m)
                    mlp_group(NGROUP - 1)

                @block.scalar
                def _(act):
                    A1 = nc.scalar.activation
                    norm_scalar(act, 0, lambda k: sq[:, k % 4, :], 4,
                                [lambda e, n=n: split_high(e, n) for n in range(AHEAD)])
                    norm_high(act, 0, h_hi)
                    act.wait_ge(S("params").sem, 16 * 6)

                    def out_of(n, rows=P):
                        if n + AHEAD < N_GDN or N_GDN <= n < N_TILES - AHEAD:
                            split_high(act, n + AHEAD)
                        act.wait_ge(S("proj").sem, n + 1)
                        return whole(n % 4, rows)

                    for n in range(12):
                        src = out_of(n)
                        if n >= 3:
                            act.wait_ge(S("conv_done").sem, n - 2)
                            act.wait_ge(S("tail_out").sem, n - 2)
                        S("pre_out").on(A1(halves(pre[:, n % 3, :]), src, ACT.Copy))
                        S("proj_out").on(A1(halves(qkv[:, n, :]), src, ACT.Copy, scale=convw[:, n, CONV - 1:CONV]))
                    def z_out(n):
                        S("proj_out").on(A1(halves(zT[:, n - 12, :]), out_of(n), ACT.Silu))

                    z_out(12)
                    z_out(13)
                    act.wait_ge(S("conv_done").sem, 12)
                    act.wait_ge(S("sconv_done").sem, 1)
                    for n in range(12):
                        S("silu").on(A1(qkv[:, n, :], qkv[:, n, :], ACT.Silu))
                        if n in (3, 7):
                            z_out(14 + n // 4)
                    act.wait_ge(S("h_ready").sem, KT)
                    S("proj_out").on(A1(halves(rs[0:SMALLW, :]), out_of(16, SMALLW), ACT.Copy))

                    def l2_square(n):
                        if n >= 4:
                            act.wait_ge(S("l2_sum").sem, n - 3)
                        act.wait_ge(S("silu").sem, n + 1)
                        S("l2_square").on(A1(sq[:, n % 4, :], qkv[:, n, :], ACT.Square))

                    for n in range(4):
                        l2_square(n)
                    for n in range(4, 8):
                        l2_square(n)
                    for i in range(2):
                        act.wait_ge(S("l2_out").sem, i + 1)
                        S("l2_root").on(A1(r_a[:, i, :], r_a[:, i, :], ACT.Sqrt))

                    act.wait_ge(S("decay_tensor").sem, 1)
                    act.wait_ge(S("zeroed").sem, 4)
                    W4 = TT * SMALLW
                    A1(tok_small[:, 0:TT, :].rearrange("p a b -> p (a b)"), ps[:, 7, 0:W4], ACT.Copy)
                    S("gates_act").on(A1(tok_small[0:NS, TT, :], ps[0:NS, 7, W4:W4 + SMALLW], ACT.Copy))
                    S("gates_act").on(A1(alog[:], alog[:], ACT.Exp))
                    act.wait_ge(S("gates_act").sem, 1)
                    S("gates_act").on(A1(sig[:], tok_small[:, :, NH:SMALLW], ACT.Exp, scale=-1.0))
                    act.wait_ge(S("decay_vector").sem, 1)
                    S("gates_act").on(A1(gt3[:], gt3[:], ACT.Exp, scale=-1.0))
                    act.wait_ge(S("gates_act").sem, 4)
                    S("gates_act").on(A1(gt3[:], gt3[:], ACT.Ln, bias=1.0))
                    act.wait_ge(S("decay_vector").sem, 3)
                    S("gates_act").on(A1(egc[:], gcum[:], ACT.Exp))
                    act.wait_ge(S("decay_vector").sem, 4)
                    S("gates_act").on(A1(edec[:], edec[:], ACT.Exp))
                    for q in range(TT + 1):
                        n = tile_len(q)
                        act.wait_ge(S("gchan_sum").sem, q + 1)
                        S("Eg_out").on(A1(Eg[:, :, cols(q)], heads4(ps[:, 2 + q, :], n), ACT.Exp))

                    def prepare(q):
                        n = tile_len(q)

                        def out(sem, name, hf, bank, wait):
                            act.wait_ge(S(wait).sem, S(sem).n + 1)
                            S(sem).on(A1(prep[name][0:n, hf, :, 0:n], heads4(ps[0:n, bank, :], n), ACT.Copy))

                        act.wait_ge(S("kv_turned").sem, q + 1)
                        S("v_out").on(A1(vtok[0:n].rearrange("p h d -> p (h d)"), ps[0:n, 7, :], ACT.Copy))
                        for hf in range(2):
                            act.wait_ge(S("G_masked").sem, 2 * q + hf + 1)
                            S("E_ready").on(A1(prep["a"][0:n, hf, :, 0:n], prep["a"][0:n, hf, :, 0:n], ACT.Exp))
                        for hf in range(2):
                            out("A_out", "a", hf, 2 + 3 * hf, "A_turned")
                        if q:
                            scan_out(2 * q - 2)
                        for hf in range(2):
                            out("D2_out", "f", hf, 3 + 3 * hf, "D2")
                        for hf in range(2):
                            out("D2T_out", "b", hf, 2 + 3 * hf, "D2T")
                        if q:
                            scan_out(2 * q - 1)
                        if q < TT:
                            for hf in range(2):
                                out("ID4T_out", "b", hf, 2 + 3 * hf, "ID4T")
                            for i in range(3):
                                for hf in range(2):
                                    out("PT_out", "b", hf, 4 + 3 * hf, "PT")
                        for hf in range(2):
                            act.wait_ge(S("wu").sem, 2 * q + hf + 1)
                            S("wT_out").on(A1(wqT[:, 0, 2 * hf:2 * hf + 2, 0:n],
                                              ps[:, 4 + 3 * hf, 0:2 * P].rearrange("p (a i) -> p a i", a=2)[:, :, 0:n],
                                              ACT.Copy))

                    def scan_out(n):
                        act.wait_ge(S("oS").sem, n + 1)
                        S("oS_out").on(A1(mixT[:, 0:4, HD * n:HD * (n + 1)],
                                          ps[:, 1, 0:4 * HD].rearrange("p (a i) -> p a i", a=4), ACT.Copy))

                    for q in range(TT + 1):
                        prepare(q)

                    act.wait_ge(S("sample_dve").sem, 3)
                    act.wait_ge(S("sadd_out").sem, 4)
                    act.wait_ge(S("oT_out").sem, 2 * TT)
                    for hp in range(4):
                        S("o_square").on(A1(osq[:, hp, :], mixT[:, hp, :], ACT.Square))
                    act.wait_ge(S("o_norm_vector").sem, 1)
                    S("o_root").on(A1(qkv[:, 8, :], qkv[:, 8, :], ACT.Sqrt))

                    act.wait_ge(S("gdn_stored").sem, 48)
                    for n in range(N_GDN, N_GDN + AHEAD):
                        split_high(act, n)
                    act.wait_ge(S("gdn_mixed").sem, 4)
                    win = A["state_win"][l].rearrange("b (g p) s h d -> p b g (s h d)", p=P)
                    for b in range(NB):
                        for kv in range(2):
                            act.dma_start(rows[:, kv, 1, b], win[:, b][:, :, P * kv:P * (kv + 1)]).then_inc(
                                S("window_in").sem, 16)
                    for n in range(N_GDN, N_TILES):
                        S("proj_out").on(A1(halves(nsaT[:, n - N_GDN, :]), out_of(n), ACT.Copy))
                    for i in range(1, 2 * NB, 2):
                        act.wait_ge(S("kpast_turned").sem, i + 1)
                        for s in range(2):
                            x = A1(cmp_in[s][:, SEQ + PAST * (i // 2):SEQ + PAST * (i // 2 + 1)],
                                   ps[:, 7, PAST * s:PAST * (s + 1)], ACT.Copy)
                        S("cpast_out").on(x)
                    for s in range(2):
                        act.wait_ge(S("v_turned").sem, s + 1)
                        S("v_copied").on(A1(vtp[:, s].rearrange("p a b -> p (a b)"), ps[:, s, :], ACT.Copy))
                    act.wait_ge(S("cv_turned").sem, 1)
                    S("cv_out").on(A1(vshort.rearrange("p (a b) e -> p a (b e)", a=2), ps[0:SHORT, 4:6, :], ACT.Copy))
                    act.wait_ge(S("compressed_pool").sem, 1)
                    act.wait_ge(S("rope_done").sem, len(ROPED))
                    for s in range(2):
                        for g in range(KVH):
                            r = slice(HD * g, HD * (g + 1))
                            S("kz_ready").on(A1(kz[r, s, g, :], nsaT[r, 6 + 2 * s, 0:SEQ], ACT.Copy))
                    act.wait_ge(S("compressed_vector").sem, 3)
                    S("compressed_scalar").on(A1(pc, pc, ACT.Exp, scale=SCALE))

                    def softmax(uu):
                        q, n, z = uu // NH, P * (uu // NH + 1), uu % 2
                        act.wait_ge(S("p_max").sem, uu + 1)
                        if uu >= 2:
                            act.wait_ge(S("pT").sem, 2 * (uu - 1))
                            act.wait_ge(S("r_ready").sem, uu - 1)
                        for s in range(2):
                            S("p_exp").on(A1(att[:, z, s, 0:n], ps[:, 2 * z + s, 0:n], ACT.Exp,
                                             bias=stat[:, 8 * z + 2 + s:8 * z + 3 + s], scale=SCALE,
                                             accum_out=stat[:, 8 * z + 4 + s:8 * z + 5 + s]))

                    def turned(uu):
                        n = P * (uu // NH + 1)
                        act.wait_ge(S("pT").sem, 2 * uu + 1)
                        if uu:
                            act.wait_ge(S("nsa").sem, uu)
                        S("pT_out0").on(A1(attT[:, 0, 0:n], ps[:, 4, 0:n], ACT.Copy))

                    def outputs(q):
                        act.wait_ge(S("o_turned").sem, q + 1)
                        S("o_out").on(A1(mixT[:, 4:8, cols(q)], heads4(ps[:, 4, :], P), ACT.Copy))

                    for what, i in SCHEDULE[:2]:
                        softmax(i)
                    act.wait_ge(S("compressed_tensor").sem, 2)
                    S("compressed_scalar").on(A1(pcT.rearrange("p q n -> p (q n)"), ps[:, 7, :], ACT.Copy))
                    for what, i in SCHEDULE[2:]:
                        if what != "v":
                            {"s": softmax, "t": turned, "o": outputs}[what](i)

                    for g in range(2):
                        act.wait_ge(S("s_max").sem, g + 1)
                        n = PAST + NT
                        for i, (out, src) in enumerate((
                                (satt[:, g, n:n + NCS], ps[:, 2 * g, n:n + NCS]),
                                (satt[:, g, 0:n], ps[:, 2 * g, 0:n]),
                                (satt[:, g, n + NCS:SROW], ps[:, 2 * g + 1, 0:n]))):
                            x = A1(out, src, ACT.Exp, bias=sstat[:, g, 3 + i:4 + i], scale=SCALE,
                                   accum_out=sstat[:, g, 6 + i:7 + i])
                        S("s_exp").on(x)
                    for g in range(2):
                        act.wait_ge(S("spT").sem, g + 1)
                        S("spT_out").on(A1(attT[:, g, :], ps[:, 4 + g, :], ACT.Copy))
                        S("spT_out").on(A1(pcT[0:SHORT, g, :], ps[0:SHORT, 6, P * g:P * (g + 1)], ACT.Copy))

                    act.wait_ge(S("rows_stored").sem, 16)
                    for n in range(N_TILES, N_TILES + AHEAD):
                        split_high(act, n)
                    for k in range(KT):
                        if k == 4:
                            act.wait_ge(S("nsa_mixed").sem, 2)
                        S("mix_high").on(A1(mix_hi[:, k, :], mixT[:, k, :], ACT.Copy))
                    for n in range(N_TILES + AHEAD, N_TILES + AHEAD + 2):
                        split_high(act, n)

                    norm_scalar(act, 1, lambda k: uT[:, k, :], KT,
                                [lambda e, i=i: mlp_split_high(e, 0, i) for i in range(AHEAD)])
                    norm_high(act, 1, mix_hi)

                    def mlp_group(m, last):
                        for i in range(16):
                            mlp_split_ahead(mlp_split_high, act, m, i, last)
                            if i < 8:
                                act.wait_ge(S("up").sem, m * 8 + (i + 1))
                                A1(halves(uT[:, i, :]), whole(i % 4), ACT.Relu).then_inc(S("relu_done").sem, 1)
                            if 1 <= i < 9:
                                act.wait_ge(S("u_square").sem, m * 8 + i)
                                A1(u_hi[:, i - 1, :], uT[:, i - 1, :], ACT.Copy).then_inc(S("u_high").sem, 1)

                    with act.Fori(0, NGROUP - 1) as m:
                        mlp_group(m, False)
                    mlp_group(NGROUP - 1, True)

                @block.vector
                def _(v):
                    def done(sem, instruction):
                        S(sem).on(instruction)
                        v.wait_ge(S(sem).sem, S(sem).n)

                    S("zeroed").on(v.memset(tok_small[:], 0.0))
                    S("zeroed").on(v.memset(gcum[:], 0.0))
                    S("zeroed").on(v.memset(edec[:], 0.0))
                    S("zeroed").on(v.memset(gt2[:], 0.0))
                    S("state").on(v.memset(St[:], 0.0))
                    v.wait_ge(S("params").sem, 16 * 6)
                    norm_vector(v, 0, gmix, hT, h_hi, [lambda e, n=n: split_low(e, n) for n in range(AHEAD)])

                    for n in range(12):
                        split_low(v, n + AHEAD)
                        v.wait_ge(S("pre_out").sem, n + 1)
                        v.wait_ge(S("proj_out").sem, n + 1)
                        for s in range(1, CONV):
                            x = v.scalar_tensor_tensor(qkv[:, n, s:SEQ], pre[:, n % 3, 0:SEQ - s],
                                                       convw[:, n, CONV - 1 - s:CONV - s], qkv[:, n, s:SEQ],
                                                       ALU.mult, ALU.add)
                            done("v_step" if s < CONV - 1 else "conv_done", x)

                    for n in range(12 + AHEAD, N_GDN):
                        split_low(v, n)

                    for i in range(2):
                        v.wait_ge(S("l2_sum").sem, 4 * (i + 1))
                        S("l2_out").on(v.tensor_scalar(halves(r_a[:, i, :]), whole(i), EPS, None, ALU.add))
                    for i in range(2):
                        v.wait_ge(S("l2_root").sem, i + 1)
                        S("l2_inverse").on(v.reciprocal(r_a[:, i, :], r_a[:, i, :]))

                    v.wait_ge(S("gates_act").sem, 1)
                    done("v_step", v.tensor_tensor(gt2[:], tok_small[:, :, 0:NH], mid(dtb[:], TT + 1), ALU.add))
                    done("v_step", v.tensor_scalar(gt3[:], gt2[:], -1.0, None, ALU.mult))
                    done("decay_vector", v.tensor_tensor(gt3[:], gt3[:], gt2[:], ALU.max))
                    for n in range(8):
                        v.wait_ge(S("l2_spread").sem, n + 1)
                        S("l2_done").on(v.scalar_tensor_tensor(halves(qkv[:, n, :]), halves(qkv[:, n, :]),
                                                               SCALE if n < 4 else 1.0, whole(1 + n % 2),
                                                               ALU.mult, ALU.mult))
                    v.wait_ge(S("gates_act").sem, 3)
                    done("v_step", v.tensor_scalar(sig[:], sig[:], 1.0, None, ALU.add))
                    done("v_step", v.reciprocal(sig[:], sig[:]))
                    v.wait_ge(S("gates_act").sem, 5)
                    done("v_step", v.scalar_tensor_tensor(gt2[:], gt2[:], 0.0, gt3[:], ALU.max, ALU.add))
                    v.wait_ge(S("gates_act").sem, 2)
                    done("v_step", v.tensor_tensor(gtok[:], gt2[:], mid(alog[:], TT + 1), ALU.mult))
                    done("decay_vector", v.tensor_scalar(gtok[:], gtok[:], -1.0, None, ALU.mult))
                    v.wait_ge(S("decay_tensor").sem, 2)
                    NG = TT * NH

                    def flat(ap):
                        return ap.rearrange("p a b -> p (a b)")

                    v.tensor_copy(flat(gcum[:, 0:TT, :]), ps[:, 6, 0:NG])
                    done("decay_vector", v.tensor_copy(gcum[0:NS, TT, :], ps[0:NS, 6, NG:NG + NH]))
                    v.tensor_tensor(flat(edec[:, 0:TT, :]), ps[:, 6, 64:64 + NG], flat(gcum[:, 0:TT, :]), ALU.subtract)
                    done("decay_vector", v.tensor_tensor(edec[0:NS, TT, :], ps[0:NS, 6, 64 + NG:64 + NG + NH],
                                                  gcum[0:NS, TT, :], ALU.subtract))

                    def prepare(q):
                        n = tile_len(q)

                        def pr(name, hf):
                            return prep[name][0:n, hf, :, 0:n]

                        def bank(b):
                            return heads4(ps[0:n, b, :], n)

                        v.wait_ge(S("kv_turned").sem, q + 1)
                        v.wait_ge(S("gates_act").sem, 7)
                        k_ps = ps[0:n, 4, :].rearrange("p (h d) -> p h d", h=NH)
                        S("kb_out").on(v.tensor_tensor(kb[0:n], k_ps, bc(egc[0:n, q, :], HD), ALU.mult))
                        S("kb_out").on(v.tensor_tensor(kdec[0:n, q % 2], k_ps, bc(edec[0:n, q, :], HD), ALU.mult))
                        for hf in range(2):
                            v.wait_ge(S("grow").sem, 2 * q + hf + 1)
                            S("G_diff").on(v.tensor_tensor(pr("a", hf), bank(4 + 3 * hf),
                                                           bc(gcum[0:n, q, 4 * hf:4 * hf + 4], n), ALU.subtract))
                        if q:
                            scan_u(2 * q - 2)
                        for hf in range(2):
                            v.wait_ge(S("E_ready").sem, 2 * q + hf + 1)
                            b0 = 2 + 3 * hf

                            def gram(s):
                                return ps[0:n, b0:b0 + 2, 2 * P * s:2 * P * (s + 1)].rearrange(
                                    "p b (a i) -> p a b i", a=2)[:, :, :, 0:n]

                            def pairs(ap):
                                return ap.rearrange("p (a b) i -> p a b i", b=2)

                            v.tensor_tensor(pairs(qkm[0:n, q % 2, 4 * hf:4 * hf + 4, 0:n]), gram(1), pairs(pr("a", hf)), ALU.mult)
                            S("GE_out").on(v.tensor_tensor(pairs(pr("b", hf)), gram(0), pairs(pr("a", hf)), ALU.mult))
                        for hf in range(2):
                            v.wait_ge(S("B_ready").sem, 2 * q + hf + 1)
                            done("v_step", v.tensor_tensor(pr("d", hf), pr("b", hf), mid(C("upper", n, n), 4), ALU.mult))
                            S("D_ready").on(v.tensor_tensor(pr("e", hf), mid(C("ident", n, n), 4), pr("d", hf),
                                                            ALU.subtract))
                        if q:
                            scan_state(2 * q - 2)
                            scan_output(2 * q - 2)
                            scan_u(2 * q - 1)
                        for hf in range(2):
                            v.wait_ge(S("P1").sem, 2 * q + hf + 1)
                            v.wait_ge(S("D_ready").sem, 2 * q + 2)
                            S("P1_out").on(v.tensor_copy(pr("d", hf), bank(3 + 3 * hf)))
                            if q < TT:
                                v.wait_ge(S("D4").sem, 2 * q + hf + 1)
                                S("ID4_out").on(v.tensor_tensor(pr("f", hf), bank(4 + 3 * hf),
                                                                mid(C("ident", n, n), 4), ALU.add))
                        if q:
                            scan_state(2 * q - 1)
                        if q < TT:
                            for hf in range(2):
                                v.wait_ge(S("Pn").sem, 2 * 4 * q + hf + 1)
                                S("Pn_out").on(v.tensor_copy(pr("e", hf), bank(3 + 3 * hf)))
                        if q:
                            scan_output(2 * q - 1)
                        if q < TT:
                            for i in range(3):
                                for hf in range(2):
                                    v.wait_ge(S("X").sem, 2 * (3 * q + i) + hf + 1)
                                    S("IX_out").on(v.tensor_tensor(pr("f", hf), mid(C("ident", n, n), 4),
                                                                   bank(2 + 3 * hf), ALU.subtract))
                                for hf in range(2):
                                    v.wait_ge(S("Pn").sem, 2 * (4 * q + 1 + i) + hf + 1)
                                    S("Pn_out").on(v.tensor_copy(pr("de"[i % 2], hf), bank(3 + 3 * hf)))
                        for hf in range(2):
                            v.wait_ge(S("wu").sem, 2 * q + hf + 1)
                            S("u0_out").on(v.tensor_copy(u0[0:n, 4 * hf:4 * hf + 4, :],
                                                         ps[0:n, 2 + 3 * hf, 0:4 * HD].rearrange("p (h d) -> p h d", h=4)))

                    def scan_u(n):
                        q, r = n // 2, slice(HD * (n % 2), HD * (n % 2) + HD)
                        v.wait_ge(S("wS").sem, n + 1)
                        v.wait_ge(S("u0_out").sem, 2 * (q + 1))
                        done("v_step", v.tensor_tensor(
                            u[r].rearrange("p (a b) d -> p a b d", b=2), u0[r].rearrange("p (a b) d -> p a b d", b=2),
                            ps[r, 0:2, 0:4 * HD].rearrange("p b (a d) -> p a b d", a=4), ALU.subtract))
                        S("u_out").on(v.tensor_tensor(u[r], u[r], bc(sig[r, q, 0:NH], HD), ALU.mult))

                    def scan_state(n):
                        v.wait_ge(S("stmp_ready").sem, n + 1)
                        v.wait_ge(S("oS").sem, n + 1)
                        S("state").on(v.tensor_tensor(St[:], ps[:, 0, 0:4 * HD].rearrange("p (a e) -> p a e", a=4),
                                                      Stmp[:], ALU.add))

                    def scan_output(n):
                        v.wait_ge(S("oS_out").sem, n + 1)
                        v.wait_ge(S("oU").sem, n + 1)
                        o = mixT[:, 0:4, HD * n:HD * (n + 1)]
                        S("oT_out").on(v.tensor_tensor(o, ps[:, 1, 0:4 * HD].rearrange("p (a i) -> p a i", a=4), o,
                                                       ALU.add))

                    for q in range(TT + 1):
                        prepare(q)

                    v.wait_ge(S("sample_mm").sem, 1)
                    done("sample_dve", v.tensor_copy(xuT[:], ps[:, 0, 0:256].rearrange("p (a s i) -> p a s i", a=4, s=2)))
                    v.wait_ge(S("sample_mm").sem, 2)
                    v.wait_ge(S("u0_out").sem, 2 * (TT + 1))
                    done("v_step", v.tensor_tensor(u[0:NS], u0[0:NS], ps[0:NS, 1, :].rearrange("p (h d) -> p h d", h=NH),
                                                   ALU.subtract))
                    S("sample_dve").on(v.tensor_tensor(u[0:NS], u[0:NS], bc(sig[0:NS, TT, 0:NH], HD), ALU.mult))
                    v.wait_ge(S("sample_mm").sem, 3)
                    S("sample_dve").on(v.tensor_tensor(mixT[:, 0:4, SEQ:TOK], ps[:, 2, 0:4 * NS].rearrange("p (a i) -> p a i", a=4),
                                                   xuT[:, :, 1, :], ALU.add))
                    v.wait_ge(S("sample_dve").sem, 2)
                    for h in range(1, NH, 2):
                        S("um_odd").on(v.tensor_tensor(um[:, h], mid(u[0:NS, h, :], NB), bc(C("seqof", NS), HD), ALU.mult))
                    for hp in range(4):
                        v.wait_ge(S("sdS").sem, hp + 1)
                        v.wait_ge(S("sadd_out").sem, hp + 1)
                        S("sdS_out").on(v.tensor_tensor(Ss[:, :, hp, :], ps[:, 3 + hp, :].rearrange("p (b e) -> p b e", b=NB),
                                                        sadd[:, hp % 2], ALU.add))
                    v.wait_ge(S("o_sum").sem, 1)
                    S("o_norm_vector").on(v.tensor_scalar(halves(qkv[:, 8, :]), whole(0), 1.0 / HD, EPS, ALU.mult, ALU.add))
                    for hp in range(4):
                        S("o_norm_vector").on(v.scalar_tensor_tensor(mixT[:, hp, :], mixT[:, hp, :], ggdn[:, 0:1],
                                                               zT[:, hp, :], ALU.mult, ALU.mult))
                    v.wait_ge(S("o_root").sem, 1)
                    S("o_norm_vector").on(v.reciprocal(qkv[:, 8, :], qkv[:, 8, :]))
                    v.wait_ge(S("o_norm_vector").sem, 5)
                    for hp in range(4):
                        v.wait_ge(S("o_spread").sem, hp + 1)
                        S("gdn_mixed").on(v.tensor_tensor(halves(mixT[:, hp, :]), whole((hp + 1) % 4),
                                                          halves(mixT[:, hp, :]), ALU.mult))

                    for n in range(N_GDN, N_TILES):
                        split_low(v, n)

                    def rope(i):
                        n = ROPED[i]
                        v.wait_ge(S("rot").sem, i + 1)
                        if i:
                            v.wait_ge(S("rope_done").sem, i)
                        done("rope_sin", v.tensor_tensor(halves(rs[:]), whole(i % 3), halves(C("sin")), ALU.mult))
                        v.wait_ge(S("rope_cos").sem, i + 1)
                        S("rope_done").on(v.tensor_tensor(nsaT[:, n, :], nsaT[:, n, :], rs[:], ALU.add))

                    def past_keys_out(i):
                        v.wait_ge(S("kpast_turned").sem, i + 1)
                        v.tensor_copy(kselT[:, i // 2, 0:PAST], ps[:, 6, 0:PAST])
                        S("kpast_out").on(v.tensor_copy(kwinT[:, i // 2, NT:NT + PAST], ps[:, 6, PAST:2 * PAST]))

                    for i in range(len(ROPED)):
                        rope(i)
                    for i in range(0, 2 * NB, 2):
                        past_keys_out(i)
                    for s in range(2):
                        v.wait_ge(S("cmp").sem, s + 1)
                        done("v_step", v.tensor_copy(ckT[:, s, :], ps[:, s, 0:NCA + 1]))
                        S("ck_out").on(v.tensor_scalar(ckT[:, s, 0:NCA], ckT[:, s, 0:NCA], ckT[:, s, NCA:NCA + 1], None,
                                                       ALU.add))
                    v.wait_ge(S("ck_rot").sem, 1)
                    v.wait_ge(S("rope_done").sem, len(ROPED))
                    done("v_step", v.tensor_tensor(rs[:, 0:NCA], ps[:, 2, 0:NCA], C("sinc"), ALU.mult))
                    v.wait_ge(S("compressed_pool").sem, 2)
                    done("v_step", v.tensor_tensor(ckr[:], ckr[:], rs[:, 0:NCA], ALU.add))
                    v.wait_ge(S("compressed_pool").sem, 1)
                    for g in range(KVH):
                        r = slice(HD * g, HD * (g + 1))
                        x = v.tensor_copy(ckz[r, g, :], ckr[r, 0:NCP])
                    S("compressed_vector").on(x)
                    v.wait_ge(S("cv_turned").sem, 1)
                    S("compressed_vector").on(v.tensor_tensor(
                        cvb.rearrange("p (g j) d -> p g j d", g=KVH),
                        ps[:, 3, 0:P].rearrange("p (g d) -> p g d", g=KVH).unsqueeze(2).to_broadcast([P, KVH, GQA, HD]),
                        C("cmphead").rearrange("p (g j) -> p g j", g=KVH).unsqueeze(3).to_broadcast([P, KVH, GQA, HD]),
                        ALU.mult))

                    def gates(q):
                        return sig[:, q, NH:4 * NH].rearrange("p (h r) -> p h r", r=3)

                    v.wait_ge(S("compressed_tensor").sem, 1)
                    late = C("cmpneg").rearrange("p (q n) -> p q n", q=TT).unsqueeze(2).to_broadcast([P, TT, NH, NCP])
                    pc3 = pc.rearrange("p q h n -> p (q h) n")
                    done("v_step", v.tensor_tensor(pc, ps[:, 6, :].rearrange("p (q h n) -> p q h n", q=TT, h=NH), late,
                                                   ALU.add))
                    done("v_step", v.tensor_reduce(cstat, pc3, AX.X, ALU.max))
                    done("v_step", v.tensor_scalar(cstat, cstat, FLOOR, None, ALU.max))
                    done("compressed_vector", v.tensor_tensor(pc3, pc3, bc(cstat, NCP), ALU.subtract))

                    def compressed_sums():
                        v.wait_ge(S("compressed_scalar").sem, 1)
                        done("v_step", v.tensor_reduce(cstat, pc3, AX.X, ALU.add))
                        done("v_step", v.tensor_scalar(cstat, cstat, 1e-30, None, ALU.max))
                        done("v_step", v.reciprocal(cstat, cstat))
                        c4 = cstat.rearrange("p (q j g) -> p q j g", q=TT, j=GQA)
                        for q in range(TT):
                            x = v.tensor_tensor(c4[:, q], c4[:, q], sig[:, q, NH:4 * NH].rearrange(
                                "p (g j r) -> p r j g", g=KVH, j=GQA)[:, 0], ALU.mult)
                        done("v_step", x)
                        S("compressed_vector").on(v.tensor_tensor(pc3, pc3, bc(cstat, NCP), ALU.mult))

                    def maxima(uu):
                        q, z = uu // NH, uu % 2
                        n = P * (q + 1)
                        v.wait_ge(S("score").sem, uu + 1)
                        both = ps[:, 2 * z:2 * z + 2, :]
                        diag = both[:, :, P * q:P * (q + 1)]
                        done("v_step", v.tensor_tensor(diag, diag, mid(C("causal"), 2), ALU.add))
                        if uu >= 2:
                            v.wait_ge(S("p_exp").sem, 2 * (uu - 1))
                        done("v_step", v.tensor_reduce(stat[:, 8 * z:8 * z + 2], both[:, :, 0:n], AX.X, ALU.max))
                        S("p_max").on(v.tensor_scalar(stat[:, 8 * z + 2:8 * z + 4], stat[:, 8 * z:8 * z + 2], -SCALE, None,
                                                      ALU.mult))

                    def turned(uu):
                        n = P * (uu // NH + 1)
                        v.wait_ge(S("pT").sem, 2 * uu + 2)
                        if uu:
                            v.wait_ge(S("nsa").sem, uu)
                        S("pT_out1").on(v.tensor_copy(attT[:, 1, 0:n], ps[:, 5, 0:n]))
                        (q, h), z = divmod(uu, NH), uu % 2
                        st = stat[:, 8 * z + 4:8 * z + 6]
                        v.wait_ge(S("p_exp").sem, 2 * (uu + 1))
                        done("v_step", v.tensor_scalar(st, st, 1e-30, None, ALU.max))
                        done("v_step", v.reciprocal(st, st))
                        S("r_ready").on(v.tensor_tensor(stat[:, 48 + 3 * z:50 + 3 * z], gates(q)[:, h, 1:3], st,
                                                        ALU.mult))

                    def scale(uu):
                        z = uu % 2
                        v.wait_ge(S("nsa").sem, uu + 1)
                        v.wait_ge(S("r_ready").sem, uu + 1)
                        if uu >= 2:
                            v.wait_ge(S("o_added").sem, uu - 1)
                        S("o_scaled").on(v.tensor_tensor(
                            scaled[:, z], ps[:, 6 + z, 0:3 * HD].rearrange("p (s d) -> p s d", s=3),
                            bc(stat[:, 48 + 3 * z:51 + 3 * z], HD), ALU.mult))

                    done("v_step", v.memset(stat[:, 48:54], 1.0))
                    maxima(0)
                    maxima(1)
                    compressed_sums()
                    for what, i in SCHEDULE[2:]:
                        if what != "o":
                            {"s": maxima, "t": turned, "v": scale}[what](i)

                    n = PAST + NT
                    for g in range(2):
                        v.wait_ge(S("ss").sem, g + 1)
                        for bank, at in ((2 * g, PAST), (2 * g + 1, 0)):
                            new = ps[:, bank, at:at + NT]
                            x = v.tensor_tensor(new, new, C("newneg"), ALU.add)
                        done("v_step", x)
                        for i, src in enumerate((ps[:, 2 * g, n:n + NCS], ps[:, 2 * g, 0:n], ps[:, 2 * g + 1, 0:n])):
                            x = v.tensor_reduce(sstat[:, g, i:i + 1], src, AX.X, ALU.max)
                        done("v_step", x)
                        own = sstat[:, g, 16:16 + 3 * NH]
                        done("v_step", v.tensor_tensor(own.rearrange("p (h r) -> p h r", r=3),
                                                       ps[:, 2 * g, 320:320 + 3 * NH].rearrange("p (h r) -> p h r", r=3),
                                                       bc(C("rowhead"), 3), ALU.mult))
                        S("s_max").on(v.tensor_scalar(sstat[:, g, 3:6], sstat[:, g, 0:3], -SCALE, None, ALU.mult))
                        done("v_step", v.tensor_reduce(sstat[:, g, 9:12], own.rearrange("p (h r) -> p r h", r=3), AX.X,
                                                       ALU.add))
                    for g in range(2):
                        v.wait_ge(S("s_exp").sem, g + 1)
                        r = sstat[:, g, 6:9]
                        done("v_step", v.tensor_scalar(r, r, 1e-30, None, ALU.max))
                        done("v_step", v.reciprocal(r, r))
                        done("v_step", v.tensor_tensor(r, r, sstat[:, g, 9:12], ALU.mult))
                        for i, part in enumerate((satt[:, g, n:n + NCS], satt[:, g, 0:n], satt[:, g, n + NCS:SROW])):
                            x = v.tensor_scalar(part, part, sstat[:, g, 6 + i:7 + i], None, ALU.mult)
                        S("sp_ready").on(x)

                    def mix_low(k):
                        v.wait_ge(S("mix_high").sem, k + 1)
                        S("mix_low").on(v.tensor_tensor(mixT_r[:, k, :], mixT[:, k, :], F(mix_hi[:, k, :]), ALU.subtract))

                    for n in range(N_TILES, N_TILES + AHEAD):
                        split_low(v, n)
                    for k in range(4):
                        mix_low(k)
                    v.wait_ge(S("so_att").sem, 2)
                    for g in range(KVH):
                        r = slice(HD * g, HD * (g + 1))
                        src = ps[r, 7, 0:8 * 32].rearrange("p (b k j t) -> p k j b t", b=NB, k=KVH, j=GQA)[:, g]
                        S("nsa_mixed").on(v.tensor_copy(mixT[r, 4:8, SEQ:TOK].rearrange("p j (b t) -> p j b t", b=NB), src))
                    for k in range(4, KT):
                        mix_low(k)
                    for d in range(KT):
                        if d + AHEAD < KT:
                            split_low(v, N_TILES + d + AHEAD)
                        v.wait_ge(S("res").sem, d + 1)
                        S("res_added").on(v.tensor_tensor(halves(xT[:, d, :]), whole(d % 3), halves(xT[:, d, :]), ALU.add))
                    v.wait_ge(S("res_added").sem, KT)
                    norm_vector(v, 1, gmlp, hT, mix_hi, [lambda e, i=i: mlp_split_low(e, 0, i) for i in range(AHEAD)])

                    def mlp_group(m, last):
                        for i in range(16):
                            mlp_split_ahead(mlp_split_low, v, m, i, last)
                            if i < 8:
                                v.wait_ge(S("relu_done").sem, m * 8 + (i + 1))
                                v.tensor_tensor(uT[:, i, :], uT[:, i, :], uT[:, i, :], ALU.mult).then_inc(
                                    S("u_square").sem, 1)
                            if 1 <= i < 9:
                                v.wait_ge(S("u_high").sem, m * 8 + i)
                                v.tensor_tensor(uT_r[:, i - 1, :], uT[:, i - 1, :], F(u_hi[:, i - 1, :]), ALU.subtract).then_inc(
                                    S("u_ready").sem, 1)
                            if i >= 8:
                                d = i - 8
                                v.wait_ge(S("res").sem, m * 8 + (KT + d + 1))
                                v.tensor_tensor(halves(xT[:, d, :]), whole(d % 4), halves(xT[:, d, :]),
                                                ALU.add).then_inc(S("res_added").sem, 1)

                    with v.Fori(0, NGROUP - 1) as m:
                        mlp_group(m, False)
                    mlp_group(NGROUP - 1, True)

                @block.gpsimd
                def _(g_):
                    g = g_

                    def done(sem, instruction):
                        S(sem).on(instruction)
                        g.wait_ge(S(sem).sem, S(sem).n)

                    for n in range(12):
                        g.wait_ge(S("pre_out").sem, n + 1)
                        g.tensor_copy(xs[:, n, :, 3:7], pre[:, n % 3, SEQ:TOK].rearrange("p (b t) -> p b t", b=NB))
                        S("tail_out").on(g.tensor_copy(ctail[:, n, 0:3], pre[:, n % 3, SEQ - 3:SEQ]))
                    g.wait_ge(S("tail_out").sem, 12)
                    g.wait_ge(S("conv_state_in").sem, 16)
                    S("tail_out").on(g.tensor_copy(ctail[:, :, 3:].rearrange("p n (b t) -> p n b t", b=NB), xs[:, :, :, 4:7]))
                    g.wait_ge(S("proj_out").sem, 12)
                    for i in range(CONV - 1):
                        w = convw[:, :, i:i + 1].to_broadcast([P, 12, NS])
                        for b in range(NB):
                            x = g.tensor_tensor(cmul[:, :, NT * b:NT * (b + 1)], xs[:, :, b, i:i + NT],
                                                w[:, :, 0:NT], ALU.mult)
                        done("g_step", x)
                        done("sconv_done" if i == CONV - 2 else "g_step",
                             g.tensor_tensor(qkv[:, :, SEQ:TOK], qkv[:, :, SEQ:TOK], cmul[:], ALU.add))

                    def prepare(q):
                        n = tile_len(q)

                        def pr(name, hf):
                            return prep[name][0:n, hf, :, 0:n]

                        neg = C("negp" if q < TT else "negs", n, n)
                        cum = C("cump" if q < TT else "cums", n, n)
                        g.wait_ge(S("decay_vector").sem, 2)
                        g.wait_ge(S("kv_turned").sem, q + 1)
                        for hf in range(2):
                            S("gU_ready").on(g.tensor_tensor(pr("d", hf), mid(cum, 4),
                                                             bc(gtok[0:n, q, 4 * hf:4 * hf + 4], n), ALU.mult))
                        for hf in range(2):
                            g.wait_ge(S("G_diff").sem, 2 * q + hf + 1)
                            S("G_masked").on(g.tensor_tensor(pr("a", hf), pr("a", hf), mid(neg, 4), ALU.add))
                        if q:
                            decay_state(2 * q - 2)
                        g.wait_ge(S("gram").sem, 2 * q + 2)
                        g.wait_ge(S("Eg_out").sem, TT + 1)
                        if q < TT:
                            S("qe_out").on(g.tensor_tensor(qkv[:, 0:4, cols(q)], qkv[:, 0:4, cols(q)], Eg[:, :, cols(q)],
                                                           ALU.mult))
                        else:
                            S("qe_out").on(g.tensor_tensor(wqT[:, 1, :, 0:NS], qkv[:, 0:4, cols(q)], Eg[:, :, cols(q)],
                                                           ALU.mult))
                        for hf in range(2):
                            g.wait_ge(S("GE_out").sem, 2 * q + hf + 1)
                            S("B_ready").on(g.tensor_tensor(pr("b", hf), pr("b", hf), bc(sig[0:n, q, 4 * hf:4 * hf + 4], n),
                                                            ALU.mult))
                        for hf in range(2):
                            g.wait_ge(S("A_out").sem, 2 * q + hf + 1)
                            S("AD_ready").on(g.tensor_tensor(pr("c", hf), pr("a", hf), mid(C("lower", n, n), 4), ALU.mult))
                        for hf in range(2):
                            g.wait_ge(S("D2T_out").sem, 2 * q + hf + 1)
                            S("ID2T_out").on(g.tensor_tensor(pr("c", hf), pr("b", hf), mid(C("ident", n, n), 4), ALU.add))
                        if q:
                            decay_state(2 * q - 1)
                        if q < TT:
                            for hf in range(2):
                                g.wait_ge(S("P1").sem, 2 * q + hf + 1)
                                S("M_ready").on(g.tensor_tensor(pr("c", hf), pr("a", hf),
                                                                mid(C("low16", n, n), 4), ALU.mult))
                            for i, lev in enumerate(LEVELS[1:]):
                                for hf in range(2):
                                    g.wait_ge(S("X").sem, 2 * (3 * q + i) + hf + 1)
                                    S("M_ready").on(g.tensor_tensor(pr("c", hf), pr("a", hf),
                                                                    mid(C("low" + str(lev), n, n), 4), ALU.mult))

                    def decay_state(n):
                        g.wait_ge(S("state").sem, n + 1)
                        last = Eg[:, :, HD * n + HD - 1:HD * n + HD].to_broadcast([P, 4, HD])
                        S("stmp_ready").on(g.tensor_tensor(Stmp[:], St[:], last, ALU.mult))

                    for q in range(TT + 1):
                        prepare(q)
                    g.wait_ge(S("states_in").sem, 16)

                    def old_state(hp):
                        last = Eg[:, hp, SEQ:TOK].rearrange("p (b t) -> p b t", b=NB)[:, :, NT - 1:NT].to_broadcast(
                            [P, NB, HD])
                        S("sadd_out").on(g.tensor_tensor(sadd[:, hp % 2], Ss[:, :, hp, :], last, ALU.mult))

                    g.wait_ge(S("oU").sem, 2 * TT)
                    old_state(0)
                    old_state(1)
                    g.wait_ge(S("sample_dve").sem, 2)
                    for h in range(0, NH, 2):
                        S("um_even").on(g.tensor_tensor(um[:, h], mid(u[0:NS, h, :], NB), bc(C("seqof", NS), HD),
                                                        ALU.mult))
                    for hp in range(2, 4):
                        g.wait_ge(S("sdS_out").sem, hp - 1)
                        old_state(hp)

                    g.wait_ge(S("proj_out").sem, N_TILES)
                    g.wait_ge(S("pe_in").sem, 64)
                    for s in range(2):
                        S("cmp_in_ready").on(g.tensor_copy(cmp_in[s][:, 0:SEQ], nsaT[:, 4 + s, 0:SEQ]))
                        S("cmp_in_ready").on(g.tensor_copy(cmp_in[s][:, NCA * CMP:(NCA + 1) * CMP], pe[:, s, :]))
                    S("qs_ready").on(g.memset(qs[:], 0.0))
                    for i, n in enumerate(ROPED):
                        g.wait_ge(S("rot").sem, i + 1)
                        S("rope_cos").on(g.tensor_tensor(nsaT[:, n, :], nsaT[:, n, :], C("cos"), ALU.mult))
                    g.wait_ge(S("qs_ready").sem, 1)
                    g.wait_ge(S("rope_done").sem, len(ROPED))
                    for k in range(KVH):
                        r = slice(HD * k, HD * (k + 1))
                        done("qs_ready", g.tensor_copy(qs[r, :, k, :, :], nsaT[r, 0:4, SEQ:TOK].rearrange(
                            "p j (b t) -> p b j t", b=NB)))
                    for n, kT, at in ((6, kselT, PAST), (8, kwinT, 0)):
                        S("knew_out").on(g.tensor_copy(kT[:, :, at:at + NT],
                                                       nsaT[:, n, SEQ:TOK].rearrange("p (b t) -> p b t", b=NB)))
                    g.wait_ge(S("kpast_turned").sem, 2 * NB)
                    g.memset(ckz, 0.0)
                    for n, at in ((7, 0), (9, NT + NCS)):
                        S("vsrc_ready").on(g.tensor_copy(vsrc[:, :, at:at + NT],
                                                         nsaT[:, n, SEQ:TOK].rearrange("p (b t) -> p b t", b=NB)))
                    S("compressed_pool").on(g.memset(kz, 0.0))
                    g.wait_ge(S("ck_out").sem, 1)
                    S("compressed_pool").on(g.tensor_tensor(ckr[:], ckT[:, 0, 0:NCA], C("cosc"), ALU.mult))
                    g.wait_ge(S("ck_out").sem, 2)
                    S("vsrc_ready").on(g.tensor_copy(vsrc[:, :, NT:NT + NCS],
                                                     ckT[:, 1, NCP:NCA].rearrange("p (b n) -> p b n", b=NB)))
                    S("compressed_pool").on(g.tensor_copy(cvrep.rearrange("p (h n) -> p h n", h=NH),
                                                      mid(ckT[:, 1, 0:NCP], NH)))

                    def add(uu):
                        (q, h), z = divmod(uu, NH), uu % 2
                        out = osum[:, q % 2, h % GQA, h // GQA, :]
                        g.wait_ge(S("o_scaled").sem, uu + 1)
                        if q >= 2:
                            g.wait_ge(S("o_turned").sem, q - 1)
                        done("g_step", g.tensor_tensor(out, scaled[:, z, 0], scaled[:, z, 1], ALU.add))
                        S("o_added").on(g.tensor_tensor(out, out, scaled[:, z, 2], ALU.add))

                    for uu in range(UNITS):
                        add(uu)

            nums = sorted(x.sem.num for x in signals.values())
            assert not {setup.num, x_loaded.num} & set(range(nums[0], nums[-1] + 1))
            nc.gpsimd.sem_clear(range(nums[0], nums[-1] + 1))
            nc.all_engine_barrier()
            for x in signals.values():
                x.n = 0

        with nc.Block() as block:
            @block.tensor
            def _(t):
                norm_tensor(t, 0, lambda k: mixT[:, k, :])

            @block.scalar
            def _(act):
                norm_scalar(act, 0, lambda k: mixT[:, k, :], KT)

            @block.vector
            def _(v):
                norm_vector(v, 0, gfin, hT)

            @block.sync
            def _(sp):
                for k in range(KT):
                    sp.wait_ge(S("h_full").sem, k + 1)
                    sp.dma_start(O["yT"][:, k], hT[:, k]).then_inc(S("rows_stored").sem, 16)
                sp.wait_ge(S("rows_stored").sem, 16 * KT)


def kernel(x_prompt, x_sample, cache_kv, page_table, state_win, state_gdn, state_conv, norm_mix, w_in, conv_w,
           a_log, dt_bias, gdn_norm, cmp_pe_k, cmp_w_k, cmp_pe_v, cmp_w_v, w_out, norm_mlp, w_up, w_down,
           norm_final):
    import concourse.bacc as bacc
    from concourse.bass_utils import run_bass_kernel_spmd

    def tiled(a, axis=-1):
        a = np.moveaxis(np.asarray(a), axis, 0)
        return np.moveaxis(a.reshape((a.shape[0] // P, P) + a.shape[1:]), 1, 0)

    L = DEPTH
    x = np.concatenate([np.asarray(x_prompt)[0], np.asarray(x_sample).reshape(NS, D)], 0)
    arrays = {
        "xT": tiled(x),
        "norm_final": tiled(norm_final),
        "norm_mix": np.stack([tiled(a) for a in np.asarray(norm_mix)]),
        "norm_mlp": np.stack([tiled(a) for a in np.asarray(norm_mlp)]),
        "gdn_norm": np.concatenate([np.asarray(gdn_norm)] * 2, 1)[:, :, None],
        "conv_w": np.stack([np.moveaxis(tiled(a), 2, 2) for a in np.asarray(conv_w)]),
        "state_conv": np.stack([tiled(a) for a in np.asarray(state_conv)]),
        "state_gdn": np.asarray(state_gdn).reshape(L, NB, 4, 2, HD, HD).transpose(0, 3, 4, 1, 2, 5).reshape(
            L, P, NB, 4, HD),
        "page_table": np.asarray(page_table).reshape(1, NPG),
        "cmp_pe_k": np.asarray(cmp_pe_k).transpose(0, 2, 1),
        "cmp_pe_v": np.asarray(cmp_pe_v).transpose(0, 2, 1),
        "consts": CONST_TABLE,
        "cache_kv": cache_kv, "state_win": state_win, "w_in": w_in, "a_log": a_log, "dt_bias": dt_bias,
        "cmp_w_k": cmp_w_k, "cmp_w_v": cmp_w_v, "w_out": w_out, "w_up": w_up, "w_down": w_down,
    }
    arrays = {k: np.ascontiguousarray(np.asarray(a)) for k, a in arrays.items()}
    shapes = {
        "yT": (P, KT, TOK), "rows_T": (L, P, 6, TOK), "win_past": (L, NB, PAST - NT, 2, KVH, HD),
        "gdn_p": (L, P, 4, HD), "gdn_s": (L, P, NB, 4, HD), "conv_T": (L, P, 12, 3 + 3 * NB),
    }
    nc = bacc.Bacc("TRN2", target_bir_lowering=False, num_devices=1)
    A = {k: nc.dram_tensor("in_" + k, a.shape, mybir.dt.from_np(a.dtype), kind="ExternalInput").ap()
         for k, a in arrays.items()}
    O = {k: nc.dram_tensor("out_" + k, s, F32, kind="ExternalOutput").ap() for k, s in shapes.items()}
    build(nc, A, O)
    r = run_bass_kernel_spmd(nc, [{"in_" + k: a for k, a in arrays.items()}], core_ids=[0]).results[0]
    o = {k: np.asarray(r["out_" + k]) for k in shapes}

    y = o["yT"].transpose(2, 1, 0).reshape(TOK, D)
    rows = o["rows_T"].reshape(L, KVH, HD, 6, TOK).transpose(0, 1, 4, 3, 2)
    rows_p = rows[:, None, :, 0:SEQ, 0:4]
    rows_s = rows[:, :, SEQ:, 0:4].reshape(L, KVH, NB, NT, 4, HD).transpose(0, 2, 1, 3, 4, 5)
    win_new = rows[:, :, :, 4:6].transpose(0, 2, 3, 1, 4)
    win_p = win_new[:, None, 0:SEQ]
    win_s = np.concatenate([o["win_past"], win_new[:, SEQ:].reshape(L, NB, NT, 2, KVH, HD)], 2)
    gdn_p = o["gdn_p"].reshape(L, 2, HD, 4, HD).transpose(0, 3, 1, 2, 4).reshape(L, 1, NH, HD, HD)
    gdn_s = o["gdn_s"].reshape(L, 2, HD, NB, 4, HD).transpose(0, 3, 4, 1, 2, 5).reshape(L, NB, NH, HD, HD)
    conv = o["conv_T"].transpose(0, 3, 2, 1).reshape(L, 3 + 3 * NB, C_QKV)
    conv_p = conv[:, None, 0:3]
    conv_s = conv[:, 3:].reshape(L, NB, 3, C_QKV)
    return tuple(np.ascontiguousarray(a) for a in (
        y[None, 0:SEQ], y[SEQ:].reshape(NB, NT, D), rows_p, rows_s, win_p, win_s, gdn_p, gdn_s, conv_p, conv_s))
```
